# Optimizing a Trainium2 kernel written in Bass

```python
import jax, jax.numpy as jnp
from jax import lax
import numpy as np

D_MODEL = 1024
BATCH = 1
SEQ = 512
DEPTH = 1

FOURIER_GROUPS = 4
FOURIER_WIDTH = D_MODEL // 2
FOURIER_GROUP_DIM = FOURIER_WIDTH // FOURIER_GROUPS
MLA_HEADS = 8
QK_NOPE_DIM = 64
QK_ROPE_DIM = 32
V_HEAD_DIM = (D_MODEL // 2) // MLA_HEADS
Q_LORA_RANK = 384
KV_LORA_RANK = 256
Q_BLOCK = 128
ROPE_THETA = 10000.0
D_FF = 2816
NORM_EPS = 1e-6
N_ADA = 9
W_IN_COLS = FOURIER_WIDTH + Q_LORA_RANK + KV_LORA_RANK + QK_ROPE_DIM + 2 * D_MODEL
SPLIT_1 = FOURIER_WIDTH
SPLIT_2 = SPLIT_1 + Q_LORA_RANK
SPLIT_3 = SPLIT_2 + KV_LORA_RANK
SPLIT_4 = SPLIT_3 + QK_ROPE_DIM


def rms_norm(x, g):
    x32 = x.astype(jnp.float32)
    y = x32 * lax.rsqrt(jnp.mean(x32 * x32, axis=-1, keepdims=True) + NORM_EPS)
    return (y * g.astype(jnp.float32)).astype(x.dtype)

def modulate(h, shift, scale):
    return h * (1 + scale[:, None, :]) + shift[:, None, :]

def swiglu(h, w_gate, w_up, w_down):
    return (jax.nn.silu(h @ w_gate) * (h @ w_up)) @ w_down

def rope_tables(positions):
    half = QK_ROPE_DIM // 2
    inv_freq = 1.0 / (ROPE_THETA ** (jnp.arange(half, dtype=jnp.float32) * 2.0 / QK_ROPE_DIM))
    ang = positions.astype(jnp.float32)[..., None] * inv_freq
    return jnp.cos(ang), jnp.sin(ang)

def apply_rope(x, cos, sin):
    x32 = x.astype(jnp.float32)
    x1, x2 = jnp.split(x32, 2, axis=-1)
    out = jnp.concatenate([x1 * cos - x2 * sin, x2 * cos + x1 * sin], axis=-1)
    return out.astype(x.dtype)

def fourier_mix(u):
    b, s, _ = u.shape
    ug = u.reshape(b, s, FOURIER_GROUPS, FOURIER_GROUP_DIM).astype(jnp.float32)
    f = jnp.fft.fft2(ug, axes=(1, 3), norm="ortho").real
    return f.reshape(b, s, FOURIER_WIDTH).astype(u.dtype)

def mla_attention(q_lat, kv_lat, k_rope, positions, q_norm, w_q_up, kv_norm, w_kv_up):
    b, s, _ = q_lat.shape
    q = (rms_norm(q_lat, q_norm) @ w_q_up).reshape(b, s, MLA_HEADS, QK_NOPE_DIM + QK_ROPE_DIM)
    kv = (rms_norm(kv_lat, kv_norm) @ w_kv_up).reshape(b, s, MLA_HEADS, QK_NOPE_DIM + V_HEAD_DIM)
    q_nope, q_rot = q[..., :QK_NOPE_DIM], q[..., QK_NOPE_DIM:]
    k_nope, v = kv[..., :QK_NOPE_DIM], kv[..., QK_NOPE_DIM:]
    cos, sin = rope_tables(positions)
    q_rot = apply_rope(q_rot, cos[:, :, None, :], sin[:, :, None, :])
    k_rot = apply_rope(k_rope, cos, sin)
    sm_scale = (QK_NOPE_DIM + QK_ROPE_DIM) ** -0.5
    q_nope = q_nope * sm_scale
    q_rot = q_rot * sm_scale
    n_blk = s // Q_BLOCK
    qn_b = q_nope.reshape(b, n_blk, Q_BLOCK, MLA_HEADS, QK_NOPE_DIM).transpose(1, 0, 2, 3, 4)
    qr_b = q_rot.reshape(b, n_blk, Q_BLOCK, MLA_HEADS, QK_ROPE_DIM).transpose(1, 0, 2, 3, 4)

    def attend(blk):
        qn_i, qr_i = blk
        scores = (jnp.einsum('bqhd,bkhd->bhqk', qn_i, k_nope)
                  + jnp.einsum('bqhr,bkr->bhqk', qr_i, k_rot))
        p = jax.nn.softmax(scores.astype(jnp.float32), axis=-1).astype(v.dtype)
        return jnp.einsum('bhqk,bkhd->bqhd', p, v)

    o = lax.map(attend, (qn_b, qr_b))
    return o.transpose(1, 0, 2, 3, 4).reshape(b, s, MLA_HEADS * V_HEAD_DIM)

def first_inputs(seed: int = 0) -> dict:
    key = jax.random.key(seed)
    ks = jax.random.split(key, 24)
    f32 = jnp.float32

    def w(k, shape, fan_in, gain=1.0):
        return (jax.random.normal(k, shape, f32) * (gain * fan_in ** -0.5)).astype(f32)

    def gain(k, shape):
        return 1.0 + 0.02 * jax.random.normal(k, shape, f32)

    L, D = DEPTH, D_MODEL
    x = jax.random.normal(ks[0], (BATCH, SEQ, D), f32)
    c = jax.random.normal(ks[1], (BATCH, D), f32)
    offs = jax.random.randint(ks[2], (BATCH, 1), 0, 1024, dtype=jnp.int32)
    positions = (offs + jnp.arange(SEQ, dtype=jnp.int32)[None, :]).astype(jnp.int32)
    return {
        "x": x,
        "c": c,
        "positions": positions,
        "ada_w": w(ks[3], (L, D, N_ADA * D), D, 0.2),
        "ada_b": 0.02 * jax.random.normal(ks[4], (L, N_ADA * D), f32),
        "ffn1_norm": gain(ks[5], (L, D)),
        "ffn1_w_gate": w(ks[6], (L, D, D_FF), D),
        "ffn1_w_up": w(ks[7], (L, D, D_FF), D),
        "ffn1_w_down": w(ks[8], (L, D_FF, D), D_FF),
        "mix_norm": gain(ks[9], (L, D)),
        "w_in": w(ks[10], (L, D, W_IN_COLS), D),
        "q_norm": gain(ks[11], (L, Q_LORA_RANK)),
        "w_q_up": w(ks[12], (L, Q_LORA_RANK, MLA_HEADS * (QK_NOPE_DIM + QK_ROPE_DIM)), Q_LORA_RANK),
        "kv_norm": gain(ks[13], (L, KV_LORA_RANK)),
        "w_kv_up": w(ks[14], (L, KV_LORA_RANK, MLA_HEADS * (QK_NOPE_DIM + V_HEAD_DIM)), KV_LORA_RANK),
        "w_fourier_out": w(ks[15], (L, FOURIER_WIDTH, D), FOURIER_WIDTH),
        "w_mla_out": w(ks[16], (L, MLA_HEADS * V_HEAD_DIM, D), MLA_HEADS * V_HEAD_DIM),
        "w_out": w(ks[17], (L, D, D), D),
        "ffn2_norm": gain(ks[18], (L, D)),
        "ffn2_w_gate": w(ks[19], (L, D, D_FF), D),
        "ffn2_w_up": w(ks[20], (L, D, D_FF), D),
        "ffn2_w_down": w(ks[21], (L, D_FF, D), D_FF),
        "final_norm": gain(ks[22], (D,)),
    }

def first_block(x, c, positions, ada_w, ada_b, ffn1_norm, ffn1_w_gate, ffn1_w_up, ffn1_w_down,
              mix_norm, w_in, q_norm, w_q_up, kv_norm, w_kv_up, w_fourier_out, w_mla_out, w_out,
              ffn2_norm, ffn2_w_gate, ffn2_w_up, ffn2_w_down, final_norm):
    c_act = jax.nn.silu(c)
    for l in range(DEPTH):
        mod = c_act @ ada_w[l] + ada_b[l]
        (sh1, sc1, g1, sh2, sc2, g2, sh3, sc3, g3) = jnp.split(mod, N_ADA, axis=-1)

        h = modulate(rms_norm(x, ffn1_norm[l]), sh1, sc1)
        x = x + 0.5 * g1[:, None, :] * swiglu(h, ffn1_w_gate[l], ffn1_w_up[l], ffn1_w_down[l])

        h = modulate(rms_norm(x, mix_norm[l]), sh2, sc2)
        z = h @ w_in[l]
        u_f, q_lat, kv_lat, k_rope, gate_logits = jnp.split(
            z, [SPLIT_1, SPLIT_2, SPLIT_3, SPLIT_4], axis=-1)
        y_a = fourier_mix(u_f) @ w_fourier_out[l]
        y_b = mla_attention(q_lat, kv_lat, k_rope, positions, q_norm[l], w_q_up[l],
                            kv_norm[l], w_kv_up[l]) @ w_mla_out[l]
        gate_a, gate_b = jnp.split(jax.nn.sigmoid(gate_logits), 2, axis=-1)
        y = (gate_a * y_a + gate_b * y_b) @ w_out[l]
        x = x + g2[:, None, :] * y

        h = modulate(rms_norm(x, ffn2_norm[l]), sh3, sc3)
        x = x + 0.5 * g3[:, None, :] * swiglu(h, ffn2_w_gate[l], ffn2_w_up[l], ffn2_w_down[l])
    return rms_norm(x, final_norm)


HEAD_DIM = 64
NSA_HEADS = 8
NSA_KV = 2
DSA_HEADS = 8
IDX_HEADS = 4
IDX_DIM = 64
CMP_LEN = 32
CMP_STRIDE = 16
CMP_HIDDEN = 2 * HEAD_DIM
SLC_LEN = 64
SLC_TOPN = 16
WIN = 512
DSA_TOPK = 256
D_FF_2 = 4 * D_MODEL
D_MIX = (NSA_HEADS + DSA_HEADS) * HEAD_DIM
EPS = 1e-6
SLC_Q_BLOCK = 16
NEG = -1e30
NSA_COLS = [NSA_HEADS * HEAD_DIM] + [NSA_KV * HEAD_DIM] * 6 + [NSA_HEADS * 3]
DSA_COLS = [DSA_HEADS * HEAD_DIM, HEAD_DIM, HEAD_DIM, IDX_HEADS * IDX_DIM, IDX_DIM, IDX_HEADS]
IN_COLS = NSA_COLS + DSA_COLS
D_IN = sum(IN_COLS)


def rms_norm_2(x, g):
    xf = x.astype(jnp.float32)
    y = xf * lax.rsqrt(jnp.mean(xf * xf, axis=-1, keepdims=True) + EPS)
    return (y * g.astype(jnp.float32)).astype(x.dtype)

def rope(x, pos):
    half = x.shape[-1] // 2
    inv = ROPE_THETA ** (-jnp.arange(half, dtype=jnp.float32) / half)
    ang = pos.astype(jnp.float32)[:, :, None] * inv
    cos = jnp.cos(ang)[:, :, None, :]
    sin = jnp.sin(ang)[:, :, None, :]
    xf = x.astype(jnp.float32)
    x1, x2 = xf[..., :half], xf[..., half:]
    return jnp.concatenate([x1 * cos - x2 * sin, x2 * cos + x1 * sin], axis=-1).astype(x.dtype)

def masked_softmax(s, mask):
    s = jnp.where(mask, s.astype(jnp.float32), NEG)
    return jax.nn.softmax(s, axis=-1) * mask.astype(jnp.float32)

def compress(kv, pe, w1, w2):
    B, T, G, dh = kv.shape
    n_cmp = (T - CMP_LEN) // CMP_STRIDE + 1
    blk = np.arange(n_cmp)[:, None] * CMP_STRIDE + np.arange(CMP_LEN)[None, :]
    blocks = kv[:, blk] + pe[None, None, :, None, :]
    flat = blocks.transpose(0, 1, 3, 2, 4).reshape(B, n_cmp, G, CMP_LEN * dh)
    return jax.nn.gelu(flat @ w1) @ w2

def nsa_attention(q, kc, vc, ks, vs, kw, vw, gate_logits, pe_k, pe_v, w1k, w2k, w1v, w2v):
    B, T, H, dh = q.shape
    G = kc.shape[2]
    R = H // G
    scale = dh ** -0.5
    q_t = q.reshape(B, T, G, R, dh).transpose(0, 2, 3, 1, 4)
    t_idx = np.arange(T)

    k_cmp = compress(kc, pe_k, w1k, w2k)
    v_cmp = compress(vc, pe_v, w1v, w2v)
    n_cmp = k_cmp.shape[1]
    cmp_start = np.arange(n_cmp) * CMP_STRIDE
    cmp_end = cmp_start + CMP_LEN - 1
    mask_c = jnp.asarray(cmp_end[None, :] <= t_idx[:, None])
    s_c = jnp.einsum('bgrtd,bngd->bgrtn', q_t, k_cmp) * scale
    p_c = masked_softmax(s_c, mask_c)
    o_cmp = jnp.einsum('bgrtn,bngd->bgrtd', p_c.astype(v_cmp.dtype), v_cmp)

    n_slc = T // SLC_LEN
    n_sel = min(SLC_TOPN, n_slc)
    slc_start = np.arange(n_slc) * SLC_LEN
    slc_end = slc_start + SLC_LEN - 1
    overlap = ((cmp_start[:, None] <= slc_end[None, :]) & (cmp_end[:, None] >= slc_start[None, :])).astype(np.float32)
    imp = jnp.einsum('bgrtn,nj->bgtj', p_c, jnp.asarray(overlap))
    j = np.arange(n_slc)[None, :]
    cur = (t_idx // SLC_LEN)[:, None]
    valid = jnp.asarray(j <= cur)
    forced = jnp.asarray((j == 0) | (j == cur) | (j == cur - 1))
    sel_score = jnp.where(valid, jnp.where(forced, jnp.inf, imp), -jnp.inf)
    _, sel = lax.top_k(sel_score, n_sel)

    kb = ks.reshape(B, n_slc, SLC_LEN, G, dh).transpose(0, 3, 1, 2, 4)
    vb = vs.reshape(B, n_slc, SLC_LEN, G, dh).transpose(0, 3, 1, 2, 4)
    nq = T // SLC_Q_BLOCK
    n_key = n_sel * SLC_LEN
    q_ch = q_t.reshape(B, G, R, nq, SLC_Q_BLOCK, dh).transpose(3, 0, 1, 2, 4, 5)
    i_ch = sel.reshape(B, G, nq, SLC_Q_BLOCK, n_sel).transpose(2, 0, 1, 3, 4)
    t_ch = jnp.arange(T, dtype=jnp.int32).reshape(nq, SLC_Q_BLOCK)
    bi = jnp.arange(B)[:, None, None, None]
    gi = jnp.arange(G)[None, :, None, None]

    def sel_chunk(args):
        qc, ic, tc = args
        kg = kb[bi, gi, ic].reshape(B, G, SLC_Q_BLOCK, n_key, dh)
        vg = vb[bi, gi, ic].reshape(B, G, SLC_Q_BLOCK, n_key, dh)
        kpos = (ic[..., None] * SLC_LEN + jnp.arange(SLC_LEN)).reshape(B, G, SLC_Q_BLOCK, n_key)
        mask = (kpos <= tc[None, None, :, None])[:, :, None]
        s = jnp.einsum('bgrqd,bgqkd->bgrqk', qc, kg) * scale
        p = masked_softmax(s, mask)
        return jnp.einsum('bgrqk,bgqkd->bgrqd', p.astype(vg.dtype), vg)

    o_slc = lax.map(sel_chunk, (q_ch, i_ch, t_ch))
    o_slc = o_slc.transpose(1, 2, 3, 0, 4, 5).reshape(B, G, R, T, dh)

    kp = jnp.pad(kw, ((0, 0), (WIN, 0), (0, 0), (0, 0)))
    vp = jnp.pad(vw, ((0, 0), (WIN, 0), (0, 0), (0, 0)))
    nb = T // Q_BLOCK
    span = WIN + Q_BLOCK
    q_b = q_t.reshape(B, G, R, nb, Q_BLOCK, dh).transpose(3, 0, 1, 2, 4, 5)

    def win_block(args):
        qb, bidx = args
        s0 = bidx * Q_BLOCK
        kk = lax.dynamic_slice_in_dim(kp, s0, span, axis=1)
        vv = lax.dynamic_slice_in_dim(vp, s0, span, axis=1)
        kpos = s0 - WIN + jnp.arange(span)
        tq = s0 + jnp.arange(Q_BLOCK)
        mask = (kpos[None, :] <= tq[:, None]) & (kpos[None, :] > tq[:, None] - WIN) & (kpos[None, :] >= 0)
        s = jnp.einsum('bgrqd,bsgd->bgrqs', qb, kk) * scale
        p = masked_softmax(s, mask)
        return jnp.einsum('bgrqs,bsgd->bgrqd', p.astype(vv.dtype), vv)

    o_win = lax.map(win_block, (q_b, jnp.arange(nb)))
    o_win = o_win.transpose(1, 2, 3, 0, 4, 5).reshape(B, G, R, T, dh)

    g = jax.nn.sigmoid(gate_logits.astype(jnp.float32)).reshape(B, T, G, R, 3)
    g = g.transpose(0, 2, 3, 1, 4).astype(q.dtype)
    o = g[..., 0:1] * o_cmp + g[..., 1:2] * o_slc + g[..., 2:3] * o_win
    return o.transpose(0, 3, 1, 2, 4).reshape(B, T, H * dh)

def dsa_attention(q, k, v, q_idx, k_idx, w_idx):
    B, T, H, dh = q.shape
    k_top = min(DSA_TOPK, T // 4)
    scale = dh ** -0.5
    idx_scale = (IDX_HEADS ** -0.5) * (IDX_DIM ** -0.5)
    nb = T // Q_BLOCK
    bi = jnp.arange(B)[:, None, None]
    key_pos = jnp.arange(T)

    def blocks(a):
        return a.reshape((B, nb, Q_BLOCK) + a.shape[2:]).swapaxes(0, 1)

    def dsa_block(args):
        qb, qib, wb, bidx = args
        tq = bidx * Q_BLOCK + jnp.arange(Q_BLOCK)
        logits = jnp.einsum('bqhd,bsd->bqhs', qib, k_idx).astype(jnp.float32)
        score = jnp.einsum('bqh,bqhs->bqs', wb.astype(jnp.float32) * idx_scale, jax.nn.relu(logits))
        score = jnp.where(key_pos[None, None, :] <= tq[None, :, None], score, -jnp.inf)
        _, sel = lax.top_k(score, k_top)
        kg = k[bi, sel]
        vg = v[bi, sel]
        mask = (sel <= tq[None, :, None])[:, None]
        s = jnp.einsum('bqhd,bqkd->bhqk', qb, kg) * scale
        p = masked_softmax(s, mask)
        return jnp.einsum('bhqk,bqkd->bqhd', p.astype(vg.dtype), vg)

    o = lax.map(dsa_block, (blocks(q), blocks(q_idx), blocks(w_idx), jnp.arange(nb)))
    return o.swapaxes(0, 1).reshape(B, T, H * dh)

def second_inputs(seed: int = 0) -> dict:
    key = jax.random.key(seed)
    ks = jax.random.split(key, 20)

    def nrm(k, shape, s):
        return jax.random.normal(k, shape, jnp.float32) * s

    x = nrm(ks[0], (BATCH, SEQ, D_MODEL), 1.0)
    c = nrm(ks[1], (BATCH, D_MODEL), 1.0)
    start = jax.random.randint(ks[2], (BATCH, 1), 0, 4096, dtype=jnp.int32)
    positions = start + jnp.arange(SEQ, dtype=jnp.int32)[None, :]
    return {
        'x': x,
        'c': c,
        'positions': positions,
        'w_ada': nrm(ks[3], (DEPTH, D_MODEL, 6 * D_MODEL), 0.1 * D_MODEL ** -0.5),
        'b_ada': nrm(ks[4], (DEPTH, 6 * D_MODEL), 0.01),
        'g_pre_mix': 1.0 + nrm(ks[5], (DEPTH, D_MODEL), 0.05),
        'g_post_mix': 1.0 + nrm(ks[6], (DEPTH, D_MODEL), 0.05),
        'g_pre_ffn': 1.0 + nrm(ks[7], (DEPTH, D_MODEL), 0.05),
        'g_post_ffn': 1.0 + nrm(ks[8], (DEPTH, D_MODEL), 0.05),
        'w_in': nrm(ks[9], (DEPTH, D_MODEL, D_IN), D_MODEL ** -0.5),
        'cmp_pe_k': nrm(ks[10], (DEPTH, CMP_LEN, HEAD_DIM), 0.02),
        'cmp_pe_v': nrm(ks[11], (DEPTH, CMP_LEN, HEAD_DIM), 0.02),
        'cmp_w1_k': nrm(ks[12], (DEPTH, CMP_LEN * HEAD_DIM, CMP_HIDDEN), (CMP_LEN * HEAD_DIM) ** -0.5),
        'cmp_w2_k': nrm(ks[13], (DEPTH, CMP_HIDDEN, HEAD_DIM), CMP_HIDDEN ** -0.5),
        'cmp_w1_v': nrm(ks[14], (DEPTH, CMP_LEN * HEAD_DIM, CMP_HIDDEN), (CMP_LEN * HEAD_DIM) ** -0.5),
        'cmp_w2_v': nrm(ks[15], (DEPTH, CMP_HIDDEN, HEAD_DIM), CMP_HIDDEN ** -0.5),
        'w_out': nrm(ks[16], (DEPTH, D_MIX, D_MODEL), D_MIX ** -0.5),
        'w_up': nrm(ks[17], (DEPTH, D_MODEL, D_FF_2), D_MODEL ** -0.5),
        'w_down': nrm(ks[18], (DEPTH, D_FF_2, D_MODEL), D_FF_2 ** -0.5),
    }

def second_block(x, c, positions, w_ada, b_ada, g_pre_mix, g_post_mix, g_pre_ffn, g_post_ffn,
              w_in, cmp_pe_k, cmp_pe_v, cmp_w1_k, cmp_w2_k, cmp_w1_v, cmp_w2_v,
              w_out, w_up, w_down):
    B, T, _ = x.shape
    splits = np.cumsum(IN_COLS)[:-1].tolist()

    def heads(a, n):
        return a.reshape(B, T, n, -1)

    for l in range(DEPTH):
        mod = c @ w_ada[l] + b_ada[l]
        sh1, sc1, gt1, sh2, sc2, gt2 = jnp.split(mod, 6, axis=-1)

        h = rms_norm_2(x, g_pre_mix[l]) * (1.0 + sc1[:, None]) + sh1[:, None]
        proj = h @ w_in[l]
        (q_n, kc, vc, ksl, vsl, kw, vw, gl,
         q_d, k_d, v_d, qi, ki, wi) = jnp.split(proj, splits, axis=-1)

        o_nsa = nsa_attention(
            rope(heads(q_n, NSA_HEADS), positions),
            rope(heads(kc, NSA_KV), positions), heads(vc, NSA_KV),
            rope(heads(ksl, NSA_KV), positions), heads(vsl, NSA_KV),
            rope(heads(kw, NSA_KV), positions), heads(vw, NSA_KV),
            gl, cmp_pe_k[l], cmp_pe_v[l], cmp_w1_k[l], cmp_w2_k[l], cmp_w1_v[l], cmp_w2_v[l])

        o_dsa = dsa_attention(
            rope(heads(q_d, DSA_HEADS), positions),
            rope(k_d[:, :, None, :], positions)[:, :, 0],
            v_d,
            rope(heads(qi, IDX_HEADS), positions),
            rope(ki[:, :, None, :], positions)[:, :, 0],
            wi)

        o = jnp.concatenate([o_nsa, o_dsa], axis=-1) @ w_out[l]
        x = x + gt1[:, None] * rms_norm_2(o, g_post_mix[l])

        h = rms_norm_2(x, g_pre_ffn[l]) * (1.0 + sc2[:, None]) + sh2[:, None]
        y = jnp.square(jax.nn.relu(h @ w_up[l])) @ w_down[l]
        x = x + gt2[:, None] * rms_norm_2(y, g_post_ffn[l])
    return x


def setup_inputs(seed=0):
    out = dict(first_inputs(seed))
    for name, value in second_inputs(seed + 1).items():
        if name != "x":
            out[name + "_2"] = value
    return out


def reference(
    x, c, positions, ada_w, ada_b, ffn1_norm, ffn1_w_gate, ffn1_w_up, ffn1_w_down, mix_norm,
    w_in, q_norm, w_q_up, kv_norm, w_kv_up, w_fourier_out, w_mla_out, w_out, ffn2_norm,
    ffn2_w_gate, ffn2_w_up, ffn2_w_down, final_norm, c_2, positions_2, w_ada_2, b_ada_2,
    g_pre_mix_2, g_post_mix_2, g_pre_ffn_2, g_post_ffn_2, w_in_2, cmp_pe_k_2, cmp_pe_v_2,
    cmp_w1_k_2, cmp_w2_k_2, cmp_w1_v_2, cmp_w2_v_2, w_out_2, w_up_2, w_down_2,
):
    x = first_block(
        x, c, positions, ada_w, ada_b, ffn1_norm, ffn1_w_gate, ffn1_w_up, ffn1_w_down, mix_norm,
        w_in, q_norm, w_q_up, kv_norm, w_kv_up, w_fourier_out, w_mla_out, w_out, ffn2_norm,
        ffn2_w_gate, ffn2_w_up, ffn2_w_down, final_norm,
    )
    return second_block(
        x, c_2, positions_2, w_ada_2, b_ada_2, g_pre_mix_2, g_post_mix_2, g_pre_ffn_2,
        g_post_ffn_2, w_in_2, cmp_pe_k_2, cmp_pe_v_2, cmp_w1_k_2, cmp_w2_k_2, cmp_w1_v_2,
        cmp_w2_v_2, w_out_2, w_up_2, w_down_2,
    )


_drawn_inputs = setup_inputs


def setup_inputs(seed=0):
    import zlib

    import numpy as np

    out = dict(_drawn_inputs(seed))
    spreads = {}
    factors = {'ada_b': 4.127,
     'ffn1_norm': 8.0,
     'mix_norm': 8.0,
     'q_norm': 8.0,
     'w_q_up': 8.0,
     'kv_norm': 8.0,
     'w_kv_up': 4.817,
     'w_mla_out': 4.517,
     'ffn2_norm': 8.0,
     'b_ada_2': 3.469,
     'g_pre_mix_2': 4.467,
     'g_post_mix_2': 8.0,
     'g_pre_ffn_2': 8.0,
     'g_post_ffn_2': 8.0,
     'cmp_pe_k_2': 8.0,
     'cmp_pe_v_2': 56.514,
     'cmp_w1_k_2': 3.105,
     'cmp_w2_k_2': 3.165}
    for name, (base, spread) in spreads.items():
        noise = np.random.default_rng([zlib.crc32(name.encode()), seed]).standard_normal(out[name].shape)
        drawn = base * np.exp(spread * noise) if base else spread * noise
        out[name] = __import__('jax').numpy.asarray(drawn.astype(out[name].dtype))
    for name, factor in factors.items():
        out[name] = (out[name] * factor).astype(out[name].dtype)
    return out
```

```python
from contextlib import ExitStack

import numpy as np

import concourse.bass as bass
from concourse import mybir

F32 = mybir.dt.float32
F32R = mybir.dt.float32r
I32 = mybir.dt.int32
ALU = mybir.AluOpType
ACT = mybir.ActivationFunctionType
AX = mybir.AxisListType.X

P = 128
D = 1024
T = 512
NC = D // P
NQ = T // P
D_FF = 2816
D_FF_2 = 4096
FOURIER, Q_RANK, KV_RANK, ROPE_1 = 512, 384, 256, 32
MLA_HEADS, NOPE, V_DIM = 8, 64, 64
QK = NOPE + ROPE_1
NSA_HEADS, NSA_KV, HD = 8, 2, 64
IDX_HEADS = 4
CMP_LEN, CMP_STRIDE = 32, 16
N_CMP = (T - CMP_LEN) // CMP_STRIDE + 1
TOPK = min(256, T // 4)
NEG = -1e30
TAKEN = -3e38
EPS = 1e-6
START = 3
SLOT = 2048
N_VEC = 18

IN_Q = FOURIER
IN_KV = IN_Q + Q_RANK
IN_KR = IN_KV + KV_RANK
IN_GATE = IN_KR + ROPE_1
I2 = dict(qn=0, kc=512, vc=640, ks=768, vs=896, kw=1024, vw=1152, gl=1280, qd=1304, kd=1816, vd=1880,
          qi=1944, ki=2200, wi=2264)

ITERS = (6, 5)
FFN_TILES = 2 * sum(ITERS) + 16
W_FFN1 = 0
W_MIX = W_FFN1 + FFN_TILES
W_DFT_D = W_MIX + 5
W_DFT_S = W_DFT_D + 1
W_FO = W_DFT_S + 2
W_QUP = W_FO + 2
W_KVUP = W_QUP + 2
W_GATE = W_KVUP + 1
W_MLA = W_GATE + 8
W_OUT = W_MLA + 2
W_FFN2 = W_OUT + 4
W_IN2 = W_FFN2 + FFN_TILES
W_CMP = W_IN2 + 11
W_OUT2 = W_CMP + 4
W_FFN3 = W_OUT2 + 4
N_TILES = W_FFN3 + 32

ADA_1 = 9 * D // 256
ADA_STEPS = ADA_1 + 6 * D // 256
ADA_START = 8

K_ID, K_R64, K_R96, K_CAUSAL, K_CADD, K_CMUL, K_FREQ = 0, 128, 256, 352, 864, 992, 1120
K_COLS = 1122

V_FFN1, V_MIX, V_FFN2, V_FINAL, V_QN, V_KVN, V_ADA1 = 0, 8, 16, 24, 32, 35, 37
V_ADA2, V_PREMIX, V_POSTMIX, V_PREFFN, V_POSTFFN = 128, 176, 184, 192, 200
V_PE = 256
A_FFN1, A_MIX, A_FFN2, A_PREMIX, A_POSTMIX, A_PREFFN, A_POSTFFN, A_G1, A_G3 = range(0, 72, 8)

X_INIT, X_F1A, X_F1B, X_MIX, X_F2A, X_F2B, X_FINAL, X_ATT, X_END = range(0, 72, 8)


def constants():
    k = np.zeros((P, K_COLS), np.float32)
    k[:, K_ID:K_ID + P] = np.eye(P)
    for d0 in range(0, P, 64):
        for m in range(32):
            k[d0 + m + 32, K_R64 + d0 + m] = -1
            k[d0 + m, K_R64 + d0 + m + 32] = 1
    for m in range(16):
        k[NOPE + m + 16, K_R96 + NOPE + m] = -1
        k[NOPE + m, K_R96 + NOPE + m + 16] = 1
    p = np.arange(P)[:, None]
    k[:, K_CAUSAL:K_CAUSAL + T] = np.where(np.arange(T)[None, :] <= p + T - P, 0, NEG)
    for qc in range(NQ):
        n = np.arange(32)[None, :]
        seen = (n * CMP_STRIDE + CMP_LEN - 1 <= qc * P + p) & (n < N_CMP)
        k[:, K_CADD + 32 * qc:K_CADD + 32 * qc + 32] = np.where(seen, 0, NEG)
        k[:, K_CMUL + 32 * qc:K_CMUL + 32 * qc + 32] = seen
    f1 = np.float32(1) / np.power(np.float32(10000), np.arange(16, dtype=np.float32) * np.float32(2) / np.float32(32))
    k[NOPE:QK, K_FREQ] = np.tile(f1.astype(np.float32), 2)
    f2 = (10000.0 ** (-np.arange(32) / 32)).astype(np.float32)
    k[:, K_FREQ + 1] = np.tile(f2, 4)
    d = 2 * np.pi * np.outer(np.arange(P), np.arange(P)) / P
    dft_d = np.concatenate([np.cos(d), np.sin(d)], 1).astype(np.float32)
    s = 2 * np.pi * (np.outer(np.arange(T), np.arange(T)) % T) / T
    norm = (T * P) ** -0.5
    dft_s = np.stack([np.cos(s) * norm, -np.sin(s) * norm]).astype(np.float32)
    return k, dft_d, dft_s


def build(nc, a, out, debug=None):
    ctx = ExitStack()
    base = -(-nc.sbuf_base // 64) * 64
    used = [base]

    def place(name, shape, dt=F32, at=None):
        n = 4 * int(np.prod(shape[1:]))
        if at is None:
            at = used[0]
            used[0] += -(-n // 32) * 32
        return nc.alloc_sbuf_tensor_at(name, shape, dt, offset=at)

    def sem(name):
        return ctx.enter_context(nc.semaphore(name))

    raw = place("raw", [P, 2, SLOT])
    w_hi = place("w_hi", [P, 2, SLOT], F32R)
    w_lo = place("w_lo", [P, 2, SLOT], F32R)
    xT = place("xT", [P, NC, T])
    h_hi = place("h_hi", [P, NC, T], F32R)
    h_lo = place("h_lo", [P, NC, T], F32R)
    kst = place("kst", [P, K_COLS])
    ones = place("ones", [P, P])
    vec = place("vec", [P, 320])
    mod = place("mod", [P, 120])
    fac = place("fac", [P, 72])
    cT = place("cT", [P, 2, NC])
    eps = place("eps", [P, 2])
    free = place("free", [P, 8])
    rb = place("rb", [P, T])
    sq_sum = place("sq_sum", [P, T])
    std = place("std", [P, T])
    tt = place("tt", [P, 2, T])
    sq = place("sq", [P, 2, T])
    arena = used[0]
    end = nc.sbuf_usable_end
    KB = 1024

    def at(kb):
        assert arena + kb * KB <= end, kb
        return int(arena + kb * KB)

    x_nat = place("x_nat", [P, NQ, D], at=at(0))
    vnat = place("vnat", [P, 3, P], at=at(16))
    pe_nat = place("pe_nat", [32, 2, P], at=at(18))
    g_hi = place("g_hi", [P, 16, T], F32R, at=at(0))
    g_lo = place("g_lo", [P, 16, T], F32R, at=at(32))
    sg = place("sg", [P, 2, T], at=at(64))
    ada = place("ada", [P, 2, NC, 256], at=at(68))
    ada_sum = place("ada_sum", [P, 2, 256], at=at(84))
    assert at(86) and at(88)
    ya = place("ya", [P, NC, T], at=at(0))
    ln_hi = place("ln_hi", [P, 5, T], F32R, at=at(16))
    ln_lo = place("ln_lo", [P, 5, T], F32R, at=at(26))
    lat = place("lat", [P, 5, T], at=at(36))
    kr_raw = place("kr_raw", [QK, T], at=at(86))
    sq_sum2 = place("sq_sum2", [P, T], at=at(88))
    u_hi = place("u_hi", [P, 4, T], F32R, at=at(46))
    u_lo = place("u_lo", [P, 4, T], F32R, at=at(54))
    a_hi = place("a_hi", [P, NQ, 4, 256], F32R, at=at(62))
    a_lo_0 = place("a_lo_0", [P, 2, 4, 256], F32R, at=at(78))
    a_lo_1 = place("a_lo_1", [P, 2, 4, 256], F32R, at=at(0))
    k_all = place("k_all", [QK, MLA_HEADS, T], at=at(46))
    q_all = place("q_all", [QK, MLA_HEADS, T], at=at(62))
    v_all = place("v_all", [P, NQ, T], at=at(78))
    tab1 = place("tab1", [P, 2, T], at=at(36))
    rp_raw1 = place("rp_raw1", [P, 2, T], at=at(40))
    pt1 = place("pt1", [P, 1, NQ, T], at=at(16))
    p1 = place("p1", [P, 3, T], at=at(24))
    o_hi = place("o_hi", [P, 4, T], F32R, at=at(30))
    o_lo = place("o_lo", [P, 4, T], F32R, at=at(38))
    gate = place("gate", [P, 16, T], at=at(46))
    qn = place("qn", [P, 4, T], at=at(0))
    ks = place("ks", [P, 2, T], at=at(8))
    kw = place("kw", [P, 2, T], at=at(12))
    qd = place("qd", [P, 4, T], at=at(16))
    kd = place("kd", [P, T], at=at(24))
    v2 = place("v2", [P, NQ, 320], at=at(26))
    score = place("score", [P, 1152], at=at(31))
    ptc = place("ptc", [P, NSA_KV, T], at=at(36))
    p2 = place("p2", [P, 3, T], at=at(40))
    pt2 = place("pt2", [P, 2, NQ, T], at=at(46))
    blk_hi = place("blk_hi", [P, 2, 32, 32], F32R, at=at(46))
    blk_lo = place("blk_lo", [P, 2, 32, 32], F32R, at=at(54))
    gsig = place("gsig", [P, NQ, 24], at=at(62))
    wsc = place("wsc", [P, NQ, 4], at=at(62.5))
    kcmp = place("kcmp", [P, 64], at=at(62.75))
    vcmp = place("vcmp", [P, 2, 64], at=at(63))
    w2sb = place("w2sb", [P, 3, 64], at=at(63.5))
    hid_k = place("hid_k", [P, 2, 32], at=at(64.25))
    hid_v = place("hid_v", [P, 2, 4, 32], at=at(64.5))
    cs = place("cs", [P, 2, 256], at=at(65.5))
    c8 = place("c8", [P, 4, 8], at=at(67.5))
    tab2 = place("tab2", [P, 2, T], at=at(68))
    rp_raw2 = place("rp_raw2", [P, 2, T], at=at(72))
    kc = place("kc", [P, T + CMP_STRIDE], at=at(76))
    vc = place("vc", [P, T + CMP_STRIDE], at=at(78.25))
    qi = place("qi", [P, 2, T], at=at(80.5))
    ki = place("ki", [P, T], at=at(84.5))
    relu = place("relu", [P, 2, T], at=at(86.5))
    small2 = place("small2", [P, 64], at=at(90.5))
    y2 = place("y2", [P, NC, T], at=at(64))
    small1 = place("small1", [P, 64], at=at(90))
    sg3 = place("sg3", [P, 4, T], at=at(80))
    o_nat = place("o_nat", [P, NQ, D], at=at(0))
    pos1 = place("pos1", [P, T], I32, at=at(44))
    pos2 = place("pos2", [P, T], I32, at=at(86.5))

    ps = ctx.enter_context(nc.psum_tensor("ps", [P, 8, 512], F32))
    B_ADA, B_NORM, B_NORM2 = 4, 5, 6

    raw_in = [sem("raw_in0"), sem("raw_in1")]
    hi_done = sem("hi_done")
    split_done = sem("split_done")
    tile_used = sem("tile_used")
    x_in, kst_in, vec_in, pos_in, w2_in = sem("x_in"), sem("kst_in"), sem("vec_in"), sem("pos_in"), sem("w2_in")
    set_up = sem("set_up")
    x_tr, vec_tr, vec_ready, c_ready = sem("x_tr"), sem("vec_tr"), sem("vec_ready"), sem("c_ready")
    ada_in = [sem("ada_in0"), sem("ada_in1")]
    ada_summed, ada_mm, mod_read, fac_ready = sem("ada_summed"), sem("ada_mm"), sem("mod_read"), sem("fac_ready")
    dve_step, act_step, pool_step = sem("dve_step"), sem("act_step"), sem("pool_step")
    x_ready, y_ready = sem("x_ready"), sem("y_ready")
    n_sq, n_acc, n_sum, n_std, n_rb = (sem(f"norm_{s}") for s in ("sq", "acc", "sum", "std", "rb"))
    l_sq, l_acc, l_sum, l_std, l_rb = (sem(f"lat_{s}") for s in ("sq", "acc", "sum", "std", "rb"))
    h_t, h_hi_done, h_lo_done = sem("h_t"), sem("h_hi_done"), sem("h_lo_done")
    l_t, l_hi_done, l_lo_done = sem("l_t"), sem("l_hi_done"), sem("l_lo_done")
    ffn = [{s: sem(f"ffn{i}_{s}") for s in ("gu", "silu", "hid", "down")} for i in (1, 2)]
    f3 = {s: sem(f"ffn3_{s}") for s in ("up", "relu", "sq", "hid", "down")}
    win_mm, win_hi, win_free = sem("win_mm"), sem("win_hi"), sem("win_free")
    ang, tab_ready, sin_done = sem("ang"), sem("tab_ready"), sem("sin_done")
    rp_mm, rp_raw, rp_rot, rp_out = sem("rp_mm"), sem("rp_raw"), sem("rp_rot"), sem("rp_out")
    kv_mm, kv_ev, kr_copied = sem("kv_mm"), sem("kv_ev"), sem("kr_copied")
    at_s, at_nm, at_exp, at_p, at_tr, at_ev, at_pv = (sem(f"at_{s}") for s in ("s", "nm", "exp", "p", "tr", "ev", "pv"))
    o_hi_done, o_lo_done = sem("o_hi_done"), sem("o_lo_done")
    gate_mm, gate_done, yb_mm, yb_read, yb_sum, yb_hi, yb_lo = (
        sem(s) for s in ("gate_mm", "gate_done", "yb_mm", "yb_read", "yb_sum", "yb_hi", "yb_lo"))
    wo_mm = sem("wo_mm")
    nat_mm, nat_sig, nat_ev = sem("nat_mm"), sem("nat_sig"), sem("nat_ev")
    ix_mm, ix_relu, ix_acc, score_ready = sem("ix_mm"), sem("ix_relu"), sem("ix_acc"), sem("score_ready")
    vc_ev, blk_t, blk_hi_done, blk_lo_done = sem("vc_ev"), sem("blk_t"), sem("blk_hi_done"), sem("blk_lo_done")
    cm_gelu, cm_kv, cm_kv_ev = sem("cm_gelu"), sem("cm_kv"), sem("cm_kv_ev")
    cm_s, cm_sub, cm_exp, cm_p, cm_tr, cm_ev = (sem(f"cmp_{s}") for s in ("s", "sub", "exp", "p", "tr", "ev"))
    out_tr, out_ev, out_done = sem("out_tr"), sem("out_ev"), sem("out_done")
    wo2_mm = sem("wo2_mm")

    ident = kst[:, K_ID:K_ID + P]
    block = ctx.enter_context(nc.Block())

    def w2d(w):
        return w.rearrange("o (k p) m -> p (o k) m", p=P)

    def tile_plan():
        t = {}
        w_in, w_in2 = w2d(a["w_in"]), w2d(a["w_in_2"])

        def whole(src):
            return [(src, 0, src.shape[2], 0)], src.shape[1], src.shape[2]

        for j, (c0, n) in enumerate(((IN_Q, 256), (IN_Q + 256, 256), (IN_KV + P, P + ROPE_1), (0, 256), (256, 256))):
            t[W_MIX + j] = whole(w_in[:, :, c0:c0 + n])
        t[W_DFT_D] = whole(a["dft_d"].rearrange("(k p) m -> p k m", p=P))
        for j in range(2):
            t[W_DFT_S + j] = whole(a["dft_s"][j].rearrange("(k p) m -> p k m", p=P))
            t[W_FO + j] = whole(w2d(a["w_fourier_out"])[:, :, 512 * j:512 * j + 512])
            t[W_QUP + j] = whole(w2d(a["w_q_up"])[:, :, 4 * QK * j:4 * QK * j + 4 * QK])
            t[W_MLA + j] = whole(w2d(a["w_mla_out"])[:, :, 512 * j:512 * j + 512])
        t[W_KVUP] = whole(w2d(a["w_kv_up"]))
        for j in range(8):
            t[W_GATE + j] = whole(w_in[:, :, IN_GATE + 256 * j:IN_GATE + 256 * j + 256])
        for j in range(4):
            t[W_OUT + j] = whole(w2d(a["w_out"])[:, :, 256 * j:256 * j + 256])
            t[W_OUT2 + j] = whole(w2d(a["w_out_2"])[:, :, 256 * j:256 * j + 256])

        def parts(*names):
            loads, c = [], 0
            for name, n in names:
                first = I2[name] if isinstance(name, str) else I2[name[0]] + name[1]
                loads.append((w_in2[:, :, first:first + n], c, n, 0))
                c += n
            return loads, NC, c

        t[W_IN2] = parts(("qi", 256))
        t[W_IN2 + 1] = parts(("kd", HD), ("kd", HD), ("ki", HD), ("ki", HD))
        t[W_IN2 + 2] = parts(("vs", 128), ("vw", 128))
        t[W_IN2 + 3] = parts(("gl", 24), ("vd", 64), ("wi", 4))
        t[W_IN2 + 4] = whole(w_in2[:, :, 0:256])
        t[W_IN2 + 5] = whole(w_in2[:, :, 256:512])
        t[W_IN2 + 6] = whole(w_in2[:, :, I2["kc"]:I2["kc"] + 256])
        for j, name in enumerate(("ks", "kw")):
            t[W_IN2 + 7 + j] = parts(*(((name, HD * g), HD) for g in (0, 0, 1, 1)))
        t[W_IN2 + 9] = whole(w_in2[:, :, I2["qd"]:I2["qd"] + 256])
        t[W_IN2 + 10] = whole(w_in2[:, :, I2["qd"] + 256:I2["qd"] + 512])
        for j, name in enumerate(("cmp_w1_k_2", "cmp_w1_v_2")):
            src = a[name].rearrange("o (l d) j -> d (o l) j", d=HD)
            for u in range(2):
                part = src[:, 16 * u:16 * u + 16, :]
                t[W_CMP + 2 * j + u] = [(part, 0, P, 0), (part, 0, P, HD)], 16, P
        return t

    plan = tile_plan()
    loads_before = [0, 0]
    arrived = {}
    for n in range(N_TILES):
        loads_before[n % 2] += len(plan[n][0]) if n in plan else 1
        arrived[n] = 16 * loads_before[n % 2]

    def slot(t, n, kc, cols):
        return t[:, n % 2, 0:kc * cols].rearrange("p (k c) -> p k c", c=cols)

    def ffn_tiles(i):
        w = (W_FFN1, W_FFN2)[i]
        gate_w, up_w, down_w = (w2d(a[f"ffn{i + 1}_w_{s}"]) for s in ("gate", "up", "down"))
        halves, it0 = [], 0
        for iters in ITERS:
            halves.append((w, it0, iters))
            w += 2 * iters + 8
            it0 += iters
        return halves, gate_w, up_w, down_w

    def signal(ins, s, i, per, tiles=1):
        ins.then_inc(tile_used, tiles) if i % per == per - 1 else ins.then_inc(s, 1)

    def wait_product(eng, s, i, per, n0, tiles=1, before=0):
        if i % per == per - 1:
            eng.wait_ge(tile_used, n0 + (i // per + 1) * tiles)
        else:
            eng.wait_ge(s, before + i // per * (per - 1) + i % per + 1)

    ROT2 = [(W_IN2 + j, c) for j in (0, 1, 4, 5) for c in (0, 1)] + [(W_IN2 + 6, 0)]
    ROT2 += [(W_IN2 + j, c) for j in (7, 8, 9, 10) for c in (0, 1)]

    def wait_rot2(eng, i):
        if ROT2[i][1]:
            eng.wait_ge(tile_used, ROT2[i][0] + 1)
        else:
            eng.wait_ge(rp_mm, 6 + sum(1 - last for _, last in ROT2[:i + 1]))

    @block.sync
    def _(sp):
        sp.dma_start(kst[:], a["kst"]).then_inc(kst_in, 16)
        x_rows = a["x"].rearrange("o (c p) d -> p (o c) d", p=P)
        sp.dma_start(x_nat[:], x_rows).then_inc(x_in, 16)

        def ada_rows(s):
            w, c = (a["ada_w"], 256 * s) if s < ADA_1 else (a["w_ada_2"], 256 * (s - ADA_1))
            return w.rearrange("o (p j) n -> p (o j) n", j=NC), c

        def load_ada(s):
            w, c = ada_rows(s)
            if s >= 2:
                sp.wait_ge(ada_summed, s - 1)
            sp.dma_start(ada[:, s % 2], w[:, :, c:c + 256]).then_inc(ada_in[s % 2], 16)

        def load_tile(n):
            loads, kc, cols = plan[n]
            sp.wait_ge(split_done, n - 1)
            for src, c0, m, p0 in loads:
                sp.dma_start(slot(raw, n, kc, cols)[p0:p0 + src.shape[0], :, c0:c0 + m], src).then_inc(raw_in[n % 2], 16)

        def load_gu(n0, i, w, it0, u, first=False):
            if not first:
                sp.wait_ge(split_done, n0 + 2 * i + u - 1)
            src = w[:, :, bass.ds((i + it0) * 256, 256)]
            sp.dma_start(slot(raw, n0 + u, NC, 256), src).then_inc(raw_in[(n0 + u) % 2], 16)

        def load_down(n0, w, k0, kc, j, u):
            n = n0 + 2 * j + u
            sp.wait_ge(split_done, n - 1)
            sp.dma_start(slot(raw, n, kc, 256), w[:, k0 + u * kc:k0 + u * kc + kc, 256 * j:256 * j + 256]).then_inc(raw_in[n % 2], 16)

        for i in range(2):
            halves, gate_w, up_w, down_w = ffn_tiles(i)
            for half, (n0, it0, iters) in enumerate(halves):
                i0 = 0
                s0 = (ADA_START, ADA_START + 16, 38, 50)[2 * i + half]
                if n0 == 0:
                    for s in range(ADA_START):
                        load_ada(s)
                        if s in (1, 4):
                            load_gu(0, 0, (gate_w, up_w)[s == 4], 0, int(s == 4), first=True)
                    load_ada(s0)
                    load_ada(s0 + 1)
                    i0 = 1
                with sp.Fori(i0, iters) as it:
                    for u, w in enumerate((gate_w, up_w)):
                        load_gu(n0, it, w, it0, u)
                    for u in range(2):
                        s = s0 + u
                        w, c = ada_rows(s)
                        sp.wait_ge(ada_summed, it * 2 + (s - 1))
                        sp.dma_start(ada[:, s % 2], w[:, :, bass.ds(it * 512 + c, 256)]).then_inc(ada_in[s % 2], 16)
                kc = iters
                for j in range(4):
                    for u in range(2):
                        load_down(n0 + 2 * iters, down_w, 2 * it0, kc, j, u)
                    if i == 0 and j % 2 == 0:
                        for u in range(2):
                            load_ada(s0 + 2 * iters + j + u)
            if i == 0:
                for n in range(W_MIX, W_FFN2):
                    load_tile(n)
            else:
                for n in range(W_IN2, W_FFN3):
                    load_tile(n)
                    if n == W_CMP:
                        for j, name in enumerate(("cmp_w2_k_2", "cmp_w2_k_2", "cmp_w2_v_2")):
                            sp.wait_ge(split_done, n)
                            sp.dma_start(w2sb[:, j, :], a[name].rearrange("o p d -> p (o d)")).then_inc(w2_in, 16)
        up_w, down_w = w2d(a["w_up_2"]), w2d(a["w_down_2"])
        for half in range(2):
            n0 = W_FFN3 + 16 * half
            with sp.Fori(0, 4) as it:
                for u in range(2):
                    sp.wait_ge(split_done, it * 2 + (n0 + u - 1))
                    src = up_w[:, :, bass.ds(it * 512 + (2048 * half + 256 * u), 256)]
                    sp.dma_start(slot(raw, n0 + u, NC, 256), src).then_inc(raw_in[(n0 + u) % 2], 16)
            for j in range(4):
                for u in range(2):
                    load_down(n0 + 8, down_w, 16 * half, NC, j, u)
        for m in range(NC):
            sp.wait_ge(out_ev, m + 1)
            sp.dma_start(out.rearrange("o (c p) d -> p (o c) d", p=P)[:, :, P * m:P * m + P],
                         o_nat[:, :, P * m:P * m + P]).then_inc(out_done, 16)
        sp.wait_ge(out_done, 16 * NC)

    @block.gpsimd
    def _(pool):
        def split(n, kc, cols, i=0, per=0, first=False, rows=P):
            size = kc * cols
            src, hi, lo = (t[0:rows, n % 2, 0:size] for t in (raw, w_hi, w_lo))
            pool.wait_ge(raw_in[n % 2], i * (8 * per) + arrived[n])
            if not first:
                pool.wait_ge(tile_used, i * per + (n - 1))
            pool.tensor_tensor(hi[:, 0:8], src[:, 0:8], ones[:, 0:8], ALU.mult)
            hi_rest, src_rest = hi[:, 8:size], src[:, 8:size]
            pool.tensor_scalar(hi_rest, src_rest, 1.0, 1.0, ALU.mult, ALU.mult).then_inc(hi_done, 1)
            pool.wait_ge(hi_done, i * per + (n + 1))
            pool.tensor_tensor(lo, src, hi.bitcast(F32), ALU.subtract).then_inc(split_done, 1)

        def split_down(n0, kc):
            with pool.Fori(0, 4) as j:
                for u in range(2):
                    split(n0 + u, kc, 256, j, 2)

        for i in range(2):
            for n0, it0, iters in ffn_tiles(i)[0]:
                if n0 == 0:
                    pool.wait_ge(set_up, 1)
                    split(0, NC, 256, first=True)
                    split(1, NC, 256, first=True)
                with pool.Fori(1 if n0 == 0 else 0, iters) as it:
                    for u in range(2):
                        split(n0 + u, NC, 256, it, 2)
                split_down(n0 + 2 * iters, iters)
            for n in range(W_MIX, W_FFN2) if i == 0 else range(W_IN2, W_FFN3):
                split(n, *plan[n][1:])
        for half in range(2):
            n0 = W_FFN3 + 16 * half
            with pool.Fori(0, 4) as it:
                for u in range(2):
                    split(n0 + u, NC, 256, it, 2)
            split_down(n0 + 8, NC)

    def mla_units():
        return [dict(q=(lambda h, qc: q_all[:, h, P * qc:P * qc + P]), k=(lambda h, n: k_all[:, h, 0:n]), h=h,
                     width=lambda qc: T, mask=None, gate=None, scale=QK ** -0.5,
                     v=(lambda h, c: v_all[:, c, V_DIM * h:V_DIM * h + V_DIM]), causal=False,
                     first=True, last=True) for h in range(MLA_HEADS)]

    def half_of(t, h, c=None):
        r = HD * (h % 2)
        return t[r:r + HD] if c is None else t[r:r + HD, c]

    def causal_mask(qc):
        return kst[:, K_CAUSAL + T - P * (qc + 1):K_CAUSAL + T]

    SCORE_AT = [None, 0, 256, 640]

    def dsa_mask(qc):
        return causal_mask(0) if qc == 0 else score[:, SCORE_AT[qc]:SCORE_AT[qc] + P * (qc + 1)]

    def block2_units():
        units = []
        for h in range(NSA_HEADS):
            g = h // (NSA_HEADS // NSA_KV)
            for b, k in enumerate((ks, kw)):
                units.append(dict(
                    q=(lambda h, qc: half_of(qn, h, h // 2)[:, P * qc:P * qc + P]),
                    k=(lambda h, n, k=k, g=g: half_of(k, h, g)[:, 0:n]), h=h,
                    width=lambda qc: P * (qc + 1), mask=causal_mask, scale=HD ** -0.5,
                    gate=(lambda qc, h=h, b=b: gsig[:, qc, 3 * h + 1 + b:3 * h + 2 + b]),
                    v=(lambda h, c, b=b, g=g: v2[:, c, P * b + HD * g:P * b + HD * g + HD]), causal=True,
                    first=b == 0, last=b == 1, cmp=g if b == 0 else None))
        for h in range(8):
            units.append(dict(
                q=(lambda h, qc: half_of(qd, h, h // 2)[:, P * qc:P * qc + P]),
                k=(lambda h, n: half_of(kd, h)[:, 0:n]), h=h,
                width=lambda qc: P * (qc + 1), mask=dsa_mask, scale=HD ** -0.5, gate=None,
                v=(lambda h, c: v2[:, c, 256:320]), causal=True, first=True, last=True, cmp=None))
        return units

    ATT = [dict(units=mla_units(), t0=0, u0=0, c0=0, pt=pt1, p=p1, small=small1),
           dict(units=block2_units(), t0=4 * MLA_HEADS, u0=MLA_HEADS, c0=4, pt=pt2, p=p2, small=small2)]
    B_S, B_T, B_O = (0, 1, 2), (3, 5), (6, 7)

    def pairs_done(units, u):
        return sum(x["last"] and x["h"] % 2 == 1 for x in units[:u + 1])

    @block.tensor
    def _(pe):
        def mm3(o, wh, wl, xh, xl, start, stop):
            pe.matmul(o, wh, xh, start=start, stop=False)
            pe.matmul(o, wh, xl, start=False, stop=False)
            return pe.matmul(o, wl, xh, start=False, stop=stop)

        def group(o, n, kc, cols, c0, m, xh, xl, k0=0, start=True, stop=True):
            wh, wl = slot(w_hi, n, kc, cols), slot(w_lo, n, kc, cols)
            for k in range(kc):
                last = mm3(o, wh[:, k, c0:c0 + m], wl[:, k, c0:c0 + m], xh[:, k0 + k], xl[:, k0 + k],
                           start and k == 0, stop and k == kc - 1)
            return last

        def norm_sum(i):
            pe.wait_ge(n_acc, 8 * i + 8)
            if i:
                pe.wait_ge(n_std, i)
            pe.matmul(ps[:, B_NORM], ones[:], sq_sum[:], start=True, stop=True).then_inc(n_sum, 1)

        def ada_mm_step(s, i=0, per=0, col=None):
            pe.wait_ge(ada_summed, i * per + (s + 1))
            for half in range(2):
                c = 2 * s + half
                o = ps[:, B_ADA, c:c + 1] if per == 0 else ps[:, B_ADA, bass.ds(i * (2 * per) + c, 1)]
                last = pe.matmul(o, ada_sum[:, s % 2, P * half:P * half + P], ones[:, 0:1], start=True, stop=True)
            last.then_inc(ada_mm, 1)

        pe.wait_ge(kst_in, 16)
        pe.wait_ge(x_in, 16)
        for m in range(NC):
            if m >= 4:
                pe.wait_ge(x_ready, X_INIT + m - 3)
            for c in range(NQ):
                last = pe.transpose(ps[:, m % 4, P * c:P * c + P], x_nat[:, c, P * m:P * m + P], ident)
            last.then_inc(x_tr, 1)
        pe.wait_ge(vec_in, 16 * N_VEC)
        pe.transpose(ps[:, B_NORM2, 0:109], vnat[0:109, 0, :], ident[0:109, 0:109])
        pe.transpose(ps[:, B_NORM2, 128:208], vnat[0:80, 1, :], ident[0:80, 0:80])
        for j in range(2):
            last = pe.transpose(ps[:, B_NORM2, V_PE + 32 * j:V_PE + 32 * j + 32], pe_nat[:, j, :], ident[0:32, 0:32])
        last.then_inc(vec_tr, 1)
        pe.wait_ge(set_up, 1)
        norm_sum(0)
        for s in range(ADA_START):
            ada_mm_step(s)

        def run_ffn(i):
            f = ffn[i]
            halves = ffn_tiles(i)[0]
            pe.wait_ge(h_lo_done, (8, 24)[i])
            for half, (n0, it0, iters) in enumerate(halves):
                s0 = (ADA_START, ADA_START + 16, 38, 50)[2 * i + half]
                x0 = ((X_F1A, X_F1B), (X_F2A, X_F2B))[i][half]
                if half:
                    pe.wait_ge(x_ready, x0)
                pe.wait_ge(mod_read, (1, 2, 3, 3)[2 * i + half])
                with pe.Fori(0, iters) as it:
                    for u in range(2):
                        pe.wait_ge(split_done, it * 2 + (n0 + u + 1))
                        pe.wait_ge((f["silu"], f["hid"])[u], it * 2 + (2 * it0 + START))
                        for m in range(2):
                            last = group(ps[:, 2 * u + m], n0 + u, NC, 256, P * m, P, h_hi, h_lo)
                            if m == 0:
                                last.then_inc(f["gu"], 1)
                        last.then_inc(tile_used, 1)
                    for u in range(2):
                        ada_mm_step(s0 + u, it, 2)
                pe.wait_ge(f["hid"], 2 * (it0 + iters) + START)
                if i == 0:
                    pe.wait_ge(mod_read, 2)
                n1 = n0 + 2 * iters
                with pe.Fori(0, 2) as jj:
                    for jo in range(2):
                        pe.wait_ge(x_ready, jj * 4 + (x0 + 2 * jo - 2))
                        for u in range(2):
                            n = n1 + 2 * jo + u
                            pe.wait_ge(split_done, jj * 4 + (n + 1))
                            for m in range(2):
                                last = group(ps[:, 2 * jo + m], n, iters, 256, P * m, P, g_hi, g_lo,
                                             k0=iters * u, start=u == 0, stop=u == 1)
                            last.then_inc(tile_used, 1)
                    if i == 0:
                        for u in range(2):
                            ada_mm_step(s0 + 2 * iters + u, jj, 2)

        run_ffn(0)

        norm_sum(1)
        pe.wait_ge(h_lo_done, 16)

        def win_group(g, n, kc, cols, c0, m, xh, xl):
            if g >= 4:
                pe.wait_ge(win_free, g - 3)
            return group(ps[0:m, g % 4], n, kc, cols, c0, m, xh, xl)

        g = 0
        for j, outs in enumerate((((0, P), (P, P)), ((0, P), (P, P)), ((0, P), (64, QK)), ((0, P), (P, P)), ((0, P), (P, P)))):
            n = W_MIX + j
            pe.wait_ge(split_done, n + 1)
            for c0, m in outs:
                last = win_group(g, n, NC, plan[n][2], c0, m, h_hi, h_lo)
                signal(last, win_mm, g, 2)
                g += 1
        for i, (b, s) in enumerate(((B_NORM, sq_sum), (B_NORM2, sq_sum2))):
            pe.wait_ge(l_acc, (3, 5)[i])
            pe.matmul(ps[:, b], ones[:], s[:], start=True, stop=True).then_inc(l_sum, 1)
        n = W_DFT_D
        pe.wait_ge(split_done, n + 1)
        ch, cl = slot(w_hi, n, 1, 256)[:, 0], slot(w_lo, n, 1, 256)[:, 0]
        for gr in range(4):
            for sp2 in range(2):
                pe.wait_ge(win_free, g - 3)
                if sp2 == 0:
                    pe.wait_ge(win_free, 7 + gr)
                for c in range(2):
                    s = slice(P * (2 * sp2 + c), P * (2 * sp2 + c) + P)
                    last = mm3(ps[:, g % 4, 256 * c:256 * c + 256], u_hi[:, gr, s], u_lo[:, gr, s], ch, cl, True, True)
                signal(last, win_mm, g - 10, 8)
                g += 1
        pe.wait_ge(split_done, W_DFT_S + 2)
        for gr in range(4):
            pe.wait_ge(win_free, max(g - 3, 18))
            for j in range(2):
                th, tl = slot(w_hi, W_DFT_S + j, 4, T), slot(w_lo, W_DFT_S + j, 4, T)
                for c in range(NQ):
                    lo = (a_lo_0, a_lo_1)[c // 2][:, c % 2, gr, P * j:P * j + P]
                    last = mm3(ps[:, g % 4], a_hi[:, c, gr, P * j:P * j + P], lo, th[:, c], tl[:, c],
                               j == 0 and c == 0, j == 1 and c == NQ - 1)
            signal(last, win_mm, gr, 4, tiles=2)
            g += 1
        for j in range(2):
            n = W_FO + j
            pe.wait_ge(split_done, n + 1)
            for m in range(4):
                pe.wait_ge(win_free, max(g - 3, 22))
                signal(group(ps[:, g % 4], n, 4, 512, P * m, P, u_hi, u_lo), win_mm, m, 4)
                g += 1

        pe.wait_ge(win_free, 30)
        pe.wait_ge(l_lo_done, 5)

        def rot(r, lhs, rows, src):
            pe.wait_ge(rp_raw, r + 1)
            if r >= 2:
                pe.wait_ge(rp_out, r - 1)
            pe.matmul(ps[0:rows, 2 + r % 2], lhs, src[0:rows, r % 2], start=True, stop=True).then_inc(rp_rot, 1)

        R96 = kst[0:QK, K_R96:K_R96 + QK]
        for r in range(10):
            if 1 <= r <= 8:
                h = r - 1
                if h % 4 == 0:
                    pe.wait_ge(split_done, W_QUP + h // 4 + 1)
                if r >= 3:
                    pe.wait_ge(rp_raw, r - 1)
                signal(group(ps[0:QK, r % 2], W_QUP + h // 4, 3, 4 * QK, QK * (h % 4), QK, ln_hi, ln_lo), rp_mm, h, 4)
            if r >= 1:
                rot(r - 1, R96, QK, rp_raw1)
        n = W_KVUP
        pe.wait_ge(split_done, n + 1)
        pe.wait_ge(l_std, 2)
        for h in range(MLA_HEADS):
            if h >= 3:
                pe.wait_ge(kv_ev, h - 2)
            group(ps[0:NOPE, 5 + h % 3], n, 2, 1024, P * h, NOPE, ln_hi, ln_lo, k0=3).then_inc(kv_mm, 1)
        vh, vl = (slot(t, n, 2, 1024).rearrange("p k (h c) -> p k h c", c=P) for t in (w_hi, w_lo))
        for c in range(NQ):
            i = MLA_HEADS + c
            pe.wait_ge(kv_ev, i - 2)
            for k in range(2):
                s = slice(P * c, P * c + P)
                last = mm3(ps[:, 5 + i % 3], ln_hi[:, 3 + k, s], ln_lo[:, 3 + k, s],
                           vh[:, k, :, NOPE:P], vl[:, k, :, NOPE:P], k == 0, k == 1)
            signal(last, kv_mm, i, MLA_HEADS + NQ)

        def attention(att):
            units, t0, u0, pt = att["units"], att["t0"], att["u0"], att["pt"]
            np_ = pt.shape[1]
            steps = 4 * len(units)

            def scores(t):
                x, qc = units[t // 4], t % 4
                if t >= 3:
                    pe.wait_ge(at_exp, t0 + t - 2)
                w = x["width"](qc)
                pe.matmul(ps[:, B_S[t % 3], 0:w], x["q"](x["h"], qc), x["k"](x["h"], w),
                          start=True, stop=True).then_inc(at_s, 1)

            def transposes(t):
                x, qc = units[t // 4], t % 4
                pe.wait_ge(at_p, t0 + t + 1)
                if t >= 2:
                    pe.wait_ge(at_ev, t0 + t - 1)
                for c in range(x["width"](qc) // P):
                    last = pe.transpose(ps[:, B_T[t % 2], P * c:P * c + P],
                                        att["p"][:, t % 3, P * c:P * c + P], ident)
                last.then_inc(at_tr, 1)

            def values(u):
                x = units[u]
                h = x["h"]
                r = HD * (h % 2)
                pair = pairs_done(units, u - 1) if u else 0
                o = ps[r:r + HD, B_O[pair % 2]]
                pe.wait_ge(at_ev, t0 + 4 * u + 4)
                if x["first"] and h % 2 == 0 and pair >= 2:
                    pe.wait_ge(o_lo_done, att["c0"] + pair - 1)
                if x.get("cmp") is not None:
                    c = 32 * (h % 4)
                    pe.matmul(o, vcmp[c:c + 32, x["cmp"], :], ptc[c:c + 32, x["cmp"], :], start=True, stop=False,
                              tile_position=(c, r))
                for c in range(NQ):
                    q0 = P * c if x["causal"] else 0
                    last = pe.matmul(o[:, q0:T], x["v"](h, c), pt[:, u % np_, c, q0:T],
                                     start=c == 0 and x["first"] and x.get("cmp") is None,
                                     stop=x["last"] and c == NQ - 1)
                last.then_inc(at_pv, 1)

            for t in range(steps + 3):
                if t < steps:
                    scores(t)
                if 2 <= t < steps + 2:
                    transposes(t - 2)
                if t >= 6 and (t - 2) % 4 == 0:
                    values((t - 6) // 4)
            assert (steps + 2 - 2) % 4 == 0

        pe.wait_ge(rp_out, 9)
        pe.wait_ge(kv_ev, MLA_HEADS + NQ)
        pe.wait_ge(kr_copied, 8)
        attention(ATT[0])

        for i in range(16):
            n = W_GATE + i // 2
            if i % 2 == 0:
                pe.wait_ge(split_done, n + 1)
            if i >= 4:
                pe.wait_ge(gate_done, i - 3)
            last = group(ps[:, i % 4], n, NC, 256, P * (i % 2), P, h_hi, h_lo)
            signal(last, gate_mm, i, 2)
        pe.wait_ge(o_lo_done, 4)
        for i in range(8):
            n = W_MLA + i // 4
            if i % 4 == 0:
                pe.wait_ge(split_done, n + 1)
            pe.wait_ge(gate_done, 13 + i) if i < 4 else pe.wait_ge(yb_read, i - 3)
            signal(group(ps[:, i % 4], n, 4, 512, P * (i % 4), P, o_hi, o_lo), yb_mm, i, 4)
        pe.wait_ge(yb_lo, 8)
        for i in range(8):
            n = W_OUT + i // 2
            if i % 2 == 0:
                pe.wait_ge(split_done, n + 1)
            pe.wait_ge(yb_read, 5 + i) if i < 4 else pe.wait_ge(x_ready, X_MIX + i - 3)
            signal(group(ps[:, i % 4], n, NC, 256, P * (i % 2), P, h_hi, h_lo), wo_mm, i, 2)
        norm_sum(2)
        run_ffn(1)
        norm_sum(3)
        norm_sum(4)

        pe.wait_ge(h_lo_done, 32)
        R64 = kst[:, K_R64:K_R64 + P]
        pend = [None]
        r = [0]

        def flush():
            if pend[0] is not None:
                rot(9 + pend[0], R64, P, rp_raw2)
                pend[0] = None

        def proj(n, half):
            i = 9 + r[0]
            pe.wait_ge(rp_raw, i - 1)
            signal(group(ps[:, i % 2], n, NC, 256, P * half, P, h_hi, h_lo), rp_mm, half, 2)
            flush()
            pend[0] = r[0]
            r[0] += 1

        def next_tile(n):
            pe.wait_ge(split_done, n + 1)

        n = W_IN2
        next_tile(n)
        for c in range(2):
            proj(n, c)
        n = W_IN2 + 1
        next_tile(n)
        for c in range(2):
            proj(n, c)
        flush()
        next_tile(W_IN2 + 3)
        for c in range(NQ):
            s = slice(P * c, P * c + P)
            for j, (cols, c0) in enumerate(((256, 0), (92, 256))):
                th, tl = slot(w_hi, W_IN2 + 2 + j, NC, cols), slot(w_lo, W_IN2 + 2 + j, NC, cols)
                if j == 0 and c >= 2:
                    pe.wait_ge(nat_ev, c - 1)
                for k in range(NC):
                    last = mm3(ps[:, 6 + c % 2, c0:c0 + cols], h_hi[:, k, s], h_lo[:, k, s], th[:, k], tl[:, k],
                               k == 0, k == NC - 1)
            signal(last, nat_mm, c, NQ, tiles=2)
        pe.wait_ge(rp_out, 9 + 4)
        pe.wait_ge(nat_ev, 4)
        for j in range(12):
            qc, h = 1 + j // 4, j % 4
            if j >= 2:
                pe.wait_ge(ix_relu, j - 1)
            w = P * (qc + 1)
            pe.matmul(ps[:, 6 + j % 2, 0:w], half_of(qi, h, h // 2)[:, P * qc:P * qc + P], half_of(ki, h)[:, 0:w],
                      start=True, stop=True).then_inc(ix_mm, 1)
        for j in range(2):
            next_tile(W_IN2 + 4 + j)
            for c in range(2):
                proj(W_IN2 + 4 + j, c)
            n = W_IN2 + 6
        next_tile(n)
        proj(n, 0)
        flush()
        pe.wait_ge(ix_relu, 11)
        group(ps[:, 6], n, NC, 256, P, P, h_hi, h_lo).then_inc(tile_used, 1)
        for j in range(4):
            next_tile(W_IN2 + 7 + j)
            for c in range(2):
                proj(W_IN2 + 7 + j, c)
        flush()

        for j in range(2):
            pe.wait_ge(blk_lo_done, j + 1)
            pe.wait_ge(vc_ev, 1)
            if j:
                pe.wait_ge(cm_gelu, 1)
            for u in range(2):
                n = W_CMP + 2 * j + u
                next_tile(n)
                wh, wl = slot(w_hi, n, 16, P), slot(w_lo, n, 16, P)
                for gr in range(2):
                    rows = slice(HD * gr, HD * gr + HD)
                    for l in range(16):
                        last = mm3(ps[:, (5, 7)[gr], 0:32], wh[rows, l], wl[rows, l],
                                   blk_hi[rows, j, 16 * u + l], blk_lo[rows, j, 16 * u + l],
                                   u == 0 and l == 0, u == 1 and l == 15)
                last.then_inc(tile_used, 1)
        pe.wait_ge(w2_in, 48)
        pe.wait_ge(cm_gelu, 2)
        pe.matmul(ps[:, 6, 0:64], w2sb[:, 0:2, :], hid_k[:, :, :], start=True, stop=True)
        for gr in range(2):
            last = pe.matmul(ps[:, 6, 64 + 64 * gr:128 + 64 * gr], hid_v[:, gr, :, :], w2sb[:, 2, :],
                             start=True, stop=True)
        last.then_inc(cm_kv, 1)
        pe.wait_ge(cm_kv_ev, 1)
        pe.wait_ge(rp_out, 9 + 17)
        for qc in range(NQ):
            if qc >= 2:
                pe.wait_ge(cm_sub, qc - 1)
            for h in range(NSA_HEADS):
                gr = h // 4
                last = pe.matmul(ps[:, 5 - qc % 2 + 2 * (h % 2), 32 * (h // 2):32 * (h // 2) + 32],
                                 half_of(qn, h, h // 2)[:, P * qc:P * qc + P],
                                 half_of(kcmp, h)[:, 32 * gr:32 * gr + 32], start=True, stop=True)
            last.then_inc(cm_s, 1)
        for qc in range(NQ):
            pe.wait_ge(cm_p, qc + 1)
            if qc >= 2:
                pe.wait_ge(cm_ev, qc - 1)
            for gr in range(2):
                last = pe.transpose(ps[:, 3 * (qc % 2), P * gr:P * gr + P], cs[:, qc % 2, P * gr:P * gr + P], ident)
            last.then_inc(cm_tr, 1)
        pe.wait_ge(cm_ev, NQ)
        attention(ATT[1])

        pe.wait_ge(o_lo_done, 12)
        for i in range(8):
            n = W_OUT2 + i // 2
            if i % 2 == 0:
                next_tile(n)
            if i >= 4:
                pe.wait_ge(y_ready, i - 3)
            signal(group(ps[:, i % 4], n, NC, 256, P * (i % 2), P, h_hi, h_lo), wo2_mm, i, 2)
        norm_sum(5)
        norm_sum(6)

        pe.wait_ge(h_lo_done, 40)
        for half in range(2):
            n0 = W_FFN3 + 16 * half
            if half:
                pe.wait_ge(y_ready, 16)
            with pe.Fori(0, 4) as it:
                for u in range(2):
                    pe.wait_ge(split_done, it * 2 + (n0 + u + 1))
                    pe.wait_ge(f3["relu"], it * 4 + (16 * half - 2 + 2 * u + START))
                    for m in range(2):
                        last = group(ps[:, 2 * u + m], n0 + u, NC, 256, P * m, P, h_hi, h_lo)
                        if m == 0:
                            last.then_inc(f3["up"], 1)
                    last.then_inc(tile_used, 1)
            pe.wait_ge(f3["hid"], 16 * half + 16 + START)
            n1 = n0 + 8
            with pe.Fori(0, 2) as jj:
                for jo in range(2):
                    pe.wait_ge(y_ready, jj * 4 + (8 * half + 8 + 2 * jo - 2))
                    for u in range(2):
                        n = n1 + 2 * jo + u
                        pe.wait_ge(split_done, jj * 4 + (n + 1))
                        for m in range(2):
                            last = group(ps[:, 2 * jo + m], n, NC, 256, P * m, P, g_hi, g_lo,
                                         k0=8 * u, start=u == 0, stop=u == 1)
                        last.then_inc(tile_used, 1)
        norm_sum(7)
        for m in range(NC):
            pe.wait_ge(x_ready, X_END + m + 1)
            if m >= 4:
                pe.wait_ge(out_ev, m - 3)
            for c in range(NQ):
                last = pe.transpose(ps[:, m % 4, P * c:P * c + P], xT[:, m, P * c:P * c + P], ident)
            last.then_inc(out_tr, 1)

    def norm_squares(act, i, ready, first, src):
        for m in range(NC):
            act.wait_ge(ready, first + m + 1)
            if 8 * i + m >= 2:
                act.wait_ge(n_acc, 8 * i + m - 1)
            act.activation(sq[:, m % 2], src[:, m], ACT.Square).then_inc(n_sq, 1)

    def norm_root(act, i):
        act.wait_ge(n_sum, i + 1)
        if i:
            act.wait_ge(n_rb, i)
        act.activation(std[:], ps[:, B_NORM], ACT.Sqrt, scale=1.0 / D, bias=eps[:, 0:1]).then_inc(n_std, 1)

    def mod_high(act, i, shift):
        for m in range(NC):
            act.wait_ge(h_t, 8 * i + m + 1)
            act.activation(h_hi[:, m], tt[:, m % 2], ACT.Identity, bias=mod[:, shift + m:shift + m + 1]).then_inc(h_hi_done, 1)

    @block.scalar
    def _(act):
        def step(ins):
            steps[0] += 1
            ins.then_inc(act_step, 1)
            act.wait_ge(act_step, steps[0])
        steps = [0]

        def rows(v, lo, n, r, c=0):
            src = v.rearrange("o (m p) -> (o m) p", p=P) if len(v.shape) == 2 else v.rearrange("(m p) -> m p", p=P)
            act.dma_start(vnat[r:r + n, c, :], src[lo:lo + n]).then_inc(vec_in, 16)

        for j, name in enumerate(("c", "c_2")):
            act.dma_start(cT[:, j, :], a[name].rearrange("o (p j) -> p (o j)", j=NC)).then_inc(vec_in, 16)
        for name, n, r in (("ffn1_norm", 8, V_FFN1), ("mix_norm", 8, V_MIX), ("ffn2_norm", 8, V_FFN2),
                           ("final_norm", 8, V_FINAL), ("q_norm", 3, V_QN), ("kv_norm", 2, V_KVN), ("ada_b", 72, V_ADA1)):
            rows(a[name], 0, n, r)
        for name, n, r in (("b_ada_2", 48, V_ADA2), ("g_pre_mix_2", 8, V_PREMIX), ("g_post_mix_2", 8, V_POSTMIX),
                           ("g_pre_ffn_2", 8, V_PREFFN), ("g_post_ffn_2", 8, V_POSTFFN)):
            rows(a[name], 0, n, r - P, 1)
        for j, name in enumerate(("cmp_pe_k_2", "cmp_pe_v_2")):
            for u in range(2):
                act.dma_start(pe_nat[:, j, HD * u:HD * u + HD], a[name].rearrange("o l d -> (o l) d")).then_inc(vec_in, 16)
        act.wait_ge(vec_in, 16 * N_VEC)
        act.activation(cT[:, 0, :], cT[:, 0, :], ACT.Silu).then_inc(c_ready, 1)
        act.wait_ge(set_up, 1)
        norm_squares(act, 0, x_ready, X_INIT, xT)
        norm_root(act, 0)
        mod_high(act, 0, 0)

        def run_ffn(i):
            f = ffn[i]
            for half, (n0, it0, iters) in enumerate(ffn_tiles(i)[0]):
                with act.Fori(0, iters) as it:
                    for m in range(2):
                        act.wait_ge(f["gu"], it * 2 + (2 * it0 + 1)) if m == 0 else act.wait_ge(tile_used, it * 2 + (n0 + 1))
                        act.wait_ge(f["hid"], it * 2 + (2 * it0 + START))
                        act.activation(sg[:, m], ps[:, m], ACT.Silu).then_inc(f["silu"], 1)
            norm_squares(act, (1, 3)[i], x_ready, (X_F1B, X_F2B)[i], xT)

        run_ffn(0)
        norm_root(act, 1)
        mod_high(act, 1, 24)

        for j in range(5):
            act.wait_ge(win_free, j + 1)
            act.wait_ge(l_acc, j - 1) if j >= 2 else act.wait_ge(n_acc, 16)
            act.activation(sq[:, j % 2], lat[:, j], ACT.Square).then_inc(l_sq, 1)
        for j in range(4):
            wait_product(act, win_mm, 6 + j, 2, W_MIX)
            act.copy(u_hi[:, j], ps[:, (6 + j) % 4]).then_inc(win_hi, 1)
        for i, (b, dst, n) in enumerate(((B_NORM, std, Q_RANK), (B_NORM2, rb, KV_RANK))):
            act.wait_ge(l_sum, i + 1)
            act.wait_ge(h_lo_done, 16)
            act.activation(dst[:], ps[:, b], ACT.Sqrt, scale=1.0 / n, bias=eps[:, 0:1]).then_inc(l_std, 1)
        for j in range(5):
            act.wait_ge(l_t, j + 1)
            act.copy(ln_hi[:, j], tt[:, j % 2]).then_inc(l_hi_done, 1)
        for j in range(8):
            g = 10 + j
            wait_product(act, win_mm, j, 8, W_DFT_D, before=5)
            act.copy(a_hi[:, 2 * (j % 2):2 * (j % 2) + 2, j // 2, :],
                     ps[:, g % 4].rearrange("p (c m) -> p c m", c=2)).then_inc(win_hi, 1)
        for j in range(4):
            g = 18 + j
            wait_product(act, win_mm, j, 4, W_DFT_S, tiles=2, before=12)
            act.copy(u_hi[:, j], ps[:, g % 4]).then_inc(win_hi, 1)

        def sines(tab, src):
            b = src
            act.wait_ge(ang, 2 * b + 1)
            act.activation(tab[:, 0], tt[:, 0], ACT.Sin, scale=0.5).then_inc(sin_done, 1)
            act.wait_ge(ang, 2 * b + 2)
            act.activation(tab[:, 1], tt[:, 1], ACT.Sin, scale=-0.5, bias=eps[:, 1:2]).then_inc(sin_done, 1)

        act.wait_ge(l_t, 5)
        act.dma_start(pos1[:], a["positions"].broadcast_to([P, T])).then_inc(pos_in, 16)
        sines(tab1, 0)
        for r in range(9):
            if r >= 2:
                act.wait_ge(rp_out, r - 1)
            if r == 0:
                act.wait_ge(win_free, 30)
                act.copy(rp_raw1[0:QK, 0], kr_raw[:]).then_inc(rp_raw, 1)
            else:
                wait_product(act, rp_mm, r - 1, 4, W_QUP)
                act.copy(rp_raw1[0:QK, r % 2], ps[0:QK, r % 2]).then_inc(rp_raw, 1)
        for i in range(MLA_HEADS + NQ):
            wait_product(act, kv_mm, i, MLA_HEADS + NQ, W_KVUP)
            if i < MLA_HEADS:
                act.copy(k_all[0:NOPE, i], ps[0:NOPE, 5 + i % 3]).then_inc(kv_ev, 1)
            else:
                act.copy(v_all[:, i - MLA_HEADS], ps[:, 5 + i % 3]).then_inc(kv_ev, 1)

        def attention(att, oh, first_chunk):
            units, t0, u0, pt, p, small = (att[k] for k in ("units", "t0", "u0", "pt", "p", "small"))
            np_ = pt.shape[1]
            steps = 4 * len(units)

            def exps(t):
                x, qc = units[t // 4], t % 4
                w = x["width"](qc)
                act.wait_ge(at_nm, t0 + t + 1)
                if t >= 3:
                    act.wait_ge(at_tr, t0 + t - 2)
                src = ps[:, B_S[t % 3], 0:w] if x["mask"] is None else p[:, t % 3, 0:w]
                act.activation(p[:, t % 3, 0:w], src, ACT.Exp, bias=small[:, 8 + t % 8:9 + t % 8], scale=x["scale"],
                               accum_out=small[:, 16 + t % 8:17 + t % 8]).then_inc(at_exp, 1)

            def turn(t):
                x, qc = units[t // 4], t % 4
                u = t // 4
                n = x["width"](qc) // P
                act.wait_ge(at_tr, t0 + t + 1)
                if u >= np_:
                    act.wait_ge(at_pv, u0 + u - np_ + 1)
                act.copy(pt[:, u % np_, 0:n, P * qc:P * qc + P],
                         ps[:, B_T[t % 2], 0:P * n].rearrange("p (c q) -> p c q", q=P)).then_inc(at_ev, 1)

            def out_high(u):
                x = units[u]
                if x["last"] and x["h"] % 2:
                    act.wait_ge(at_pv, u0 + u + 1)
                    pair = pairs_done(units, u) - 1
                    act.copy(oh[:, pair], ps[:, B_O[pair % 2]]).then_inc(o_hi_done, 1)

            for t in range(steps + 4):
                if t < steps:
                    exps(t)
                if 2 <= t < steps + 2:
                    turn(t - 2)
                if t >= 7 and (t - 3) % 4 == 0:
                    out_high((t - 7) // 4)

        act.wait_ge(l_lo_done, 5)
        attention(ATT[0], o_hi, 0)
        for i in range(16):
            wait_product(act, gate_mm, i, 2, W_GATE)
            act.activation(gate[:, i], ps[:, i % 4], ACT.Sigmoid).then_inc(gate_done, 1)
        for i in range(8):
            act.wait_ge(yb_sum, i + 1)
            act.copy(h_hi[:, i], tt[:, i % 2]).then_inc(yb_hi, 1)
        norm_squares(act, 2, x_ready, X_MIX, xT)
        norm_root(act, 2)
        mod_high(act, 2, 48)
        run_ffn(1)
        norm_root(act, 3)
        norm_squares(act, 4, x_ready, X_FINAL, xT)
        norm_root(act, 4)
        mod_high(act, 3, 72)

        act.dma_start(pos2[:], a["positions_2"].broadcast_to([P, T])).then_inc(pos_in, 16)
        sines(tab2, 1)

        def raw_copy(i):
            wait_rot2(act, i)
            act.wait_ge(rp_out, 9 + i - 1)
            act.copy(rp_raw2[:, (9 + i) % 2], ps[:, (9 + i) % 2]).then_inc(rp_raw, 1)

        for i in range(4):
            raw_copy(i)
        for c in range(NQ):
            wait_product(act, nat_mm, c, NQ, W_IN2 + 2, tiles=2)
            act.activation(gsig[:, c, :], ps[:, 6 + c % 2, 256:280], ACT.Sigmoid).then_inc(nat_sig, 1)
        for j in range(12):
            act.wait_ge(ix_mm, j + 1)
            if j >= 2:
                act.wait_ge(ix_acc, j - 1)
            w = P * (2 + j // 4)
            act.activation(relu[:, j % 2, 0:w], ps[:, 6 + j % 2, 0:w], ACT.Relu).then_inc(ix_relu, 1)
        for i in range(4, 9):
            raw_copy(i)
        act.wait_ge(tile_used, W_IN2 + 7)
        act.copy(vc[:, 0:T], ps[:, 6]).then_inc(vc_ev, 1)
        for i in range(9, 17):
            raw_copy(i)
            if i in (12, 14):
                j = (i - 12) // 2
                act.wait_ge(blk_t, 2 * j + 2)
                act.copy(blk_hi[:, j].rearrange("p l n -> p (l n)"), tt[:].rearrange("p a b -> p (a b)")).then_inc(blk_hi_done, 1)
        for j in range(2):
            act.wait_ge(tile_used, W_CMP + 2 * j + 2)
            if j == 0:
                for gr in range(2):
                    last = act.activation(hid_k[:, gr, 0:N_CMP], ps[:, (5, 7)[gr], 0:N_CMP], ACT.Gelu_apprx_tanh)
            else:
                for gr in range(2):
                    for rep in range(4):
                        last = act.activation(hid_v[:, gr, rep, 0:N_CMP], ps[:, (5, 7)[gr], 0:N_CMP], ACT.Gelu_apprx_tanh)
            last.then_inc(cm_gelu, 1)
        for qc in range(NQ):
            act.wait_ge(cm_sub, qc + 1)
            act.activation(cs[:, qc % 2], cs[:, qc % 2], ACT.Exp, scale=HD ** -0.5).then_inc(cm_exp, 1)
        for qc in range(NQ):
            act.wait_ge(cm_tr, qc + 1)
            act.copy(ptc[:, :, P * qc:P * qc + P],
                     ps[:, 3 * (qc % 2), 0:2 * P].rearrange("p (g q) -> p g q", g=2)).then_inc(cm_ev, 1)
        attention(ATT[1], h_hi, 0)

        norm_squares(act, 5, y_ready, 0, y2)
        norm_root(act, 5)
        norm_squares(act, 6, x_ready, X_ATT, xT)
        norm_root(act, 6)
        mod_high(act, 4, 72 + 24)
        for half in range(2):
            n0 = W_FFN3 + 16 * half
            with act.Fori(0, 4) as it:
                for j in range(4):
                    u, m = j // 2, j % 2
                    act.wait_ge(f3["up"], it * 2 + (8 * half + u + 1)) if m == 0 else act.wait_ge(tile_used, it * 2 + (n0 + u + 1))
                    act.wait_ge(f3["sq"], it * 4 + (16 * half + START))
                    act.activation(sg3[:, j], ps[:, j], ACT.Relu).then_inc(f3["relu"], 1)
        norm_squares(act, 7, y_ready, 16, y2)
        norm_root(act, 7)

    @block.vector
    def _(dve):
        count = [0]

        def step(ins):
            count[0] = count[0] + 1
            ins.then_inc(dve_step, 1)
            dve.wait_ge(dve_step, count[0])

        def column(t, c):
            return t[:, c:c + 1]

        step(dve.memset(eps[:, 0:1], EPS))
        step(dve.memset(eps[:, 1:2], float(np.pi / 2)))
        dve.memset(ones[:], 1.0).then_inc(set_up, 1)
        for k, s in enumerate([f[name] for f in ffn for name in ("silu", "hid")] + [f3[name] for name in ("relu", "sq", "hid")]):
            dve.memset(free[:, k:k + 1], 0.0).then_inc(s, START)

        def norm_add(i, m):
            dve.wait_ge(n_sq, 8 * i + m + 1)
            if m == 0:
                if i:
                    dve.wait_ge(n_sum, i)
                    dve.wait_ge(n_acc, 8 * i)
                dve.tensor_copy(sq_sum[:], sq[:, 0]).then_inc(n_acc, 1)
            else:
                dve.wait_ge(n_acc, 8 * i + m)
                dve.tensor_tensor(sq_sum[:], sq_sum[:], sq[:, m % 2], ALU.add).then_inc(n_acc, 1)

        def norm_inverse(i):
            dve.wait_ge(n_std, i + 1)
            dve.reciprocal(rb[:], std[:]).then_inc(n_rb, 1)
            dve.wait_ge(n_rb, i + 1)

        def chunks_then_add(i, chunk):
            for m in range(NC + 1):
                if m < NC:
                    chunk(m)
                if m >= 1:
                    norm_add(i, m - 1)

        def modulated(i, factor, shift):
            for m in range(NC + 1):
                if m < NC:
                    if m >= 2:
                        dve.wait_ge(h_lo_done, 8 * i + m - 1)
                    dve.scalar_tensor_tensor(tt[:, m % 2], xT[:, m], column(fac, factor + m), rb[:],
                                             ALU.mult, ALU.mult).then_inc(h_t, 1)
                if m >= 1:
                    k = m - 1
                    dve.wait_ge(h_hi_done, 8 * i + k + 1)
                    dve.wait_ge(h_t, 8 * i + k + 1)
                    dve.scalar_tensor_tensor(h_lo[:, k], tt[:, k % 2], column(mod, shift + k), h_hi[:, k].bitcast(F32),
                                             ALU.add, ALU.subtract).then_inc(h_lo_done, 1)

        def ada_step(s, i=0, per=0):
            b = s % 2
            c = 0 if s < ADA_1 else 1
            dve.wait_ge(ada_in[b], i * (8 * per) + 16 * (s // 2 + 1))
            if s >= 2:
                dve.wait_ge(ada_mm, i * per + (s - 1))
            step(dve.tensor_scalar(ada_sum[:, b], ada[:, b, 0], cT[:, c, 0:1], None, ALU.mult))
            for j in range(1, NC):
                ins = dve.scalar_tensor_tensor(ada_sum[:, b], ada[:, b, j], cT[:, c, j:j + 1], ada_sum[:, b],
                                               ALU.mult, ALU.add)
                if j < NC - 1:
                    step(ins)
            ins.then_inc(ada_summed, 1)

        def copy_x(m):
            dve.wait_ge(x_tr, m + 1)
            dve.tensor_copy(xT[:, m], ps[:, m % 4]).then_inc(x_ready, 1)

        chunks_then_add(0, copy_x)
        dve.wait_ge(vec_tr, 1)
        for lo, hi in ((0, 109), (128, 208), (256, 320)):
            ins = dve.tensor_copy(vec[:, lo:hi], ps[:, B_NORM2, lo:hi])
        step(ins)
        norm_inverse(0)
        dve.wait_ge(c_ready, 1)
        for s in range(ADA_START):
            ada_step(s)

        def read_mod(lo, hi, bias, steps_done):
            dve.wait_ge(ada_mm, steps_done)
            dve.tensor_tensor(mod[:, lo:hi], ps[:, B_ADA, lo:hi], vec[:, bias:bias + hi - lo], ALU.add).then_inc(mod_read, 1)
            reads[0] += 1
            dve.wait_ge(mod_read, reads[0])
        reads = [0]

        def gained(dst, scale_at, gain):
            step(dve.scalar_tensor_tensor(fac[:, dst:dst + 8], mod[:, scale_at:scale_at + 8], 1.0, vec[:, gain:gain + 8],
                                          ALU.add, ALU.mult))

        read_mod(0, 16, V_ADA1, ADA_START)
        gained(A_FFN1, 8, V_FFN1)
        modulated(0, A_FFN1, 0)

        def add_product(bank, m, factor):
            dve.scalar_tensor_tensor(xT[:, m], ps[:, bank], column(fac, factor + m), xT[:, m],
                                     ALU.mult, ALU.add).then_inc(x_ready, 1)

        def run_ffn(i):
            f = ffn[i]
            for half, (n0, it0, iters) in enumerate(ffn_tiles(i)[0]):
                s0 = (ADA_START, ADA_START + 16, 38, 50)[2 * i + half]
                start = count[0]
                per = 14 + 4
                with dve.Fori(0, iters) as it:
                    count[0] = it * per + start
                    for u in range(2):
                        ada_step(s0 + u, it, 2)
                    for m in range(2):
                        dve.wait_ge(f["silu"], it * 2 + (2 * it0 + m + 1 + START))
                        dve.wait_ge(f["gu"], it * 2 + (2 * it0 + 2)) if m == 0 else dve.wait_ge(tile_used, it * 2 + (n0 + 2))
                        k = 2 * it + m
                        dve.wait_ge(f["hid"], it * 2 + (2 * it0 + m + START))
                        step(dve.tensor_tensor(tt[:, m], sg[:, m], ps[:, 2 + m], ALU.mult))
                        step(dve.tensor_copy(g_hi[:, bass.ds(k, 1)], tt[:, m:m + 1]))
                        dve.tensor_tensor(g_lo[:, bass.ds(k, 1)], tt[:, m:m + 1], g_hi[:, bass.ds(k, 1)].bitcast(F32),
                                          ALU.subtract).then_inc(f["hid"], 1)
                count[0] = start + per * iters
                if i == 0 and half == 0:
                    read_mod(16, 40, V_ADA1 + 16, ADA_START + 12)
                    step(dve.tensor_scalar(fac[:, A_G1:A_G1 + 8], mod[:, 16:24], 0.5, None, ALU.mult))
                x0 = ((X_F1A, X_F1B), (X_F2A, X_F2B))[i][half]
                n1 = n0 + 2 * iters

                def down(m):
                    if i == 0 and m % 4 == 0:
                        for u in range(2):
                            ada_step(s0 + 2 * iters + m // 2 + u)
                    dve.wait_ge(tile_used, n1 + 2 * (m // 2) + 2)
                    add_product(m % 4, m, (A_G1, A_G3)[i])

                if half == 0:
                    for m in range(NC):
                        down(m)
                    dve.wait_ge(x_ready, x0 + 8)
                else:
                    chunks_then_add((1, 3)[i], down)

        run_ffn(0)
        read_mod(40, 72, V_ADA1 + 40, 38)
        gained(A_MIX, 32, V_MIX)
        gained(A_FFN2, 56, V_FFN2)
        step(dve.tensor_scalar(fac[:, A_G3:A_G3 + 8], mod[:, 64:72], 0.5, None, ALU.mult))
        norm_inverse(1)
        modulated(1, A_MIX, 24)

        for j in range(5):
            wait_product(dve, win_mm, j, 2, W_MIX)
            dve.tensor_copy(lat[:, j], ps[:, j % 4]).then_inc(win_free, 1)
        wait_product(dve, win_mm, 5, 2, W_MIX)
        dve.tensor_copy(kr_raw[:], ps[0:QK, 1]).then_inc(win_free, 1)
        for j in range(5):
            dve.wait_ge(l_sq, j + 1)
            s = sq_sum if j < 3 else sq_sum2
            if j in (0, 3):
                dve.wait_ge(n_sum, 2)
                dve.tensor_copy(s[:], sq[:, j % 2]).then_inc(l_acc, 1)
            else:
                dve.wait_ge(l_acc, j)
                dve.tensor_tensor(s[:], s[:], sq[:, j % 2], ALU.add).then_inc(l_acc, 1)
        for j in range(4):
            dve.wait_ge(win_hi, j + 1)
            dve.tensor_tensor(u_lo[:, j], ps[:, (6 + j) % 4], u_hi[:, j].bitcast(F32), ALU.subtract).then_inc(win_free, 1)
        for i, dst in enumerate((std, rb)):
            dve.wait_ge(l_std, i + 1)
            dve.reciprocal(dst[:], dst[:]).then_inc(l_rb, 1)
        dve.wait_ge(l_rb, 2)
        for j in range(6):
            if j < 5:
                if j >= 2:
                    dve.wait_ge(l_lo_done, j - 1)
                dve.scalar_tensor_tensor(tt[:, j % 2], lat[:, j], column(vec, V_QN + j), (std if j < 3 else rb)[:],
                                         ALU.mult, ALU.mult).then_inc(l_t, 1)
            if j >= 1:
                k = j - 1
                dve.wait_ge(l_hi_done, k + 1)
                dve.wait_ge(l_t, k + 1)
                dve.tensor_tensor(ln_lo[:, k], tt[:, k % 2], ln_hi[:, k].bitcast(F32), ALU.subtract).then_inc(l_lo_done, 1)
        for j in range(8):
            g = 10 + j
            dve.wait_ge(win_hi, 4 + j + 1)
            sp2, gr = j % 2, j // 2
            dve.tensor_tensor((a_lo_0, a_lo_1)[sp2][:, :, gr, :], ps[:, g % 4].rearrange("p (c m) -> p c m", c=2),
                              a_hi[:, 2 * sp2:2 * sp2 + 2, gr, :].bitcast(F32), ALU.subtract).then_inc(win_free, 1)
        for j in range(4):
            dve.wait_ge(win_hi, 12 + j + 1)
            dve.tensor_tensor(u_lo[:, j], ps[:, (18 + j) % 4], u_hi[:, j].bitcast(F32), ALU.subtract).then_inc(win_free, 1)
        for j in range(NC):
            wait_product(dve, win_mm, j, 4, W_FO, before=15)
            dve.tensor_copy(ya[:, j], ps[:, (22 + j) % 4]).then_inc(win_free, 1)

        def angles(b, pos, tab):
            freq = column(kst, K_FREQ + b)
            dve.wait_ge(pos_in, 16 * (b + 1))
            step(dve.tensor_copy(tt[:, 0], pos))
            step(dve.tensor_scalar(tt[:, 0], tt[:, 0], freq, None, ALU.mult))
            magic = 1.5 * 2.0 ** 23
            step(dve.tensor_scalar(tt[:, 1], tt[:, 0], float(1 / (2 * np.pi)), magic, ALU.mult, ALU.add))
            step(dve.tensor_scalar(tt[:, 1], tt[:, 1], -magic, None, ALU.add))
            c1 = 6.28125
            c2 = float(np.float32(np.round((2 * np.pi - c1) * 2 ** 21) / 2 ** 21))
            c3 = float(2 * np.pi - c1 - c2)
            for c in (c1, c2, c3):
                step(dve.scalar_tensor_tensor(tt[:, 0], tt[:, 1], -c, tt[:, 0], ALU.mult, ALU.add))
            dve.tensor_scalar(tt[:, 0], tt[:, 0], 1.0, None, ALU.mult).then_inc(ang, 1)
            dve.wait_ge(ang, 2 * b + 1)
            dve.scalar_tensor_tensor(tt[:, 1], tt[:, 0], -1.0, tt[:, 0], ALU.mult, ALU.max).then_inc(ang, 1)
            dve.wait_ge(sin_done, 2 * b + 2)
            step(dve.scalar_tensor_tensor(tt[:, 0], tab[:, 0], 2.0, tab[:, 1], ALU.mult, ALU.mult))
            step(dve.scalar_tensor_tensor(tt[:, 1], tab[:, 0], -2.0, tab[:, 0], ALU.mult, ALU.mult))
            step(dve.tensor_scalar(tab[:, 0], tt[:, 1], 1.0, None, ALU.add))
            step(dve.tensor_copy(tab[:, 1], tt[:, 0]))

        angles(0, pos1[:], tab1)

        def rotate(r, rows, src, tab, dst):
            dve.wait_ge(rp_raw, r + 1)
            dve.wait_ge(rp_out, r)
            step(dve.tensor_tensor(tt[0:rows, 0], src[0:rows, r % 2], tab[0:rows, 0], ALU.mult))
            dve.wait_ge(rp_rot, r + 1)
            step(dve.tensor_tensor(tt[0:rows, 1], ps[0:rows, 2 + r % 2], tab[0:rows, 1], ALU.mult))
            dve.tensor_tensor(dst, tt[0:rows, 0], tt[0:rows, 1], ALU.add).then_inc(rp_out, 1)

        rotate(0, QK, rp_raw1, tab1, kr_raw[:])
        dve.wait_ge(rp_out, 1)
        for h in range(MLA_HEADS):
            dve.tensor_copy(k_all[NOPE:QK, h], kr_raw[NOPE:QK]).then_inc(kr_copied, 1)
        for h in range(MLA_HEADS):
            rotate(1 + h, QK, rp_raw1, tab1, q_all[:, h])

        ROUNDS = TOPK // 8

        def select_round(i):
            qc, r = 1 + i // ROUNDS, i % ROUNDS
            s = score[:, SCORE_AT[qc]:SCORE_AT[qc] + P * (qc + 1)]
            step(dve.max(c8[:, 3, :], s))
            step(dve.match_replace(out=s, in_to_replace=c8[:, 3, :], in_values=s, imm_value=TAKEN))
            if r == ROUNDS - 1:
                step(dve.tensor_scalar(s, s, TAKEN / 2, NEG, ALU.is_gt, ALU.mult))

        def attention(att, oh, ol, selects=0):
            units, t0, u0, pt, p, small = (att[k] for k in ("units", "t0", "u0", "pt", "p", "small"))
            steps = 4 * len(units)

            def maxima(t):
                x, qc = units[t // 4], t % 4
                w = x["width"](qc)
                dve.wait_ge(at_s, t0 + t + 1)
                s = ps[:, B_S[t % 3], 0:w]
                mx = small[:, t % 8:t % 8 + 1]
                if x["mask"] is None:
                    step(dve.tensor_reduce(mx, s, AX, ALU.max))
                else:
                    if t >= 3:
                        dve.wait_ge(at_tr, t0 + t - 2)
                    step(dve.tensor_tensor_reduce(out=p[:, t % 3, 0:w], in0=s, in1=x["mask"](qc), scale=1.0, scalar=-3e38,
                                                  op0=ALU.add, op1=ALU.max, accum_out=mx))
                dve.tensor_scalar(small[:, 8 + t % 8:9 + t % 8], mx, -x["scale"], None, ALU.mult).then_inc(at_nm, 1)

            def normalised(t):
                x, qc = units[t // 4], t % 4
                w = x["width"](qc)
                dve.wait_ge(at_exp, t0 + t + 1)
                rs = small[:, 24 + t % 8:25 + t % 8]
                step(dve.reciprocal(rs, small[:, 16 + t % 8:17 + t % 8]))
                pr = p[:, t % 3, 0:w]
                if x["gate"] is None:
                    dve.tensor_scalar(pr, pr, rs, None, ALU.mult).then_inc(at_p, 1)
                else:
                    dve.tensor_scalar(pr, pr, rs, x["gate"](qc), ALU.mult, ALU.mult).then_inc(at_p, 1)

            def out_low(u):
                x = units[u]
                if x["last"] and x["h"] % 2:
                    pair = pairs_done(units, u) - 1
                    dve.wait_ge(o_hi_done, att["c0"] + pair + 1)
                    dve.tensor_tensor(ol[:, pair], ps[:, B_O[pair % 2]], oh[:, pair].bitcast(F32),
                                      ALU.subtract).then_inc(o_lo_done, 1)

            done = 0
            for t in range(steps + 5):
                if t < steps:
                    maxima(t)
                if 1 <= t < steps + 1:
                    normalised(t - 1)
                if t >= 8 and (t - 4) % 4 == 0:
                    out_low((t - 8) // 4)
                if done < selects:
                    select_round(done)
                    done += 1

        dve.wait_ge(rp_out, 9)
        dve.wait_ge(l_hi_done, 5)
        attention(ATT[0], o_hi, o_lo)

        for m in range(NC):
            dve.wait_ge(gate_done, m + 1)
            step(dve.tensor_tensor(ya[:, m], ya[:, m], gate[:, m], ALU.mult))
        for m in range(NC + 1):
            if m < NC:
                wait_product(dve, yb_mm, m, 4, W_MLA)
                dve.wait_ge(gate_done, 16)
                dve.tensor_tensor(gate[:, m], ps[:, m % 4], gate[:, 8 + m], ALU.mult).then_inc(yb_read, 1)
                dve.wait_ge(yb_read, m + 1)
                if m >= 2:
                    dve.wait_ge(yb_lo, m - 1)
                dve.tensor_tensor(tt[:, m % 2], gate[:, m], ya[:, m], ALU.add).then_inc(yb_sum, 1)
            if m >= 1:
                k = m - 1
                dve.wait_ge(yb_hi, k + 1)
                dve.wait_ge(yb_sum, k + 1)
                dve.tensor_tensor(h_lo[:, k], tt[:, k % 2], h_hi[:, k].bitcast(F32), ALU.subtract).then_inc(yb_lo, 1)

        def mix_out(m):
            wait_product(dve, wo_mm, m, 2, W_OUT)
            dve.scalar_tensor_tensor(xT[:, m], ps[:, m % 4], column(mod, 40 + m), xT[:, m],
                                     ALU.mult, ALU.add).then_inc(x_ready, 1)

        chunks_then_add(2, mix_out)
        norm_inverse(2)
        modulated(2, A_FFN2, 48)
        run_ffn(1)
        read_mod(72, 120, V_ADA2, ADA_STEPS)
        gained(A_PREMIX, 72 + 8, V_PREMIX)
        gained(A_PREFFN, 72 + 32, V_PREFFN)
        for dst, g, v in ((A_POSTMIX, 72 + 16, V_POSTMIX), (A_POSTFFN, 72 + 40, V_POSTFFN)):
            step(dve.tensor_tensor(fac[:, dst:dst + 8], mod[:, g:g + 8], vec[:, v:v + 8], ALU.mult))
        norm_inverse(3)

        def final_norm(m):
            dve.scalar_tensor_tensor(xT[:, m], xT[:, m], column(vec, V_FINAL + m), rb[:],
                                     ALU.mult, ALU.mult).then_inc(x_ready, 1)

        chunks_then_add(4, final_norm)
        norm_inverse(4)
        modulated(3, A_PREMIX, 72)

        dve.wait_ge(h_lo_done, 32)
        angles(1, pos2[:], tab2)
        for t in (kc, vc):
            step(dve.memset(t[:, T:T + CMP_STRIDE], 0.0))
        step(dve.memset(hid_k[:], 0.0))
        step(dve.memset(hid_v[:], 0.0))

        def rotate2(i, dst):
            rotate(9 + i, P, rp_raw2, tab2, dst)

        rotate2(0, qi[:, 0])
        rotate2(1, qi[:, 1])
        rotate2(2, kd[:])
        rotate2(3, ki[:])
        for c in range(NQ):
            dve.wait_ge(nat_sig, c + 1)
            b = 6 + c % 2
            step(dve.tensor_copy(v2[:, c, 0:256], ps[:, b, 0:256]))
            step(dve.tensor_copy(v2[:, c, 256:320], ps[:, b, 280:344]))
            dve.tensor_scalar(wsc[:, c, :], ps[:, b, 344:348], IDX_HEADS ** -0.5 * 64 ** -0.5, None, ALU.mult).then_inc(nat_ev, 1)
        dve.wait_ge(nat_ev, NQ)
        for j in range(12):
            qc, h = 1 + j // 4, j % 4
            w = P * (qc + 1)
            s = score[:, SCORE_AT[qc]:SCORE_AT[qc] + w]
            dve.wait_ge(ix_relu, j + 1)
            if h == 0:
                dve.tensor_scalar(s, relu[:, j % 2, 0:w], wsc[:, qc, 0:1], None, ALU.mult).then_inc(ix_acc, 1)
            else:
                dve.wait_ge(ix_acc, j)
                dve.scalar_tensor_tensor(s, relu[:, j % 2, 0:w], wsc[:, qc, h:h + 1], s, ALU.mult, ALU.add).then_inc(ix_acc, 1)
            if h == 3:
                dve.wait_ge(ix_acc, j + 1)
                step(dve.tensor_tensor(s, s, causal_mask(qc), ALU.add))
        for i in range(4):
            rotate2(4 + i, qn[:, i])
        rotate2(8, kc[:, 0:T])
        for i, (t, c) in enumerate(((ks, 0), (ks, 1), (kw, 0), (kw, 1))):
            rotate2(9 + i, t[:, c])

        def blocks(j):
            src = (kc, vc)[j]
            if j:
                dve.wait_ge(vc_ev, 1)
            dve.wait_ge(rp_out, 9 + 9)
            v = src[:].rearrange("p (a b) -> p b a", b=CMP_STRIDE)
            for c in range(2):
                pe_col = vec[:, V_PE + 32 * j + 16 * c:V_PE + 32 * j + 16 * c + 16].unsqueeze(2).broadcast_to([P, 16, 32])
                dve.tensor_tensor(tt[:, c].rearrange("p (l n) -> p l n", n=32), v[:, :, c:c + 32], pe_col,
                                  ALU.add).then_inc(blk_t, 1)

        def blocks_low(j):
            dve.wait_ge(blk_t, 2 * j + 2)
            dve.wait_ge(blk_hi_done, j + 1)
            dve.tensor_tensor(blk_lo[:, j].rearrange("p l n -> p (l n)"), tt[:].rearrange("p a b -> p (a b)"),
                              blk_hi[:, j].rearrange("p l n -> p (l n)").bitcast(F32), ALU.subtract).then_inc(blk_lo_done, 1)
            dve.wait_ge(blk_lo_done, j + 1)

        dve.wait_ge(rp_out, 9 + 13)
        blocks(0)
        blocks_low(0)
        rotate2(13, qd[:, 0])
        rotate2(14, qd[:, 1])
        dve.wait_ge(rp_out, 9 + 15)
        blocks(1)
        blocks_low(1)
        rotate2(15, qd[:, 2])
        rotate2(16, qd[:, 3])

        dve.wait_ge(cm_kv, 1)
        step(dve.tensor_copy(kcmp[:], ps[:, 6, 0:64]))
        dve.tensor_copy(vcmp[:].rearrange("p g d -> p (g d)"), ps[:, 6, 64:192]).then_inc(cm_kv_ev, 1)

        def per_head(col, qc):
            return c8[:, col, :].unsqueeze(2).broadcast_to([P, 8, 32])

        def mask8(first, qc):
            return kst[:, first + 32 * qc:first + 32 * qc + 32].unsqueeze(1).broadcast_to([P, 8, 32])

        def heads(t):
            return t.rearrange("p (h n) -> p h n", n=32)

        def cmp_scores(qc):
            s = heads(cs[:, qc % 2])
            dve.wait_ge(cm_s, qc + 1)
            if qc >= 2:
                dve.wait_ge(cm_tr, qc - 1)
            for odd in range(2):
                mask = kst[:, K_CADD + 32 * qc:K_CADD + 32 * qc + 32].unsqueeze(1).broadcast_to([P, 4, 32])
                ins = dve.tensor_tensor(s[:, odd:8:2], heads(ps[:, 5 - qc % 2 + 2 * odd, 0:128]), mask, ALU.add)
            step(ins)
            step(dve.tensor_reduce(c8[:, 0, :], s, AX, ALU.max))
            dve.tensor_tensor(s, s, per_head(0, qc), ALU.subtract).then_inc(cm_sub, 1)

        def cmp_probs(qc):
            s = heads(cs[:, qc % 2])
            dve.wait_ge(cm_exp, qc + 1)
            step(dve.tensor_reduce(c8[:, 1, :], s, AX, ALU.add))
            step(dve.reciprocal(c8[:, 1, :], c8[:, 1, :]))
            g = gsig[:, qc, :].rearrange("p (h b) -> p h b", b=3)[:, :, 0]
            step(dve.tensor_tensor(c8[:, 2, :], c8[:, 1, :], g, ALU.mult))
            step(dve.tensor_tensor(s, s, mask8(K_CMUL, qc), ALU.mult))
            dve.tensor_tensor(s, s, per_head(2, qc), ALU.mult).then_inc(cm_p, 1)

        for qc in range(NQ + 1):
            if qc < NQ:
                cmp_scores(qc)
            if qc >= 1:
                cmp_probs(qc - 1)
        dve.wait_ge(rp_out, 9 + 17)
        attention(ATT[1], h_hi, h_lo, selects=3 * ROUNDS)

        def out2(m):
            wait_product(dve, wo2_mm, m, 2, W_OUT2)
            dve.tensor_copy(y2[:, m], ps[:, m % 4]).then_inc(y_ready, 1)

        def add_normed(factor, first):
            def chunk(m):
                if m:
                    dve.wait_ge(x_ready, first + m)
                step(dve.scalar_tensor_tensor(tt[:, m % 2], y2[:, m], column(fac, factor + m), rb[:], ALU.mult, ALU.mult))
                dve.tensor_tensor(xT[:, m], xT[:, m], tt[:, m % 2], ALU.add).then_inc(x_ready, 1)
            return chunk

        chunks_then_add(5, out2)
        norm_inverse(5)
        dve.wait_ge(y_ready, 8)
        chunks_then_add(6, add_normed(A_POSTMIX, X_ATT))
        norm_inverse(6)
        modulated(4, A_PREFFN, 72 + 24)
        for half in range(2):
            n0 = W_FFN3 + 16 * half
            start = count[0]
            with dve.Fori(0, 4) as it:
                count[0] = it * 4 + start
                for j in range(4):
                    k = 4 * it + j
                    dve.wait_ge(f3["relu"], it * 4 + (16 * half + j + 1 + START))
                    dve.wait_ge(f3["hid"], it * 4 + (16 * half + j + START))
                    dve.tensor_tensor(tt[:, j % 2], sg3[:, j], sg3[:, j], ALU.mult).then_inc(f3["sq"], 1)
                    dve.wait_ge(f3["sq"], it * 4 + (16 * half + j + 1 + START))
                    step(dve.tensor_copy(g_hi[:, bass.ds(k, 1)], tt[:, j % 2:j % 2 + 1]))
                    dve.tensor_tensor(g_lo[:, bass.ds(k, 1)], tt[:, j % 2:j % 2 + 1], g_hi[:, bass.ds(k, 1)].bitcast(F32),
                                      ALU.subtract).then_inc(f3["hid"], 1)
            count[0] = start + 16
            n1 = n0 + 8

            def down(m):
                dve.wait_ge(tile_used, n1 + 2 * (m // 2) + 2)
                if half == 0:
                    dve.tensor_copy(y2[:, m], ps[:, m % 4]).then_inc(y_ready, 1)
                else:
                    dve.tensor_tensor(y2[:, m], y2[:, m], ps[:, m % 4], ALU.add).then_inc(y_ready, 1)

            if half == 0:
                for m in range(NC):
                    down(m)
                dve.wait_ge(y_ready, 16)
            else:
                chunks_then_add(7, down)
        norm_inverse(7)
        dve.wait_ge(y_ready, 24)

        def turned(m):
            dve.wait_ge(out_tr, m + 1)
            dve.tensor_copy(o_nat[:, :, P * m:P * m + P],
                            ps[:, m % 4].rearrange("p (c d) -> p c d", c=NQ)).then_inc(out_ev, 1)

        for m in range(NC):
            add_normed(A_POSTFFN, X_END)(m)
            if m >= 1:
                turned(m - 1)
        turned(NC - 1)
    ctx.close()


def make(nc, arrays):
    handles = {name: nc.dram_tensor(f"in_{name}", list(v.shape), mybir.dt.from_np(v.dtype), kind="ExternalInput").ap()
               for name, v in arrays.items()}
    out = nc.dram_tensor("out_x", [1, T, D], F32, kind="ExternalOutput").ap()
    build(nc, handles, out)


def kernel(**inputs):
    import concourse.bacc as bacc
    from concourse.bass_utils import run_bass_kernel_spmd

    arrays = {name: np.ascontiguousarray(v) for name, v in inputs.items()}
    arrays["kst"], arrays["dft_d"], arrays["dft_s"] = constants()
    nc = bacc.Bacc("TRN2", target_bir_lowering=False, num_devices=1)
    make(nc, arrays)
    r = run_bass_kernel_spmd(nc, [{f"in_{name}": v for name, v in arrays.items()}], core_ids=[0])
    return r.results[0]["out_x"]
```

```python
from contextlib import ExitStack

import numpy as np

import concourse.bass as bass
from concourse import mybir

F32 = mybir.dt.float32
F32R = mybir.dt.float32r
I32 = mybir.dt.int32
ALU = mybir.AluOpType
ACT = mybir.ActivationFunctionType
AX = mybir.AxisListType.X

P = 128
D = 1024
T = 512
NC = D // P
NQ = T // P
D_FF = 2816
D_FF_2 = 4096
FOURIER, Q_RANK, KV_RANK, ROPE_1 = 512, 384, 256, 32
MLA_HEADS, NOPE, V_DIM = 8, 64, 64
QK = NOPE + ROPE_1
NSA_HEADS, NSA_KV, HD = 8, 2, 64
IDX_HEADS = 4
CMP_LEN, CMP_STRIDE = 32, 16
N_CMP = (T - CMP_LEN) // CMP_STRIDE + 1
TOPK = min(256, T // 4)
NEG = -1e30
TAKEN = -3e38
EPS = 1e-6
START = 3
SLOT = 2048
N_VEC = 16

IN_Q = FOURIER
IN_KV = IN_Q + Q_RANK
IN_KR = IN_KV + KV_RANK
IN_GATE = IN_KR + ROPE_1
I2 = dict(qn=0, kc=512, vc=640, ks=768, vs=896, kw=1024, vw=1152, gl=1280, qd=1304, kd=1816, vd=1880,
          qi=1944, ki=2200, wi=2264)

ITERS = (6, 5)
FFN_TILES = 2 * sum(ITERS) + 16
W_FFN1 = 0
W_MIX = W_FFN1 + FFN_TILES
W_DFT_D = W_MIX + 5
W_DFT_S = W_DFT_D + 1
W_FO = W_DFT_S + 2
W_QUP = W_FO + 2
W_KVUP = W_QUP + 2
W_GATE = W_KVUP + 1
W_MLA = W_GATE + 8
W_OUT = W_MLA + 2
W_FFN2 = W_OUT + 4
W_IN2 = W_FFN2 + FFN_TILES
W_CMP = W_IN2 + 10
W_OUT2 = W_CMP + 4
W_FFN3 = W_OUT2 + 4
N_TILES = W_FFN3 + 32

ADA_1 = 9 * D // 256
ADA_STEPS = ADA_1 + 6 * D // 256
ADA_STEPS_1 = 38
START_STEPS = (0, 4, 1, 5, 2, 6, 3, 7)
ADA_START = len(START_STEPS)
ROWS = ADA_START // 2

K_ID, K_R64, K_R96, K_CAUSAL, K_CADD, K_CMUL, K_FREQ = 0, 128, 256, 352, 864, 992, 1120
K_COLS = 1122

V_FFN1, V_MIX, V_FFN2, V_FINAL, V_QN, V_KVN, V_ADA1 = 0, 8, 16, 24, 32, 35, 37
V_ADA2, V_PREMIX, V_POSTMIX, V_PREFFN, V_POSTFFN = 128, 176, 184, 192, 200
V_PE = 256
A_FFN1, A_MIX, A_FFN2, A_PREMIX, A_POSTMIX, A_PREFFN, A_POSTFFN, A_G1, A_G3 = range(0, 72, 8)

X_INIT, X_F1A, X_F1B, X_MIX, X_F2A, X_F2B, X_FINAL, X_ATT, X_END = range(0, 72, 8)


def constants():
    k = np.zeros((P, K_COLS), np.float32)
    k[:, K_ID:K_ID + P] = np.eye(P)
    for d0 in range(0, P, 64):
        for m in range(32):
            k[d0 + m + 32, K_R64 + d0 + m] = -1
            k[d0 + m, K_R64 + d0 + m + 32] = 1
    for m in range(16):
        k[NOPE + m + 16, K_R96 + NOPE + m] = -1
        k[NOPE + m, K_R96 + NOPE + m + 16] = 1
    p = np.arange(P)[:, None]
    k[:, K_CAUSAL:K_CAUSAL + T] = np.where(np.arange(T)[None, :] <= p + T - P, 0, NEG)
    for qc in range(NQ):
        n = np.arange(32)[None, :]
        seen = (n * CMP_STRIDE + CMP_LEN - 1 <= qc * P + p) & (n < N_CMP)
        k[:, K_CADD + 32 * qc:K_CADD + 32 * qc + 32] = np.where(seen, 0, NEG)
        k[:, K_CMUL + 32 * qc:K_CMUL + 32 * qc + 32] = seen
    f1 = np.float32(1) / np.power(np.float32(10000), np.arange(16, dtype=np.float32) * np.float32(2) / np.float32(32))
    k[NOPE:QK, K_FREQ] = np.tile(f1.astype(np.float32), 2)
    f2 = (10000.0 ** (-np.arange(32) / 32)).astype(np.float32)
    k[:, K_FREQ + 1] = np.tile(f2, 4)
    d = 2 * np.pi * np.outer(np.arange(P), np.arange(P)) / P
    dft_d = np.concatenate([np.cos(d), np.sin(d)], 1).astype(np.float32)
    s = 2 * np.pi * (np.outer(np.arange(T), np.arange(T)) % T) / T
    norm = (T * P) ** -0.5
    dft_s = np.stack([np.cos(s) * norm, -np.sin(s) * norm]).astype(np.float32)
    return k, dft_d, dft_s


def build(nc, a, out):
    ctx = ExitStack()
    base = -(-nc.sbuf_base // 64) * 64
    used = [base]

    def place(name, shape, dt=F32, at=None):
        n = 4 * int(np.prod(shape[1:]))
        if at is None:
            at = used[0]
            used[0] += -(-n // 32) * 32
        return nc.alloc_sbuf_tensor_at(name, shape, dt, offset=at)

    def sem(name):
        return ctx.enter_context(nc.semaphore(name))

    raw = place("raw", [P, 2, SLOT])
    w_hi = place("w_hi", [P, 2, SLOT], F32R)
    w_lo = place("w_lo", [P, 2, SLOT], F32R)
    xT = place("xT", [P, NC, T])
    h_hi = place("h_hi", [P, NC, T], F32R)
    h_lo = place("h_lo", [P, NC, T], F32R)
    kst = place("kst", [P, K_COLS])
    ones = place("ones", [P, P])
    vec = place("vec", [P, 320])
    mod = place("mod", [P, 120])
    fac = place("fac", [P, 72])
    cT = place("cT", [P, 2, NC])
    eps = place("eps", [P, 2])
    free = place("free", [P, 8])
    rb = place("rb", [P, T])
    sq_sum = place("sq_sum", [P, T])
    std = place("std", [P, T])
    tt = place("tt", [P, 2, T])
    sq = place("sq", [P, 2, T])
    arena = used[0]
    end = nc.sbuf_usable_end
    KB = 1024

    def at(kb):
        assert arena + kb * KB <= end, kb
        return int(arena + kb * KB)

    x_nat = place("x_nat", [P, NQ, D], at=at(0))
    vnat = place("vnat", [P, 3, P], at=at(16))
    pe_nat = place("pe_nat", [32, 2, P], at=at(18))
    g_hi = place("g_hi", [P, 16, T], F32R, at=at(0))
    g_lo = place("g_lo", [P, 16, T], F32R, at=at(32))
    sg = place("sg", [P, 2, T], at=at(64))
    ada = place("ada", [P, 2, NC, 256], at=at(68))
    ada_sum = place("ada_sum", [P, 2, 256], at=at(84))
    ada_more = place("ada_more", [P, 5, NC, 256], at=at(24))
    ya = place("ya", [P, NC, T], at=at(0))
    ln_hi = place("ln_hi", [P, 5, T], F32R, at=at(16))
    ln_lo = place("ln_lo", [P, 5, T], F32R, at=at(26))
    lat = place("lat", [P, 5, T], at=at(36))
    kr_raw = place("kr_raw", [QK, T], at=at(86))
    sq_sum2 = place("sq_sum2", [P, T], at=at(88))
    u_hi = place("u_hi", [P, 4, T], F32R, at=at(46))
    u_lo = place("u_lo", [P, 4, T], F32R, at=at(54))
    a_hi = place("a_hi", [P, NQ, 4, 256], F32R, at=at(62))
    a_lo_0 = place("a_lo_0", [P, 2, 4, 256], F32R, at=at(78))
    a_lo_1 = place("a_lo_1", [P, 2, 4, 256], F32R, at=at(0))
    k_all = place("k_all", [QK, MLA_HEADS, T], at=at(46))
    q_all = place("q_all", [QK, MLA_HEADS, T], at=at(62))
    v_all = place("v_all", [P, NQ, T], at=at(78))
    tab1 = place("tab1", [P, 2, T], at=at(36))
    rp_raw1 = place("rp_raw1", [P, 2, T], at=at(40))
    o_nat1 = place("o_nat1", [P, NQ, MLA_HEADS * V_DIM], at=at(16))
    p1 = place("p1", [P, 3, T], at=at(24))
    o_hi = place("o_hi", [P, 4, T], F32R, at=at(30))
    o_lo = place("o_lo", [P, 4, T], F32R, at=at(38))
    gate = place("gate", [P, 16, T], at=at(46))
    qn = place("qn", [P, 4, T], at=at(0))
    ks = place("ks", [P, T], at=at(8))
    kw = place("kw", [P, T], at=at(12))
    qd = place("qd", [P, 4, T], at=at(16))
    kd = place("kd", [P, T], at=at(24))
    v2 = place("v2", [P, NQ, 320], at=at(26))
    score = place("score", [P, 1152], at=at(31))
    ptc = place("ptc", [P, NSA_KV, T], at=at(36))
    p2 = place("p2", [P, 3, T], at=at(40))
    o_nat2 = place("o_nat2", [P, NQ, D], at=at(46))
    v_diag = place("v_diag", [P, NSA_KV, 4, HD], at=at(86.5))
    blk_hi = place("blk_hi", [P, CMP_LEN, NSA_KV, 32], F32R, at=at(46))
    blk_lo = place("blk_lo", [P, CMP_LEN, NSA_KV, 32], F32R, at=at(54))
    gsig = place("gsig", [P, NQ, 24], at=at(62))
    wsc = place("wsc", [P, NQ, 4], at=at(62.5))
    kcmp = place("kcmp", [P, 64], at=at(62.75))
    w2sb = place("w2sb", [P, 3, 64], at=at(63.5))
    hid_k = place("hid_k", [P, 2, 32], at=at(64.25))
    hid_v = place("hid_v", [P, 2, 4, 32], at=at(64.5))
    cs = place("cs", [P, 2, 256], at=at(65.5))
    hid_nat = place("hid_nat", [HD, 2, P], at=at(65.5))
    c8 = place("c8", [P, 4, 8], at=at(67.5))
    tab2 = place("tab2", [P, 2, T], at=at(68))
    rp_raw2 = place("rp_raw2", [P, 2, T], at=at(72))
    kc = place("kc", [P, T + CMP_STRIDE], at=at(76))
    vc = place("vc", [P, T + CMP_STRIDE], at=at(78.25))
    qi = place("qi", [P, 2, T], at=at(80.5))
    ki = place("ki", [P, T], at=at(84.5))
    relu = place("relu", [P, 2, T], at=at(86.5))
    small2 = place("small2", [P, 64], at=at(90.5))
    y2 = place("y2", [P, NC, T], at=at(64))
    small1 = place("small1", [P, 64], at=at(90))
    sg3 = place("sg3", [P, 4, T], at=at(80))
    o_nat = place("o_nat", [P, NQ, D], at=at(0))
    pos1 = place("pos1", [P, T], I32, at=at(44))
    pos2 = place("pos2", [P, T], I32, at=at(86.5))

    ps = ctx.enter_context(nc.psum_tensor("ps", [P, 8, 512], F32))
    B_ADA, B_NORM, B_NORM2 = 4, 5, 6

    id_in, row_summed, row_ready = sem("id_in"), sem("row_summed"), sem("row_ready")
    c_in = sem("c_in")
    start_in = [sem(f"start_in{q}") for q in range(ADA_START)]
    raw_in = [sem("raw_in0"), sem("raw_in1")]
    hi_done = sem("hi_done")
    split_done = sem("split_done")
    tile_used = sem("tile_used")
    x_in = [sem(f"x_in{j}") for j in range(4)]
    kst_in, vec_in, pos_in, w2_in = sem("kst_in"), sem("vec_in"), sem("pos_in"), sem("w2_in")
    set_up = sem("set_up")
    x_tr, vec_tr, vec_ready, c_ready = sem("x_tr"), sem("vec_tr"), sem("vec_ready"), sem("c_ready")
    ada_in = [sem("ada_in0"), sem("ada_in1")]
    ada_summed, ada_mm, mod_read = sem("ada_summed"), sem("ada_mm"), sem("mod_read")
    dve_step = sem("dve_step")
    x_ready, y_ready = sem("x_ready"), sem("y_ready")
    n_sq, n_acc, n_sum, n_std, n_rb = (sem(f"norm_{s}") for s in ("sq", "acc", "sum", "std", "rb"))
    l_sq, l_acc, l_sum, l_std, l_rb = (sem(f"lat_{s}") for s in ("sq", "acc", "sum", "std", "rb"))
    h_t, h_hi_done, h_lo_done = sem("h_t"), sem("h_hi_done"), sem("h_lo_done")
    l_t, l_hi_done, l_lo_done = sem("l_t"), sem("l_hi_done"), sem("l_lo_done")
    ffn = [{s: sem(f"ffn{i}_{s}") for s in ("silu", "hid")} for i in (1, 2)]
    f3 = {s: sem(f"ffn3_{s}") for s in ("relu", "sq", "hid")}
    win_mm, win_hi, win_free = sem("win_mm"), sem("win_hi"), sem("win_free")
    ang, sin_done = sem("ang"), sem("sin_done")
    rp_mm, rp_raw, rp_rot, rp_out = sem("rp_mm"), sem("rp_raw"), sem("rp_rot"), sem("rp_out")
    kv_mm, kv_ev, kr_copied = sem("kv_mm"), sem("kv_ev"), sem("kr_copied")
    at_s, at_nm, at_exp, at_tr, at_ev, at_pv, at_o, at_sum, at_pt = (sem(f"at_{s}") for s in ("s", "nm", "exp", "tr", "ev", "pv", "o", "sum", "pt"))
    o_hi_done, o_lo_done = sem("o_hi_done"), sem("o_lo_done")
    gate_mm, gate_done, yb_mm, yb_read, yb_sum, yb_hi, yb_lo = (
        sem(s) for s in ("gate_mm", "gate_done", "yb_mm", "yb_read", "yb_sum", "yb_hi", "yb_lo"))
    wo_mm = sem("wo_mm")
    nat_mm, nat_sig, nat_ev = sem("nat_mm"), sem("nat_sig"), sem("nat_ev")
    ix_mm, ix_relu, ix_acc = sem("ix_mm"), sem("ix_relu"), sem("ix_acc")
    vc_ev, blk_t, blk_hi_done, blk_lo_done = sem("vc_ev"), sem("blk_t"), sem("blk_hi_done"), sem("blk_lo_done")
    cm_o, cm_o_ev = sem("cmp_o"), sem("cmp_o_ev")
    cm_hid, cm_hid_ev, blk_clear = sem("cm_hid"), sem("cm_hid_ev"), sem("blk_clear")
    cm_gelu, cm_kv, cm_kv_ev = sem("cm_gelu"), sem("cm_kv"), sem("cm_kv_ev")
    cm_s, cm_sub, cm_exp, cm_p, cm_tr, cm_ev = (sem(f"cmp_{s}") for s in ("s", "sub", "exp", "p", "tr", "ev"))
    out_tr, out_ev, out_done = sem("out_tr"), sem("out_ev"), sem("out_done")
    wo2_mm = sem("wo2_mm")

    ident = kst[:, K_ID:K_ID + P]
    DIRECT = (4, 6)

    def added(i, m):
        return 8 * i + m + 1 - sum(d < i for d in DIRECT)

    def last_added(i):
        return added(i, 6 if i in DIRECT else 7)

    block = ctx.enter_context(nc.Block())

    def start_ada(q):
        return ada_more[:, q - 2] if 2 <= q < 7 else ada[:, q % 2]

    def w2d(w):
        return w.rearrange("o (k p) m -> p (o k) m", p=P)

    def tile_plan():
        t = {}
        w_in, w_in2 = w2d(a["w_in"]), w2d(a["w_in_2"])

        def whole(src):
            return [(src, 0, src.shape[2], 0)], src.shape[1], src.shape[2]

        for j, (c0, n) in enumerate(((IN_Q, 256), (IN_Q + 256, 256), (IN_KV + P, P + ROPE_1), (0, 256), (256, 256))):
            t[W_MIX + j] = whole(w_in[:, :, c0:c0 + n])
        t[W_DFT_D] = whole(a["dft_d"].rearrange("(k p) m -> p k m", p=P))
        for j in range(2):
            t[W_DFT_S + j] = whole(a["dft_s"][j].rearrange("(k p) m -> p k m", p=P))
            t[W_FO + j] = whole(w2d(a["w_fourier_out"])[:, :, 512 * j:512 * j + 512])
            t[W_QUP + j] = whole(w2d(a["w_q_up"])[:, :, 4 * QK * j:4 * QK * j + 4 * QK])
            t[W_MLA + j] = whole(w2d(a["w_mla_out"])[:, :, 512 * j:512 * j + 512])
        t[W_KVUP] = whole(w2d(a["w_kv_up"]))
        for j in range(8):
            t[W_GATE + j] = whole(w_in[:, :, IN_GATE + 256 * j:IN_GATE + 256 * j + 256])
        for j in range(4):
            t[W_OUT + j] = whole(w2d(a["w_out"])[:, :, 256 * j:256 * j + 256])
            t[W_OUT2 + j] = whole(w2d(a["w_out_2"])[:, :, 256 * j:256 * j + 256])

        def parts(*names):
            loads, c = [], 0
            for name, n in names:
                first = I2[name] if isinstance(name, str) else I2[name[0]] + name[1]
                loads.append((w_in2[:, :, first:first + n], c, n, 0))
                c += n
            return loads, NC, c

        t[W_IN2] = parts(("qi", 256))
        t[W_IN2 + 1] = parts(("kd", HD), ("kd", HD), ("ki", HD), ("ki", HD))
        t[W_IN2 + 2] = parts(("vs", 128), ("vw", 128))
        t[W_IN2 + 3] = parts(("gl", 24), ("vd", 64), ("wi", 4))
        for j in range(2):
            t[W_IN2 + 4 + j] = parts(*((("qn", HD * h), HD) for h in (2 * j, 2 * j + 4, 2 * j + 1, 2 * j + 5)))
        t[W_IN2 + 6] = whole(w_in2[:, :, I2["kc"]:I2["kc"] + 256])
        t[W_IN2 + 7] = parts(("ks", P), ("kw", P))
        t[W_IN2 + 8] = whole(w_in2[:, :, I2["qd"]:I2["qd"] + 256])
        t[W_IN2 + 9] = whole(w_in2[:, :, I2["qd"] + 256:I2["qd"] + 512])
        for j, name in enumerate(("cmp_w1_k_2", "cmp_w1_v_2")):
            src = a[name].rearrange("o (l d) j -> d (o l) j", d=HD)
            for u in range(2):
                part = src[:, 16 * u:16 * u + 16, :]
                t[W_CMP + 2 * j + u] = [(part, 0, P, 0), (part, 0, P, HD)], 16, P
        return t

    plan = tile_plan()
    loads_before = [0, 0]
    arrived = {}
    for n in range(N_TILES):
        loads_before[n % 2] += len(plan[n][0]) if n in plan else 1
        arrived[n] = 16 * loads_before[n % 2]

    def slot(t, n, kc, cols):
        return t[:, n % 2, 0:kc * cols].rearrange("p (k c) -> p k c", c=cols)

    def ffn_tiles(i):
        w = (W_FFN1, W_FFN2)[i]
        gate_w, up_w, down_w = (w2d(a[f"ffn{i + 1}_w_{s}"]) for s in ("gate", "up", "down"))
        halves, it0 = [], 0
        for iters in ITERS:
            halves.append((w, it0, iters))
            w += 2 * iters + 8
            it0 += iters
        return halves, gate_w, up_w, down_w

    def signal(ins, s, i, per, tiles=1):
        ins.then_inc(tile_used, tiles) if i % per == per - 1 else ins.then_inc(s, 1)

    def wait_product(eng, s, i, per, n0, tiles=1, before=0):
        if i % per == per - 1:
            eng.wait_ge(tile_used, n0 + (i // per + 1) * tiles)
        else:
            eng.wait_ge(s, before + i // per * (per - 1) + i % per + 1)

    ROT2 = [(W_IN2 + j, c) for j in (0, 1, 4, 5) for c in (0, 1)] + [(W_IN2 + 6, 0)]
    ROT2 += [(W_IN2 + j, c) for j in (7, 8, 9) for c in (0, 1)]

    def wait_rot2(eng, i):
        if ROT2[i][1]:
            eng.wait_ge(tile_used, ROT2[i][0] + 1)
        else:
            eng.wait_ge(rp_mm, 6 + sum(1 - last for _, last in ROT2[:i + 1]))

    @block.sync
    def _(sp):
        sp.dma_start(kst[:, 0:P], a["kst"][:, 0:P]).then_inc(id_in, 16)
        x_rows = a["x"].rearrange("o (c p) d -> p (o c) d", p=P)
        for j in range(4):
            c = slice(2 * P * j, 2 * P * j + 2 * P)
            sp.dma_start(x_nat[:, :, c], x_rows[:, :, c]).then_inc(x_in[j], 16)

        def ada_rows(s):
            w, c = (a["ada_w"], 256 * s) if s < ADA_1 else (a["w_ada_2"], 256 * (s - ADA_1))
            return w.rearrange("o (p j) n -> p (o j) n", j=NC), c

        def load_ada(s):
            w, c = ada_rows(s)
            if s == ADA_START:
                sp.wait_ge(row_summed, 1)
            else:
                sp.wait_ge(ada_summed, s - 1 - ROWS)
            sp.dma_start(ada[:, s % 2], w[:, :, c:c + 256]).then_inc(ada_in[s % 2], 16)

        def load_tile(n):
            loads, kc, cols = plan[n]
            sp.wait_ge(split_done, n - 1)
            for src, c0, m, p0 in loads:
                sp.dma_start(slot(raw, n, kc, cols)[p0:p0 + src.shape[0], :, c0:c0 + m], src).then_inc(raw_in[n % 2], 16)

        def load_gu(n0, i, w, it0, u, first=False):
            if not first:
                sp.wait_ge(split_done, n0 + 2 * i + u - 1)
            src = w[:, :, bass.ds((i + it0) * 256, 256)]
            sp.dma_start(slot(raw, n0 + u, NC, 256), src).then_inc(raw_in[(n0 + u) % 2], 16)

        def load_down(n0, w, k0, kc, j, u):
            n = n0 + 2 * j + u
            sp.wait_ge(split_done, n - 1)
            sp.dma_start(slot(raw, n, kc, 256), w[:, k0 + u * kc:k0 + u * kc + kc, 256 * j:256 * j + 256]).then_inc(raw_in[n % 2], 16)

        for i in range(2):
            halves, gate_w, up_w, down_w = ffn_tiles(i)
            for half, (n0, it0, iters) in enumerate(halves):
                i0 = 0
                s0 = (ADA_START, ADA_START + 16, 38, 50)[2 * i + half]
                if n0 == 0:
                    sp.wait_ge(c_in, 32)
                    sp.wait_ge(vec_in, 16 * N_VEC)
                    for q, s in enumerate(START_STEPS):
                        w, c = ada_rows(s)
                        if q == 7:
                            sp.wait_ge(ada_summed, 1)
                        sp.dma_start(start_ada(q), w[:, :, c:c + 256]).then_inc(start_in[q], 16)
                        if q in (1, 5):
                            load_gu(0, 0, (gate_w, up_w)[q == 5], 0, int(q == 5), first=True)
                    sp.dma_start(kst[:, P:K_COLS], a["kst"][:, P:K_COLS]).then_inc(kst_in, 16)
                    load_ada(s0)
                    load_ada(s0 + 1)
                    i0 = 1
                with sp.Fori(i0, iters) as it:
                    for u, w in enumerate((gate_w, up_w)):
                        load_gu(n0, it, w, it0, u)
                    for u in range(2):
                        s = s0 + u
                        w, c = ada_rows(s)
                        sp.wait_ge(ada_summed, it * 2 + (s - 1 - ROWS))
                        sp.dma_start(ada[:, s % 2], w[:, :, bass.ds(it * 512 + c, 256)]).then_inc(ada_in[s % 2], 16)
                kc = iters
                for j in range(4):
                    for u in range(2):
                        load_down(n0 + 2 * iters, down_w, 2 * it0, kc, j, u)
                    if i == 0 and j % 2 == 0:
                        for u in range(2):
                            load_ada(s0 + 2 * iters + j + u)
            if i == 0:
                for n in range(W_MIX, W_FFN2):
                    load_tile(n)
            else:
                for n in range(W_IN2, W_FFN3):
                    load_tile(n)
                    if n == W_CMP:
                        for j, name in enumerate(("cmp_w2_k_2", "cmp_w2_k_2", "cmp_w2_v_2")):
                            sp.wait_ge(split_done, n)
                            sp.dma_start(w2sb[:, j, :], a[name].rearrange("o p d -> p (o d)")).then_inc(w2_in, 16)
        up_w, down_w = w2d(a["w_up_2"]), w2d(a["w_down_2"])
        for half in range(2):
            n0 = W_FFN3 + 16 * half
            with sp.Fori(0, 4) as it:
                for u in range(2):
                    sp.wait_ge(split_done, it * 2 + (n0 + u - 1))
                    src = up_w[:, :, bass.ds(it * 512 + (2048 * half + 256 * u), 256)]
                    sp.dma_start(slot(raw, n0 + u, NC, 256), src).then_inc(raw_in[(n0 + u) % 2], 16)
            for j in range(4):
                for u in range(2):
                    load_down(n0 + 8, down_w, 16 * half, NC, j, u)
        for m in range(NC):
            sp.wait_ge(out_ev, m + 1)
            sp.dma_start(out.rearrange("o (c p) d -> p (o c) d", p=P)[:, :, P * m:P * m + P],
                         o_nat[:, :, P * m:P * m + P]).then_inc(out_done, 16)
        sp.wait_ge(out_done, 16 * NC)

    @block.gpsimd
    def _(pool):
        def split(n, kc, cols, i=0, per=0, first=False, rows=P):
            size = kc * cols
            src, hi, lo = (t[0:rows, n % 2, 0:size] for t in (raw, w_hi, w_lo))
            pool.wait_ge(raw_in[n % 2], i * (8 * per) + arrived[n])
            if not first:
                pool.wait_ge(tile_used, i * per + (n - 1))
            pool.tensor_tensor(hi[:, 0:8], src[:, 0:8], ones[:, 0:8], ALU.mult)
            hi_rest, src_rest = hi[:, 8:size], src[:, 8:size]
            pool.tensor_scalar(hi_rest, src_rest, 1.0, 1.0, ALU.mult, ALU.mult).then_inc(hi_done, 1)
            pool.wait_ge(hi_done, i * per + (n + 1))
            pool.tensor_tensor(lo, src, hi.bitcast(F32), ALU.subtract).then_inc(split_done, 1)

        def split_down(n0, kc):
            with pool.Fori(0, 4) as j:
                for u in range(2):
                    split(n0 + u, kc, 256, j, 2)

        for i in range(2):
            for n0, it0, iters in ffn_tiles(i)[0]:
                if n0 == 0:
                    pool.wait_ge(set_up, 1)
                    split(0, NC, 256, first=True)
                    split(1, NC, 256, first=True)
                with pool.Fori(1 if n0 == 0 else 0, iters) as it:
                    for u in range(2):
                        split(n0 + u, NC, 256, it, 2)
                split_down(n0 + 2 * iters, iters)
            for n in range(W_MIX, W_FFN2) if i == 0 else range(W_IN2, W_FFN3):
                split(n, *plan[n][1:])
        for half in range(2):
            n0 = W_FFN3 + 16 * half
            with pool.Fori(0, 4) as it:
                for u in range(2):
                    split(n0 + u, NC, 256, it, 2)
            split_down(n0 + 8, NC)

    def mla_units():
        return [dict(q=(lambda h, qc: q_all[:, h, P * qc:P * qc + P]), k=(lambda h, n: k_all[:, h, 0:n]), h=h,
                     width=lambda qc: T, mask=None, gate=None, scale=QK ** -0.5,
                     v=(lambda h, c: v_all[:, c, P * (h // 2):P * (h // 2) + P]), at=V_DIM * (h % 2), col=V_DIM * h,
                     added=0, last=True) for h in range(MLA_HEADS)]

    def half_of(t, h, c=None):
        r = HD * (h % 2)
        return t[r:r + HD] if c is None else t[r:r + HD, c]

    def causal_mask(qc):
        return kst[:, K_CAUSAL + T - P * (qc + 1):K_CAUSAL + T]

    SCORE_AT = [None, 0, 256, 640]

    def dsa_mask(qc):
        return causal_mask(0) if qc == 0 else score[:, SCORE_AT[qc]:SCORE_AT[qc] + P * (qc + 1)]

    def block2_units():
        units = []
        for h in range(NSA_HEADS):
            g = h // (NSA_HEADS // NSA_KV)
            for b, k in enumerate((ks, kw)):
                units.append(dict(
                    q=(lambda h, qc, g=g: half_of(qn, g, h % 4)[:, P * qc:P * qc + P]),
                    k=(lambda h, n, k=k, g=g: half_of(k, g)[:, 0:n]), h=h,
                    width=lambda qc: P * (qc + 1), mask=causal_mask, scale=HD ** -0.5,
                    gate=gsig[:, :, 3 * h + 1 + b:3 * h + 2 + b],
                    v=(lambda h, c, b=b: v2[:, c, P * b:P * b + P]), at=HD * g, col=HD * h,
                    added=2 * h + b + 1, last=b == 1))
        for h in range(8):
            units.append(dict(
                q=(lambda h, qc: half_of(qd, h, h // 2)[:, P * qc:P * qc + P]),
                k=(lambda h, n: half_of(kd, h)[:, 0:n]), h=h,
                width=lambda qc: P * (qc + 1), mask=dsa_mask, scale=HD ** -0.5, gate=None,
                v=(lambda h, c: v2[:, c, 192:320]), at=HD, col=HD * (NSA_HEADS + h), added=0, last=True))
        return units

    ATT = [dict(units=mla_units(), t0=0, u0=0, c0=0, o=o_nat1, p=p1, small=small1),
           dict(units=block2_units(), t0=4 * MLA_HEADS, u0=MLA_HEADS, c0=4, o=o_nat2, p=p2, small=small2)]
    B_S, B_T, B_O, B_PAIR = (0, 1, 2), (3, 5), (6, 7), 4
    pt = sq

    def finished_pair(att, u):
        if 0 <= u < len(att["units"]):
            x = att["units"][u]
            if x["last"] and x["h"] % 2 == 1:
                return pairs_done(att["units"], u) - 1
        return None

    def pairs_done(units, u):
        return sum(x["last"] and x["h"] % 2 == 1 for x in units[:u + 1])

    @block.tensor
    def _(pe):
        def mm3(o, wh, wl, xh, xl, start, stop):
            pe.matmul(o, wh, xh, start=start, stop=False)
            pe.matmul(o, wh, xl, start=False, stop=False)
            return pe.matmul(o, wl, xh, start=False, stop=stop)

        def group(o, n, kc, cols, c0, m, xh, xl, k0=0, start=True, stop=True):
            wh, wl = slot(w_hi, n, kc, cols), slot(w_lo, n, kc, cols)
            for k in range(kc):
                last = mm3(o, wh[:, k, c0:c0 + m], wl[:, k, c0:c0 + m], xh[:, k0 + k], xl[:, k0 + k],
                           start and k == 0, stop and k == kc - 1)
            return last

        def pair_of_groups(banks, n, h_ready, first_done=None):
            wh, wl = slot(w_hi, n, NC, 256), slot(w_lo, n, NC, 256)
            for k in range(NC):
                pe.wait_ge(h_lo_done, h_ready + k + 1)
                for m in range(2):
                    c = slice(P * m, P * m + P)
                    last = mm3(ps[:, banks[m]], wh[:, k, c], wl[:, k, c], h_hi[:, k], h_lo[:, k], k == 0, k == NC - 1)
                    if first_done is not None and k == NC - 1 and m == 0:
                        last.then_inc(first_done, 1)
            return last

        def norm_sum(i):
            if i:
                pe.wait_ge(n_std, i)
            if i in DIRECT:
                for m in range(NC):
                    pe.wait_ge(n_sq, 8 * i + m + 1)
                    last = pe.matmul(ps[:, B_NORM], ones[:], sq[:, m % 2], start=m == 0, stop=m == NC - 1)
                    last.then_inc(n_acc if m < NC - 1 else n_sum, 1)
                return
            pe.wait_ge(n_acc, added(i, 7))
            pe.matmul(ps[:, B_NORM], ones[:], sq_sum[:], start=True, stop=True).then_inc(n_sum, 1)

        def ada_mm_step(s, i=0, per=0, col=None):
            pe.wait_ge(ada_summed, i * per + (s + 1 - ROWS))
            for half in range(2):
                c = 2 * s + half
                o = ps[:, B_ADA, c:c + 1] if per == 0 else ps[:, B_ADA, bass.ds(i * (2 * per) + c, 1)]
                last = pe.matmul(o, ada_sum[:, s % 2, P * half:P * half + P], ones[:, 0:1], start=True, stop=True)
            last.then_inc(ada_mm, 1)

        pe.wait_ge(id_in, 16)
        for m in range(NC):
            if m % 2 == 0:
                pe.wait_ge(x_in[m // 2], 16)
            if m >= 4:
                pe.wait_ge(x_ready, X_INIT + m - 3)
            for c in range(NQ):
                last = pe.transpose(ps[:, m % 4, P * c:P * c + P], x_nat[:, c, P * m:P * m + P], ident)
            last.then_inc(x_tr, 1)
        pe.wait_ge(vec_in, 16 * N_VEC)
        pe.transpose(ps[:, B_NORM2, 0:109], vnat[0:109, 0, :], ident[0:109, 0:109])
        pe.transpose(ps[:, B_NORM2, 128:208], vnat[0:80, 1, :], ident[0:80, 0:80])
        for j in range(2):
            last = pe.transpose(ps[:, B_NORM2, V_PE + 32 * j:V_PE + 32 * j + 32], pe_nat[:, j, :], ident[0:32, 0:32])
        last.then_inc(vec_tr, 1)
        pe.wait_ge(set_up, 1)

        def start_row(pair):
            if pair == 0:
                pe.wait_ge(c_ready, 1)
            else:
                pe.wait_ge(row_ready, pair)
            pe.wait_ge(start_in[2 * pair], 16)
            for j in range(NC):
                last = pe.matmul(ps[0:1, 7, 0:256], cT[:, 0, j:j + 1], start_ada(2 * pair)[:, j], start=j == 0, stop=j == NC - 1)
            last.then_inc(row_summed, 1)

        def start_columns(pair):
            if pair:
                pe.wait_ge(mod_read, pair)
            for q, ready in ((0, row_ready), (1, ada_summed)):
                pe.wait_ge(ready, pair + 1)
                rows = slice(0, (1, P)[q])
                for half in range(2):
                    c = 2 * START_STEPS[2 * pair + q] + half
                    last = pe.matmul(ps[:, B_ADA, c:c + 1], ada_sum[rows, q, P * half:P * half + P], ones[rows, 0:1],
                                     start=True, stop=True)
                last.then_inc(ada_mm, 1)

        def first_gates(pair):
            wh, wl = slot(w_hi, 0, NC, 256), slot(w_lo, 0, NC, 256)
            pe.wait_ge(split_done, 1)
            for k in (2 * pair, 2 * pair + 1):
                pe.wait_ge(h_lo_done, k + 1)
                for m in range(2):
                    c = slice(P * m, P * m + P)
                    last = mm3(ps[:, m], wh[:, k, c], wl[:, k, c], h_hi[:, k], h_lo[:, k], k == 0, k == NC - 1)
            return last

        for pair in range(4):
            if pair == 0:
                start_row(0)
                norm_sum(0)
            start_columns(pair)
            if pair < 3:
                start_row(pair + 1)
            if pair:
                first_gates(pair - 1)
        first_gates(3).then_inc(tile_used, 1)

        def gate_up(i, half, it, tiles=(0, 1)):
            f = ffn[i]
            n0, it0, iters = ffn_tiles(i)[0][half]
            x0 = ((X_F1A, X_F1B), (X_F2A, X_F2B))[i][half]
            s0 = (ADA_START, ADA_START + 16, 38, 50)[2 * i + half]
            for u in tiles:
                pe.wait_ge(split_done, it * 2 + (n0 + u + 1))
                pe.wait_ge((f["silu"], f["hid"])[u], it * 2 + (2 * it0 + START))
                if half:
                    pe.wait_ge(x_ready, x0 - 2 + 2 * u)
                pair_of_groups((2 * u, 2 * u + 1), n0 + u, (0, 16)[i]).then_inc(tile_used, 1)
            for u in range(2):
                ada_mm_step(s0 + u, it, 2)

        def run_ffn(i):
            f = ffn[i]
            halves = ffn_tiles(i)[0]
            for half, (n0, it0, iters) in enumerate(halves):
                s0 = (ADA_START, ADA_START + 16, 38, 50)[2 * i + half]
                x0 = ((X_F1A, X_F1B), (X_F2A, X_F2B))[i][half]
                pe.wait_ge(mod_read, (4, 5, 7, 7)[2 * i + half])
                first = i == 0 and half == 0
                if first:
                    gate_up(0, 0, 0, tiles=(1,))
                with pe.Fori(int(first), iters) as it:
                    gate_up(i, half, it)
                pe.wait_ge(f["silu"], 2 * (it0 + iters) + START)
                n1 = n0 + 2 * iters
                with pe.Fori(0, 2) as jj:
                    for jo in range(2):
                        pe.wait_ge(x_ready, jj * 4 + (x0 + 2 * jo - 2))
                        for u in range(2):
                            n = n1 + 2 * jo + u
                            pe.wait_ge(split_done, jj * 4 + (n + 1))
                            pe.wait_ge(f["hid"], 2 * it0 + iters * (u + 1) + START)
                            for m in range(2):
                                last = group(ps[:, 2 * jo + m], n, iters, 256, P * m, P, g_hi, g_lo,
                                             k0=iters * u, start=u == 0, stop=u == 1)
                            last.then_inc(tile_used, 1)
                    if i == 0:
                        pe.wait_ge(mod_read, 5)
                        for u in range(2):
                            ada_mm_step(s0 + 2 * iters + u, jj, 2)

        run_ffn(0)

        norm_sum(1)

        def win_group(g, n, kc, cols, c0, m, xh, xl):
            if g >= 4:
                pe.wait_ge(win_free, g - 3)
            return group(ps[0:m, g % 4], n, kc, cols, c0, m, xh, xl)

        g = 0
        for j, outs in enumerate((((0, P), (P, P)), ((0, P), (P, P)), ((0, P), (64, QK)), ((0, P), (P, P)), ((0, P), (P, P)))):
            n = W_MIX + j
            pe.wait_ge(split_done, n + 1)
            if j == 0:
                signal(pair_of_groups((0, 1), n, 8, win_mm), win_mm, 1, 2)
                g = 2
                continue
            for c0, m in outs:
                last = win_group(g, n, NC, plan[n][2], c0, m, h_hi, h_lo)
                signal(last, win_mm, g, 2)
                g += 1
        for i, (b, s) in enumerate(((B_NORM, sq_sum), (B_NORM2, sq_sum2))):
            pe.wait_ge(l_acc, (3, 5)[i])
            pe.matmul(ps[:, b], ones[:], s[:], start=True, stop=True).then_inc(l_sum, 1)
        n = W_DFT_D
        pe.wait_ge(split_done, n + 1)
        ch, cl = slot(w_hi, n, 1, 256)[:, 0], slot(w_lo, n, 1, 256)[:, 0]
        for gr in range(4):
            for sp2 in range(2):
                pe.wait_ge(win_free, g - 3)
                if sp2 == 0:
                    pe.wait_ge(win_free, 7 + gr)
                for c in range(2):
                    s = slice(P * (2 * sp2 + c), P * (2 * sp2 + c) + P)
                    last = mm3(ps[:, g % 4, 256 * c:256 * c + 256], u_hi[:, gr, s], u_lo[:, gr, s], ch, cl, True, True)
                signal(last, win_mm, g - 10, 8)
                g += 1
        pe.wait_ge(win_free, 18)
        for j in range(2):
            pe.wait_ge(split_done, W_DFT_S + j + 1)
            th, tl = slot(w_hi, W_DFT_S + j, 4, T), slot(w_lo, W_DFT_S + j, 4, T)
            for gr in range(4):
                for c in range(NQ):
                    lo = (a_lo_0, a_lo_1)[c // 2][:, c % 2, gr, P * j:P * j + P]
                    last = mm3(ps[:, (g + gr) % 4], a_hi[:, c, gr, P * j:P * j + P], lo, th[:, c], tl[:, c],
                               j == 0 and c == 0, j == 1 and c == NQ - 1)
                if j == 1:
                    signal(last, win_mm, gr, 4)
                elif gr == 3:
                    last.then_inc(tile_used, 1)
        g += 4
        for j in range(2):
            n = W_FO + j
            pe.wait_ge(split_done, n + 1)
            for m in range(4):
                pe.wait_ge(win_free, max(g - 3, 22))
                signal(group(ps[:, g % 4], n, 4, 512, P * m, P, u_hi, u_lo), win_mm, m, 4)
                g += 1

        pe.wait_ge(win_free, 30)
        pe.wait_ge(l_lo_done, 5)

        def rot(r, lhs, rows, src):
            pe.wait_ge(rp_raw, r + 1)
            if r >= 2:
                pe.wait_ge(rp_out, r - 1)
            pe.matmul(ps[0:rows, 2 + r % 2], lhs, src[0:rows, r % 2], start=True, stop=True).then_inc(rp_rot, 1)

        pe.wait_ge(kst_in, 16)
        R96 = kst[0:QK, K_R96:K_R96 + QK]
        for r in range(10):
            if 1 <= r <= 8:
                h = r - 1
                if h % 4 == 0:
                    pe.wait_ge(split_done, W_QUP + h // 4 + 1)
                if r >= 3:
                    pe.wait_ge(rp_raw, r - 1)
                signal(group(ps[0:QK, r % 2], W_QUP + h // 4, 3, 4 * QK, QK * (h % 4), QK, ln_hi, ln_lo), rp_mm, h, 4)
            if r >= 1:
                rot(r - 1, R96, QK, rp_raw1)
        n = W_KVUP
        pe.wait_ge(split_done, n + 1)
        pe.wait_ge(l_std, 2)
        for h in range(MLA_HEADS):
            if h >= 3:
                pe.wait_ge(kv_ev, h - 2)
            group(ps[0:NOPE, 5 + h % 3], n, 2, 1024, P * h, NOPE, ln_hi, ln_lo, k0=3).then_inc(kv_mm, 1)
        vh, vl = (slot(t, n, 2, 1024).rearrange("p k (h c) -> p k h c", c=P) for t in (w_hi, w_lo))
        for c in range(NQ):
            i = MLA_HEADS + c
            pe.wait_ge(kv_ev, i - 2)
            for k in range(2):
                s = slice(P * c, P * c + P)
                last = mm3(ps[:, 5 + i % 3], ln_hi[:, 3 + k, s], ln_lo[:, 3 + k, s],
                           vh[:, k, :, NOPE:P], vl[:, k, :, NOPE:P], k == 0, k == 1)
            signal(last, kv_mm, i, MLA_HEADS + NQ)

        def attention(att):
            units, t0, u0 = att["units"], att["t0"], att["u0"]
            steps = 4 * len(units)

            def scores(t):
                x, qc = units[t // 4], t % 4
                if t >= 3:
                    pe.wait_ge(at_exp, t0 + t - 2)
                w = x["width"](qc)
                pe.matmul(ps[:, B_S[t % 3], 0:w], x["q"](x["h"], qc), x["k"](x["h"], w),
                          start=True, stop=True).then_inc(at_s, 1)

            def transposes(t):
                x, qc = units[t // 4], t % 4
                pe.wait_ge(at_exp, t0 + t + 1)
                if t >= 2:
                    pe.wait_ge(at_ev, t0 + t - 1)
                for c in range(x["width"](qc) // P):
                    last = pe.transpose(ps[:, B_T[t % 2], P * c:P * c + P],
                                        att["p"][:, t % 3, P * c:P * c + P], ident)
                last.then_inc(at_tr, 1)

            def values(t):
                u, qc = t // 4, t % 4
                x = units[u]
                pe.wait_ge(at_ev, t0 + t + 1)
                if qc == 0 and u >= 2:
                    pe.wait_ge(at_o, u0 + u - 1)
                n = x["width"](qc) // P
                for c in range(n):
                    last = pe.matmul(ps[:, B_O[u % 2], P * qc:P * qc + P], pt[:, t % 2, P * c:P * c + P],
                                     x["v"](x["h"], c), start=c == 0, stop=c == n - 1)
                last.then_inc(at_pv, 1)

            def turn_pair(u):
                pair = finished_pair(att, u)
                if pair is None:
                    return
                x = units[u]
                if x["added"]:
                    pe.wait_ge(at_sum, x["added"])
                else:
                    pe.wait_ge(at_o, u0 + u + 1)
                if pair:
                    pe.wait_ge(o_lo_done, att["c0"] + pair)
                for qc in range(NQ):
                    last = pe.transpose(ps[:, B_PAIR, P * qc:P * qc + P],
                                        att["o"][:, qc, x["col"] - HD:x["col"] + HD], ident)
                last.then_inc(at_pt, 1)

            for t in range(steps + 7):
                if t < steps:
                    scores(t)
                if 2 <= t < steps + 2:
                    transposes(t - 2)
                if 4 <= t < steps + 4:
                    values(t - 4)
                if t % 4 == 2:
                    turn_pair(t // 4 - 2)

        pe.wait_ge(rp_out, 9)
        pe.wait_ge(kv_ev, MLA_HEADS + NQ)
        pe.wait_ge(kr_copied, 8)
        attention(ATT[0])

        for i in range(16):
            n = W_GATE + i // 2
            if i % 2 == 0:
                pe.wait_ge(split_done, n + 1)
            if i >= 4:
                pe.wait_ge(gate_done, i - 3)
            last = group(ps[:, i % 4], n, NC, 256, P * (i % 2), P, h_hi, h_lo)
            signal(last, gate_mm, i, 2)
        pe.wait_ge(o_lo_done, 4)
        for i in range(8):
            n = W_MLA + i // 4
            if i % 4 == 0:
                pe.wait_ge(split_done, n + 1)
            pe.wait_ge(gate_done, 13 + i) if i < 4 else pe.wait_ge(yb_read, i - 3)
            signal(group(ps[:, i % 4], n, 4, 512, P * (i % 4), P, o_hi, o_lo), yb_mm, i, 4)
        pe.wait_ge(yb_lo, 8)
        for i in range(8):
            n = W_OUT + i // 2
            if i % 2 == 0:
                pe.wait_ge(split_done, n + 1)
            pe.wait_ge(yb_read, 5 + i) if i < 4 else pe.wait_ge(x_ready, X_MIX + i - 3)
            signal(group(ps[:, i % 4], n, NC, 256, P * (i % 2), P, h_hi, h_lo), wo_mm, i, 2)
        norm_sum(2)
        run_ffn(1)
        norm_sum(3)
        norm_sum(4)

        R64 = kst[:, K_R64:K_R64 + P]
        pend = [None]
        r = [0]

        def flush():
            if pend[0] is not None:
                rot(9 + pend[0], R64, P, rp_raw2)
                pend[0] = None

        def proj(n, half):
            i = 9 + r[0]
            pe.wait_ge(rp_raw, i - 1)
            signal(group(ps[:, i % 2], n, NC, 256, P * half, P, h_hi, h_lo), rp_mm, half, 2)
            flush()
            pend[0] = r[0]
            r[0] += 1

        def next_tile(n):
            pe.wait_ge(split_done, n + 1)

        n = W_IN2
        next_tile(n)
        pe.wait_ge(rp_raw, 9)
        signal(pair_of_groups((1, 0), n, 24, rp_mm), rp_mm, 1, 2)
        rot(9, R64, P, rp_raw2)
        pend[0], r[0] = 1, 2
        n = W_IN2 + 1
        next_tile(n)
        for c in range(2):
            proj(n, c)
        flush()
        next_tile(W_IN2 + 3)
        for c in range(NQ):
            s = slice(P * c, P * c + P)
            for j, (cols, c0) in enumerate(((256, 0), (92, 256))):
                th, tl = slot(w_hi, W_IN2 + 2 + j, NC, cols), slot(w_lo, W_IN2 + 2 + j, NC, cols)
                if j == 0 and c >= 2:
                    pe.wait_ge(nat_ev, c - 1)
                for k in range(NC):
                    last = mm3(ps[:, 6 + c % 2, c0:c0 + cols], h_hi[:, k, s], h_lo[:, k, s], th[:, k], tl[:, k],
                               k == 0, k == NC - 1)
            signal(last, nat_mm, c, NQ, tiles=2)
        pe.wait_ge(rp_out, 9 + 4)
        pe.wait_ge(nat_ev, 4)
        for j in range(12):
            qc, h = 1 + j // 4, j % 4
            if j >= 2:
                pe.wait_ge(ix_relu, j - 1)
            w = P * (qc + 1)
            pe.matmul(ps[:, 6 + j % 2, 0:w], half_of(qi, h, h // 2)[:, P * qc:P * qc + P], half_of(ki, h)[:, 0:w],
                      start=True, stop=True).then_inc(ix_mm, 1)
        for j in range(2):
            next_tile(W_IN2 + 4 + j)
            for c in range(2):
                proj(W_IN2 + 4 + j, c)
            n = W_IN2 + 6
        next_tile(n)
        proj(n, 0)
        flush()
        pe.wait_ge(ix_relu, 11)
        group(ps[:, 6], n, NC, 256, P, P, h_hi, h_lo).then_inc(tile_used, 1)
        for j in range(3):
            next_tile(W_IN2 + 7 + j)
            for c in range(2):
                proj(W_IN2 + 7 + j, c)
        flush()

        for j in range(2):
            pe.wait_ge(blk_lo_done, j + 1)
            pe.wait_ge(vc_ev, 1)
            for u in range(2):
                n = W_CMP + 2 * j + u
                next_tile(n)
                wh, wl = slot(w_hi, n, 16, P), slot(w_lo, n, 16, P)
                for l in range(16):
                    bh, bl = (t[:, 16 * u + l].rearrange("p g n -> p (g n)") for t in (blk_hi, blk_lo))
                    last = mm3(ps[0:2 * 32, (5, 7)[j], 0:P], bh, bl, wh[:, l], wl[:, l],
                               u == 0 and l == 0, u == 1 and l == 15)
                last.then_inc(tile_used, 1)
        for j in range(2):
            pe.wait_ge(cm_gelu, j + 1)
            pe.transpose(ps[:, (3, 1)[j], 0:HD], hid_nat[:, j], ident[0:HD, 0:HD]).then_inc(cm_hid, 1)
        pe.wait_ge(w2_in, 48)
        pe.wait_ge(cm_hid_ev, 2)
        pe.matmul(ps[:, 6, 0:64], w2sb[:, 0:2, :], hid_k[:, :, :], start=True, stop=True)
        for gr in range(2):
            last = pe.matmul(ps[:, 6, 64 + 64 * gr:128 + 64 * gr], hid_v[:, gr, :, :], w2sb[:, 2, :],
                             start=True, stop=True)
        last.then_inc(cm_kv, 1)
        pe.wait_ge(cm_kv_ev, 1)
        pe.wait_ge(rp_out, 9 + 15)
        for qc in range(NQ):
            if qc >= 2:
                pe.wait_ge(cm_sub, qc - 1)
            for h in range(NSA_HEADS):
                gr = h // 4
                last = pe.matmul(ps[:, 5 - qc % 2 + 2 * gr, 32 * (h % 4):32 * (h % 4) + 32],
                                 half_of(qn, gr, h % 4)[:, P * qc:P * qc + P],
                                 half_of(kcmp, gr)[:, 32 * gr:32 * gr + 32], start=True, stop=True)
            last.then_inc(cm_s, 1)
        for qc in range(NQ):
            pe.wait_ge(cm_p, qc + 1)
            if qc >= 2:
                pe.wait_ge(cm_ev, qc - 1)
            for gr in range(2):
                last = pe.transpose(ps[:, 3 * (qc % 2), P * gr:P * gr + P], cs[:, qc % 2, P * gr:P * gr + P], ident)
            last.then_inc(cm_tr, 1)
        for qc in range(NQ):
            pe.wait_ge(cm_ev, qc + 1)
            if qc >= 2:
                pe.wait_ge(cm_o_ev, qc - 1)
            for gr in range(NSA_KV):
                last = pe.matmul(ps[:, 1 + qc % 2, 4 * HD * gr:4 * HD * gr + 4 * HD], ptc[:, gr, P * qc:P * qc + P],
                                 v_diag[:, gr, :, :], start=True, stop=True)
            last.then_inc(cm_o, 1)
        pe.wait_ge(cm_o_ev, NQ)
        attention(ATT[1])

        pe.wait_ge(o_lo_done, 12)
        for i in range(8):
            n = W_OUT2 + i // 2
            if i % 2 == 0:
                next_tile(n)
            if i >= 4:
                pe.wait_ge(y_ready, i - 3)
            signal(group(ps[:, i % 4], n, NC, 256, P * (i % 2), P, h_hi, h_lo), wo2_mm, i, 2)
        norm_sum(5)
        norm_sum(6)

        for half in range(2):
            n0 = W_FFN3 + 16 * half
            with pe.Fori(0, 4) as it:
                for u in range(2):
                    pe.wait_ge(split_done, it * 2 + (n0 + u + 1))
                    pe.wait_ge(f3["relu"], it * 4 + (16 * half - 2 + 2 * u + START))
                    if half:
                        pe.wait_ge(y_ready, 14 + 2 * u)
                    pair_of_groups((2 * u, 2 * u + 1), n0 + u, 32).then_inc(tile_used, 1)
            pe.wait_ge(f3["relu"], 16 * half + 16 + START)
            n1 = n0 + 8
            with pe.Fori(0, 2) as jj:
                for jo in range(2):
                    pe.wait_ge(y_ready, jj * 4 + (8 * half + 8 + 2 * jo - 2))
                    for u in range(2):
                        n = n1 + 2 * jo + u
                        pe.wait_ge(split_done, jj * 4 + (n + 1))
                        pe.wait_ge(f3["hid"], 16 * half + 8 * (u + 1) + START)
                        for m in range(2):
                            last = group(ps[:, 2 * jo + m], n, NC, 256, P * m, P, g_hi, g_lo,
                                         k0=8 * u, start=u == 0, stop=u == 1)
                        last.then_inc(tile_used, 1)
        norm_sum(7)
        for m in range(NC):
            pe.wait_ge(x_ready, X_END + m + 1)
            if m >= 4:
                pe.wait_ge(out_ev, m - 3)
            for c in range(NQ):
                last = pe.transpose(ps[:, m % 4, P * c:P * c + P], xT[:, m, P * c:P * c + P], ident)
            last.then_inc(out_tr, 1)

    def norm_squares(act, i, ready, first, src):
        for m in range(NC):
            act.wait_ge(ready, first + m + 1)
            if m >= 2:
                act.wait_ge(n_acc, added(i, m - 2))
            elif i:
                act.wait_ge(n_acc, last_added(i - 1))
            act.activation(sq[:, m % 2], src[:, m], ACT.Square).then_inc(n_sq, 1)

    def norm_root(act, i):
        act.wait_ge(n_sum, i + 1)
        if i:
            act.wait_ge(n_rb, i)
        act.activation(std[:], ps[:, B_NORM], ACT.Sqrt, scale=1.0 / D, bias=eps[:, 0:1]).then_inc(n_std, 1)

    def mod_high(act, i, shift, chunks=range(NC)):
        for m in chunks:
            act.wait_ge(h_t, 8 * i + m + 1)
            act.activation(h_hi[:, m], tt[:, m % 2], ACT.Identity, bias=mod[:, shift + m:shift + m + 1]).then_inc(h_hi_done, 1)

    @block.scalar
    def _(act):

        def rows(v, lo, n, r, c=0):
            src = v.rearrange("o (m p) -> (o m) p", p=P) if len(v.shape) == 2 else v.rearrange("(m p) -> m p", p=P)
            act.dma_start(vnat[r:r + n, c, :], src[lo:lo + n]).then_inc(vec_in, 16)

        for j, name in enumerate(("c", "c_2")):
            act.dma_start(cT[:, j, :], a[name].rearrange("o (p j) -> p (o j)", j=NC)).then_inc(c_in, 16)
        for name, n, r in (("ffn1_norm", 8, V_FFN1), ("mix_norm", 8, V_MIX), ("ffn2_norm", 8, V_FFN2),
                           ("final_norm", 8, V_FINAL), ("q_norm", 3, V_QN), ("kv_norm", 2, V_KVN), ("ada_b", 72, V_ADA1)):
            rows(a[name], 0, n, r)
        for name, n, r in (("b_ada_2", 48, V_ADA2), ("g_pre_mix_2", 8, V_PREMIX), ("g_post_mix_2", 8, V_POSTMIX),
                           ("g_pre_ffn_2", 8, V_PREFFN), ("g_post_ffn_2", 8, V_POSTFFN)):
            rows(a[name], 0, n, r - P, 1)
        for j, name in enumerate(("cmp_pe_k_2", "cmp_pe_v_2")):
            for u in range(2):
                act.dma_start(pe_nat[:, j, HD * u:HD * u + HD], a[name].rearrange("o l d -> (o l) d")).then_inc(vec_in, 16)
        act.wait_ge(c_in, 32)
        act.activation(cT[:, 0, :], cT[:, 0, :], ACT.Silu).then_inc(c_ready, 1)
        act.wait_ge(set_up, 1)
        norm_squares(act, 0, x_ready, X_INIT, xT)
        for pair in range(4):
            act.wait_ge(row_summed, pair + 1)
            if pair:
                act.wait_ge(ada_mm, 2 * pair)
            act.copy(ada_sum[0:1, 0, :], ps[0:1, 7, 0:256]).then_inc(row_ready, 1)
            if pair == 0:
                norm_root(act, 0)
            mod_high(act, 0, 0, chunks=(2 * pair, 2 * pair + 1))

        def run_ffn(i):
            f = ffn[i]
            for half, (n0, it0, iters) in enumerate(ffn_tiles(i)[0]):
                with act.Fori(0, iters) as it:
                    for m in range(2):
                        act.wait_ge(tile_used, it * 2 + (n0 + 1))
                        act.wait_ge(f["hid"], it * 2 + (2 * it0 + START))
                        act.activation(sg[:, m], ps[:, m], ACT.Silu).then_inc(f["silu"], 1)
            norm_squares(act, (1, 3)[i], x_ready, (X_F1B, X_F2B)[i], xT)

        run_ffn(0)
        norm_root(act, 1)
        mod_high(act, 1, 24)

        for j in range(5):
            act.wait_ge(win_free, j + 1)
            act.wait_ge(l_acc, j - 1) if j >= 2 else act.wait_ge(n_acc, 16)
            act.activation(sq[:, j % 2], lat[:, j], ACT.Square).then_inc(l_sq, 1)
        for j in range(4):
            wait_product(act, win_mm, 6 + j, 2, W_MIX)
            act.copy(u_hi[:, j], ps[:, (6 + j) % 4]).then_inc(win_hi, 1)
        for j in range(8):
            g = 10 + j
            wait_product(act, win_mm, j, 8, W_DFT_D, before=5)
            act.copy(a_hi[:, 2 * (j % 2):2 * (j % 2) + 2, j // 2, :],
                     ps[:, g % 4].rearrange("p (c m) -> p c m", c=2)).then_inc(win_hi, 1)
        for i, (b, dst, n) in enumerate(((B_NORM, std, Q_RANK), (B_NORM2, rb, KV_RANK))):
            act.wait_ge(l_sum, i + 1)
            act.wait_ge(h_lo_done, 16)
            act.activation(dst[:], ps[:, b], ACT.Sqrt, scale=1.0 / n, bias=eps[:, 0:1]).then_inc(l_std, 1)
        for j in range(5):
            act.wait_ge(l_t, j + 1)
            act.copy(ln_hi[:, j], tt[:, j % 2]).then_inc(l_hi_done, 1)
        act.wait_ge(l_t, 5)
        act.dma_start(pos1[:], a["positions"].broadcast_to([P, T])).then_inc(pos_in, 16)
        for j in range(4):
            g = 18 + j
            wait_product(act, win_mm, j, 4, W_DFT_S, tiles=2, before=12)
            act.copy(u_hi[:, j], ps[:, g % 4]).then_inc(win_hi, 1)

        def sines(tab, src):
            b = src
            act.wait_ge(ang, 2 * b + 1)
            act.activation(tab[:, 0], tt[:, 0], ACT.Sin, scale=0.5).then_inc(sin_done, 1)
            act.wait_ge(ang, 2 * b + 2)
            act.activation(tab[:, 1], tt[:, 1], ACT.Sin, scale=-0.5, bias=eps[:, 1:2]).then_inc(sin_done, 1)

        sines(tab1, 0)
        for r in range(9):
            if r >= 2:
                act.wait_ge(rp_out, r - 1)
            if r == 0:
                act.wait_ge(win_free, 30)
                act.copy(rp_raw1[0:QK, 0], kr_raw[:]).then_inc(rp_raw, 1)
            else:
                wait_product(act, rp_mm, r - 1, 4, W_QUP)
                act.copy(rp_raw1[0:QK, r % 2], ps[0:QK, r % 2]).then_inc(rp_raw, 1)
        for i in range(MLA_HEADS + NQ):
            wait_product(act, kv_mm, i, MLA_HEADS + NQ, W_KVUP)
            if i < MLA_HEADS:
                act.copy(k_all[0:NOPE, i], ps[0:NOPE, 5 + i % 3]).then_inc(kv_ev, 1)
            else:
                act.copy(v_all[:, i - MLA_HEADS], ps[:, 5 + i % 3]).then_inc(kv_ev, 1)

        def attention(att, oh):
            units, t0, u0, p, small = (att[k] for k in ("units", "t0", "u0", "p", "small"))
            steps = 4 * len(units)

            def exps(t):
                x, qc = units[t // 4], t % 4
                w = x["width"](qc)
                act.wait_ge(at_nm, t0 + t + 1)
                if t >= 3:
                    act.wait_ge(at_tr, t0 + t - 2)
                src = ps[:, B_S[t % 3], 0:w] if x["mask"] is None else p[:, t % 3, 0:w]
                if qc == 0 and t >= 16:
                    act.wait_ge(at_o, u0 + t // 4 - 3)
                act.activation(p[:, t % 3, 0:w], src, ACT.Exp, bias=small[:, 8 + t % 8:9 + t % 8], scale=x["scale"],
                               accum_out=small[:, 16 + t % 16:17 + t % 16]).then_inc(at_exp, 1)

            def turn(t):
                x, qc = units[t // 4], t % 4
                w = x["width"](qc)
                act.wait_ge(at_tr, t0 + t + 1)
                if t >= 2:
                    act.wait_ge(at_pv, t0 + t - 1)
                act.copy(pt[:, t % 2, 0:w], ps[:, B_T[t % 2], 0:w]).then_inc(at_ev, 1)

            def out_high(u):
                pair = finished_pair(att, u)
                if pair is not None:
                    act.wait_ge(at_pt, att["c0"] + pair + 1)
                    act.copy(oh[:, pair], ps[:, B_PAIR]).then_inc(o_hi_done, 1)

            for t in range(steps + 8):
                if 3 <= t < steps + 3:
                    turn(t - 3)
                if t < steps:
                    exps(t)
                if t % 4 == 3:
                    out_high(t // 4 - 2)

        act.wait_ge(l_lo_done, 5)
        attention(ATT[0], o_hi)
        for i in range(16):
            wait_product(act, gate_mm, i, 2, W_GATE)
            act.activation(gate[:, i], ps[:, i % 4], ACT.Sigmoid).then_inc(gate_done, 1)
        for i in range(8):
            act.wait_ge(yb_sum, i + 1)
            act.copy(h_hi[:, i], tt[:, i % 2]).then_inc(yb_hi, 1)
        norm_squares(act, 2, x_ready, X_MIX, xT)
        norm_root(act, 2)
        mod_high(act, 2, 48)
        act.dma_start(pos2[:], a["positions_2"].broadcast_to([P, T])).then_inc(pos_in, 16)
        run_ffn(1)
        norm_root(act, 3)
        norm_squares(act, 4, x_ready, X_FINAL, xT)
        norm_root(act, 4)
        mod_high(act, 3, 72)

        sines(tab2, 1)

        def raw_copy(i):
            wait_rot2(act, i)
            act.wait_ge(rp_out, 9 + i - 1)
            act.copy(rp_raw2[:, (9 + i) % 2], ps[:, (9 + i) % 2]).then_inc(rp_raw, 1)

        for i in range(4):
            raw_copy(i)
        for c in range(NQ):
            wait_product(act, nat_mm, c, NQ, W_IN2 + 2, tiles=2)
            act.activation(gsig[:, c, :], ps[:, 6 + c % 2, 256:280], ACT.Sigmoid).then_inc(nat_sig, 1)
        for j in range(12):
            act.wait_ge(ix_mm, j + 1)
            if j >= 2:
                act.wait_ge(ix_acc, j - 1)
            w = P * (2 + j // 4)
            act.activation(relu[:, j % 2, 0:w], ps[:, 6 + j % 2, 0:w], ACT.Relu).then_inc(ix_relu, 1)
        for i in range(4, 9):
            raw_copy(i)
        act.wait_ge(tile_used, W_IN2 + 7)
        act.copy(vc[:, 0:T], ps[:, 6]).then_inc(vc_ev, 1)
        for i in range(9, 15):
            raw_copy(i)
            if i in (10, 14):
                j = (i - 10) // 4
                act.wait_ge(blk_clear, 2)
                act.wait_ge(blk_t, 2 * j + 2)
                if j:
                    act.wait_ge(tile_used, W_CMP + 2)
                for gr in range(2):
                    rows = slice(HD * gr, HD * gr + HD)
                    last = act.copy(blk_hi[rows, :, gr, :], tt[rows].rearrange("p a (l n) -> p (a l) n", n=32))
                last.then_inc(blk_hi_done, 1)
        for j in range(2):
            act.wait_ge(tile_used, W_CMP + 2 * j + 2)
            act.activation(hid_nat[:, j], ps[0:HD, (5, 7)[j], 0:P], ACT.Gelu_apprx_tanh).then_inc(cm_gelu, 1)
        for qc in range(NQ):
            act.wait_ge(cm_sub, qc + 1)
            act.activation(cs[:, qc % 2], cs[:, qc % 2], ACT.Exp, scale=HD ** -0.5).then_inc(cm_exp, 1)
        for qc in range(NQ):
            act.wait_ge(cm_tr, qc + 1)
            act.copy(ptc[:, :, P * qc:P * qc + P],
                     ps[:, 3 * (qc % 2), 0:2 * P].rearrange("p (g q) -> p g q", g=2)).then_inc(cm_ev, 1)
        for qc in range(NQ):
            act.wait_ge(cm_o, qc + 1)
            act.copy(o_nat2[:, qc, 0:NSA_HEADS * HD], ps[:, 1 + qc % 2]).then_inc(cm_o_ev, 1)
        attention(ATT[1], h_hi)

        norm_squares(act, 5, y_ready, 0, y2)
        norm_root(act, 5)
        norm_squares(act, 6, x_ready, X_ATT, xT)
        norm_root(act, 6)
        mod_high(act, 4, 72 + 24)
        for half in range(2):
            n0 = W_FFN3 + 16 * half
            with act.Fori(0, 4) as it:
                for j in range(4):
                    u, m = j // 2, j % 2
                    act.wait_ge(tile_used, it * 2 + (n0 + u + 1))
                    act.wait_ge(f3["sq"], it * 4 + (16 * half + START))
                    act.activation(sg3[:, j], ps[:, j], ACT.Relu).then_inc(f3["relu"], 1)
        norm_squares(act, 7, y_ready, 16, y2)
        norm_root(act, 7)
        for m in range(NC):
            act.wait_ge(out_tr, m + 1)
            act.copy(o_nat[:, :, P * m:P * m + P], ps[:, m % 4].rearrange("p (c d) -> p c d", c=NQ)).then_inc(out_ev, 1)

    @block.vector
    def _(dve):
        count = [0]

        def step(ins):
            count[0] = count[0] + 1
            ins.then_inc(dve_step, 1)
            dve.wait_ge(dve_step, count[0])

        def column(t, c):
            return t[:, c:c + 1]

        step(dve.memset(eps[:, 0:1], EPS))
        step(dve.memset(eps[:, 1:2], float(np.pi / 2)))
        dve.memset(ones[:], 1.0).then_inc(set_up, 1)
        for k, s in enumerate([f[name] for f in ffn for name in ("silu", "hid")] + [f3[name] for name in ("relu", "sq", "hid")]):
            dve.memset(free[:, k:k + 1], 0.0).then_inc(s, START)

        def norm_add(i, m):
            dve.wait_ge(n_sq, 8 * i + m + 1)
            if m == 0:
                if i:
                    dve.wait_ge(n_sum, i)
                    dve.wait_ge(n_acc, last_added(i - 1))
                dve.tensor_copy(sq_sum[:], sq[:, 0]).then_inc(n_acc, 1)
            else:
                dve.wait_ge(n_acc, added(i, m - 1))
                dve.tensor_tensor(sq_sum[:], sq_sum[:], sq[:, m % 2], ALU.add).then_inc(n_acc, 1)

        def norm_inverse(i):
            dve.wait_ge(n_std, i + 1)
            dve.reciprocal(rb[:], std[:]).then_inc(n_rb, 1)
            dve.wait_ge(n_rb, i + 1)

        def chunks_then_add(i, chunk):
            for m in range(NC + 1):
                if m < NC:
                    chunk(m)
                if m >= 1 and i not in DIRECT:
                    norm_add(i, m - 1)

        def modulated(i, factor, shift, chunks=range(NC)):
            for m in [*chunks, None]:
                if m is not None:
                    if m >= 2:
                        dve.wait_ge(h_lo_done, 8 * i + m - 1)
                    dve.scalar_tensor_tensor(tt[:, m % 2], xT[:, m], column(fac, factor + m), rb[:],
                                             ALU.mult, ALU.mult).then_inc(h_t, 1)
                if m != chunks[0]:
                    k = chunks[-1] if m is None else m - 1
                    dve.wait_ge(h_hi_done, 8 * i + k + 1)
                    dve.wait_ge(h_t, 8 * i + k + 1)
                    dve.scalar_tensor_tensor(h_lo[:, k], tt[:, k % 2], column(mod, shift + k), h_hi[:, k].bitcast(F32),
                                             ALU.add, ALU.subtract).then_inc(h_lo_done, 1)

        def weighted_sum(dst, w, c):
            step(dve.tensor_scalar(dst, w[:, 0], cT[:, c, 0:1], None, ALU.mult))
            for j in range(1, NC):
                ins = dve.scalar_tensor_tensor(dst, w[:, j], cT[:, c, j:j + 1], dst, ALU.mult, ALU.add)
                if j < NC - 1:
                    step(ins)
            ins.then_inc(ada_summed, 1)

        def ada_step(s, i=0, per=0):
            b = s % 2
            dve.wait_ge(ada_in[b], i * (8 * per) + 16 * ((s - ADA_START) // 2 + 1))
            dve.wait_ge(ada_mm, i * per + (s - 1))
            weighted_sum(ada_sum[:, b], ada[:, b], 0 if s < ADA_1 else 1)

        def copy_x(m):
            dve.wait_ge(x_tr, m + 1)
            dve.tensor_copy(xT[:, m], ps[:, m % 4]).then_inc(x_ready, 1)

        chunks_then_add(0, copy_x)
        dve.wait_ge(vec_tr, 1)
        for lo, hi in ((0, 109), (128, 208), (256, 320)):
            ins = dve.tensor_copy(vec[:, lo:hi], ps[:, B_NORM2, lo:hi])
        ins.then_inc(vec_ready, 1)
        dve.wait_ge(vec_ready, 1)
        def read_mod(lo, hi, bias, steps_done):
            dve.wait_ge(ada_mm, steps_done)
            dve.tensor_tensor(mod[:, lo:hi], ps[:, B_ADA, lo:hi], vec[:, bias:bias + hi - lo], ALU.add).then_inc(mod_read, 1)
            reads[0] += 1
            dve.wait_ge(mod_read, reads[0])
        reads = [0]

        def gained(dst, scale_at, gain):
            step(dve.scalar_tensor_tensor(fac[:, dst:dst + 8], mod[:, scale_at:scale_at + 8], 1.0, vec[:, gain:gain + 8],
                                          ALU.add, ALU.mult))

        for pair in range(4):
            c = slice(2 * pair, 2 * pair + 2)
            if pair == 0:
                dve.wait_ge(c_ready, 1)
            else:
                dve.wait_ge(ada_mm, 2 * pair)
            dve.wait_ge(start_in[2 * pair + 1], 16)
            weighted_sum(ada_sum[:, 1], start_ada(2 * pair + 1), 0)
            if pair == 0:
                norm_inverse(0)
            dve.wait_ge(ada_mm, 2 * pair + 2)
            m2, p2v, v2v = (t.rearrange("p (a b) -> p a b", a=2)[:, :, c]
                            for t in (mod[:, 0:16], ps[:, B_ADA, 0:16], vec[:, V_ADA1:V_ADA1 + 16]))
            dve.tensor_tensor(m2, p2v, v2v, ALU.add).then_inc(mod_read, 1)
            reads[0] += 1
            dve.wait_ge(mod_read, reads[0])
            step(dve.scalar_tensor_tensor(fac[:, A_FFN1 + c.start:A_FFN1 + c.stop], mod[:, 8 + c.start:8 + c.stop], 1.0,
                                          vec[:, V_FFN1 + c.start:V_FFN1 + c.stop], ALU.add, ALU.mult))
            modulated(0, A_FFN1, 0, chunks=(c.start, c.start + 1))

        def add_product(bank, m, factor):
            dve.scalar_tensor_tensor(xT[:, m], ps[:, bank], column(fac, factor + m), xT[:, m],
                                     ALU.mult, ALU.add).then_inc(x_ready, 1)

        def run_ffn(i):
            f = ffn[i]
            for half, (n0, it0, iters) in enumerate(ffn_tiles(i)[0]):
                s0 = (ADA_START, ADA_START + 16, 38, 50)[2 * i + half]
                start = count[0]
                per = 14 + 4
                with dve.Fori(0, iters) as it:
                    count[0] = it * per + start
                    for u in range(2):
                        ada_step(s0 + u, it, 2)
                    for m in range(2):
                        dve.wait_ge(f["silu"], it * 2 + (2 * it0 + m + 1 + START))
                        dve.wait_ge(tile_used, it * 2 + (n0 + 2))
                        k = 2 * it + m
                        dve.wait_ge(f["hid"], it * 2 + (2 * it0 + m + START))
                        step(dve.tensor_tensor(tt[:, m], sg[:, m], ps[:, 2 + m], ALU.mult))
                        step(dve.tensor_copy(g_hi[:, bass.ds(k, 1)], tt[:, m:m + 1]))
                        dve.tensor_tensor(g_lo[:, bass.ds(k, 1)], tt[:, m:m + 1], g_hi[:, bass.ds(k, 1)].bitcast(F32),
                                          ALU.subtract).then_inc(f["hid"], 1)
                count[0] = start + per * iters
                if i == 0 and half == 0:
                    read_mod(16, 40, V_ADA1 + 16, ADA_START + 12)
                    step(dve.tensor_scalar(fac[:, A_G1:A_G1 + 8], mod[:, 16:24], 0.5, None, ALU.mult))
                x0 = ((X_F1A, X_F1B), (X_F2A, X_F2B))[i][half]
                n1 = n0 + 2 * iters

                def down(m):
                    if i == 0 and m % 4 == 0:
                        for u in range(2):
                            ada_step(s0 + 2 * iters + m // 2 + u)
                    dve.wait_ge(tile_used, n1 + 2 * (m // 2) + 2)
                    add_product(m % 4, m, (A_G1, A_G3)[i])

                if half == 0:
                    for m in range(NC):
                        down(m)
                    dve.wait_ge(x_ready, x0 + 8)
                else:
                    chunks_then_add((1, 3)[i], down)

        run_ffn(0)
        read_mod(40, 72, V_ADA1 + 40, ADA_STEPS_1)
        read_mod(72, 2 * ADA_STEPS_1, V_ADA2, ADA_STEPS_1)
        gained(A_MIX, 32, V_MIX)
        gained(A_FFN2, 56, V_FFN2)
        step(dve.tensor_scalar(fac[:, A_G3:A_G3 + 8], mod[:, 64:72], 0.5, None, ALU.mult))
        norm_inverse(1)
        modulated(1, A_MIX, 24)

        for j in range(5):
            wait_product(dve, win_mm, j, 2, W_MIX)
            dve.tensor_copy(lat[:, j], ps[:, j % 4]).then_inc(win_free, 1)
        wait_product(dve, win_mm, 5, 2, W_MIX)
        dve.tensor_copy(kr_raw[:], ps[0:QK, 1]).then_inc(win_free, 1)
        for j in range(5):
            dve.wait_ge(l_sq, j + 1)
            s = sq_sum if j < 3 else sq_sum2
            if j in (0, 3):
                dve.wait_ge(n_sum, 2)
                dve.tensor_copy(s[:], sq[:, j % 2]).then_inc(l_acc, 1)
            else:
                dve.wait_ge(l_acc, j)
                dve.tensor_tensor(s[:], s[:], sq[:, j % 2], ALU.add).then_inc(l_acc, 1)
        for j in range(4):
            dve.wait_ge(win_hi, j + 1)
            dve.tensor_tensor(u_lo[:, j], ps[:, (6 + j) % 4], u_hi[:, j].bitcast(F32), ALU.subtract).then_inc(win_free, 1)
        for j in range(8):
            g = 10 + j
            dve.wait_ge(win_hi, 4 + j + 1)
            sp2, gr = j % 2, j // 2
            dve.tensor_tensor((a_lo_0, a_lo_1)[sp2][:, :, gr, :], ps[:, g % 4].rearrange("p (c m) -> p c m", c=2),
                              a_hi[:, 2 * sp2:2 * sp2 + 2, gr, :].bitcast(F32), ALU.subtract).then_inc(win_free, 1)
        for i, dst in enumerate((std, rb)):
            dve.wait_ge(l_std, i + 1)
            dve.reciprocal(dst[:], dst[:]).then_inc(l_rb, 1)
        dve.wait_ge(l_rb, 2)
        for j in range(6):
            if j < 5:
                if j >= 2:
                    dve.wait_ge(l_lo_done, j - 1)
                dve.scalar_tensor_tensor(tt[:, j % 2], lat[:, j], column(vec, V_QN + j), (std if j < 3 else rb)[:],
                                         ALU.mult, ALU.mult).then_inc(l_t, 1)
            if j >= 1:
                k = j - 1
                dve.wait_ge(l_hi_done, k + 1)
                dve.wait_ge(l_t, k + 1)
                dve.tensor_tensor(ln_lo[:, k], tt[:, k % 2], ln_hi[:, k].bitcast(F32), ALU.subtract).then_inc(l_lo_done, 1)
        for j in range(4):
            dve.wait_ge(win_hi, 12 + j + 1)
            dve.tensor_tensor(u_lo[:, j], ps[:, (18 + j) % 4], u_hi[:, j].bitcast(F32), ALU.subtract).then_inc(win_free, 1)
        def angles(b, pos, tab):
            freq = column(kst, K_FREQ + b)
            dve.wait_ge(kst_in, 16)
            dve.wait_ge(pos_in, 16 * (b + 1))
            dve.wait_ge(l_lo_done, 5)
            step(dve.tensor_copy(tt[:, 0], pos))
            step(dve.tensor_scalar(tt[:, 0], tt[:, 0], freq, None, ALU.mult))
            magic = 1.5 * 2.0 ** 23
            step(dve.tensor_scalar(tt[:, 1], tt[:, 0], float(1 / (2 * np.pi)), magic, ALU.mult, ALU.add))
            step(dve.tensor_scalar(tt[:, 1], tt[:, 1], -magic, None, ALU.add))
            c1 = 6.28125
            c2 = float(np.float32(np.round((2 * np.pi - c1) * 2 ** 21) / 2 ** 21))
            c3 = float(2 * np.pi - c1 - c2)
            for c in (c1, c2, c3):
                step(dve.scalar_tensor_tensor(tt[:, 0], tt[:, 1], -c, tt[:, 0], ALU.mult, ALU.add))
            dve.tensor_scalar(tt[:, 0], tt[:, 0], 1.0, None, ALU.mult).then_inc(ang, 1)
            dve.wait_ge(ang, 2 * b + 1)
            dve.scalar_tensor_tensor(tt[:, 1], tt[:, 0], -1.0, tt[:, 0], ALU.mult, ALU.max).then_inc(ang, 1)
            dve.wait_ge(sin_done, 2 * b + 2)
            step(dve.scalar_tensor_tensor(tt[:, 0], tab[:, 0], 2.0, tab[:, 1], ALU.mult, ALU.mult))
            step(dve.scalar_tensor_tensor(tt[:, 1], tab[:, 0], -2.0, tab[:, 0], ALU.mult, ALU.mult))
            step(dve.tensor_scalar(tab[:, 0], tt[:, 1], 1.0, None, ALU.add))
            step(dve.tensor_copy(tab[:, 1], tt[:, 0]))

        angles(0, pos1[:], tab1)

        for j in range(NC):
            wait_product(dve, win_mm, j, 4, W_FO, before=15)
            dve.tensor_copy(ya[:, j], ps[:, (22 + j) % 4]).then_inc(win_free, 1)

        def rotate(r, rows, src, tab, dst):
            dve.wait_ge(rp_raw, r + 1)
            dve.wait_ge(rp_out, r)
            step(dve.tensor_tensor(tt[0:rows, 0], src[0:rows, r % 2], tab[0:rows, 0], ALU.mult))
            dve.wait_ge(rp_rot, r + 1)
            step(dve.tensor_tensor(tt[0:rows, 1], ps[0:rows, 2 + r % 2], tab[0:rows, 1], ALU.mult))
            dve.tensor_tensor(dst, tt[0:rows, 0], tt[0:rows, 1], ALU.add).then_inc(rp_out, 1)

        rotate(0, QK, rp_raw1, tab1, kr_raw[:])
        dve.wait_ge(rp_out, 1)
        for h in range(MLA_HEADS):
            dve.tensor_copy(k_all[NOPE:QK, h], kr_raw[NOPE:QK]).then_inc(kr_copied, 1)
        for h in range(MLA_HEADS):
            rotate(1 + h, QK, rp_raw1, tab1, q_all[:, h])

        def attention(att, oh, ol, between=None):
            units, t0, u0, p, small = (att[k] for k in ("units", "t0", "u0", "p", "small"))
            steps = 4 * len(units)

            def maxima(t):
                x, qc = units[t // 4], t % 4
                w = x["width"](qc)
                dve.wait_ge(at_s, t0 + t + 1)
                s = ps[:, B_S[t % 3], 0:w]
                mx = small[:, t % 8:t % 8 + 1]
                if x["mask"] is None:
                    step(dve.tensor_reduce(mx, s, AX, ALU.max))
                else:
                    if t >= 3:
                        dve.wait_ge(at_tr, t0 + t - 2)
                    step(dve.tensor_tensor_reduce(out=p[:, t % 3, 0:w], in0=s, in1=x["mask"](qc), scale=1.0, scalar=-3e38,
                                                  op0=ALU.add, op1=ALU.max, accum_out=mx))
                dve.tensor_scalar(small[:, 8 + t % 8:9 + t % 8], mx, -x["scale"], None, ALU.mult).then_inc(at_nm, 1)

            def normalised(u):
                x = units[u]
                rs = small[:, 32 + 4 * (u % 2):36 + 4 * (u % 2)]
                dve.wait_ge(at_pv, t0 + 4 * u + 4)
                step(dve.reciprocal(rs, small[:, 16 + 4 * (u % 4):20 + 4 * (u % 4)]))
                if x["gate"] is not None:
                    step(dve.tensor_tensor(rs, rs, x["gate"].rearrange("p q o -> p (q o)"), ALU.mult))
                src = ps[:, B_O[u % 2]].rearrange("p (q d) -> p q d", q=NQ)[:, :, x["at"]:x["at"] + HD]
                rs_all = rs.unsqueeze(2).broadcast_to([P, NQ, HD])
                dst = att["o"][:, :, x["col"]:x["col"] + HD]
                if not x["added"]:
                    dve.tensor_tensor(dst, src, rs_all, ALU.mult).then_inc(at_o, 1)
                else:
                    new = tt[:, 0, 0:NQ * HD].rearrange("p (q d) -> p q d", q=NQ)
                    if x["added"] > 1:
                        dve.wait_ge(at_sum, x["added"] - 1)
                    dve.tensor_tensor(new, src, rs_all, ALU.mult).then_inc(at_o, 1)
                    dve.wait_ge(at_o, u0 + u + 1)
                    dve.tensor_tensor(dst, dst, new, ALU.add).then_inc(at_sum, 1)

            def out_low(u):
                pair = finished_pair(att, u)
                if pair is not None:
                    dve.wait_ge(o_hi_done, att["c0"] + pair + 1)
                    dve.tensor_tensor(ol[:, pair], ps[:, B_PAIR], oh[:, pair].bitcast(F32),
                                      ALU.subtract).then_inc(o_lo_done, 1)

            for t in range(steps + 10):
                if t < steps:
                    maxima(t)
                if t % 4 == 0 and 0 <= t // 4 - 2 < len(units):
                    normalised(t // 4 - 2)
                if t % 4 == 1:
                    out_low(t // 4 - 3)
                if between and t % 3 == 2:
                    between(1)

        dve.wait_ge(rp_out, 9)
        dve.wait_ge(l_hi_done, 5)
        attention(ATT[0], o_hi, o_lo)

        for m in range(NC):
            dve.wait_ge(gate_done, m + 1)
            step(dve.tensor_tensor(ya[:, m], ya[:, m], gate[:, m], ALU.mult))
        for m in range(NC + 1):
            if m < NC:
                wait_product(dve, yb_mm, m, 4, W_MLA)
                dve.wait_ge(gate_done, 16)
                dve.tensor_tensor(gate[:, m], ps[:, m % 4], gate[:, 8 + m], ALU.mult).then_inc(yb_read, 1)
                dve.wait_ge(yb_read, m + 1)
                if m >= 2:
                    dve.wait_ge(yb_lo, m - 1)
                dve.tensor_tensor(tt[:, m % 2], gate[:, m], ya[:, m], ALU.add).then_inc(yb_sum, 1)
            if m >= 1:
                k = m - 1
                dve.wait_ge(yb_hi, k + 1)
                dve.wait_ge(yb_sum, k + 1)
                dve.tensor_tensor(h_lo[:, k], tt[:, k % 2], h_hi[:, k].bitcast(F32), ALU.subtract).then_inc(yb_lo, 1)

        def mix_out(m):
            wait_product(dve, wo_mm, m, 2, W_OUT)
            dve.scalar_tensor_tensor(xT[:, m], ps[:, m % 4], column(mod, 40 + m), xT[:, m],
                                     ALU.mult, ALU.add).then_inc(x_ready, 1)

        chunks_then_add(2, mix_out)
        norm_inverse(2)
        modulated(2, A_FFN2, 48)
        run_ffn(1)
        read_mod(2 * ADA_STEPS_1, 120, V_ADA2 + 2 * ADA_STEPS_1 - 72, ADA_STEPS)
        gained(A_PREMIX, 72 + 8, V_PREMIX)
        gained(A_PREFFN, 72 + 32, V_PREFFN)
        for dst, g, v in ((A_POSTMIX, 72 + 16, V_POSTMIX), (A_POSTFFN, 72 + 40, V_POSTFFN)):
            step(dve.tensor_tensor(fac[:, dst:dst + 8], mod[:, g:g + 8], vec[:, v:v + 8], ALU.mult))
        norm_inverse(3)

        def final_norm(m):
            dve.scalar_tensor_tensor(xT[:, m], xT[:, m], column(vec, V_FINAL + m), rb[:],
                                     ALU.mult, ALU.mult).then_inc(x_ready, 1)

        chunks_then_add(4, final_norm)
        norm_inverse(4)
        modulated(3, A_PREMIX, 72)

        dve.wait_ge(h_lo_done, 32)
        angles(1, pos2[:], tab2)
        def rotate2(i, dst):
            rotate(9 + i, P, rp_raw2, tab2, dst)

        rotate2(0, qi[:, 0])
        rotate2(1, qi[:, 1])
        rotate2(2, kd[:])
        rotate2(3, ki[:])
        for t in (kc, vc):
            step(dve.memset(t[:, T:T + CMP_STRIDE], 0.0))
        step(dve.memset(hid_k[:], 0.0))
        step(dve.memset(hid_v[:], 0.0))
        for t in (blk_hi, blk_lo):
            dve.memset(t[:].bitcast(F32), 0.0).then_inc(blk_clear, 1)
        dve.wait_ge(blk_clear, 2)
        for c in range(NQ):
            dve.wait_ge(nat_sig, c + 1)
            b = 6 + c % 2
            step(dve.tensor_copy(v2[:, c, 0:256], ps[:, b, 0:256]))
            step(dve.tensor_copy(v2[:, c, 256:320], ps[:, b, 280:344]))
            dve.tensor_scalar(wsc[:, c, :], ps[:, b, 344:348], IDX_HEADS ** -0.5 * 64 ** -0.5, None, ALU.mult).then_inc(nat_ev, 1)
        dve.wait_ge(nat_ev, NQ)
        for j in range(12):
            qc, h = 1 + j // 4, j % 4
            w = P * (qc + 1)
            s = score[:, SCORE_AT[qc]:SCORE_AT[qc] + w]
            dve.wait_ge(ix_relu, j + 1)
            if h == 0:
                dve.tensor_scalar(s, relu[:, j % 2, 0:w], wsc[:, qc, 0:1], None, ALU.mult).then_inc(ix_acc, 1)
            else:
                dve.wait_ge(ix_acc, j)
                dve.scalar_tensor_tensor(s, relu[:, j % 2, 0:w], wsc[:, qc, h:h + 1], s, ALU.mult, ALU.add).then_inc(ix_acc, 1)
            if h == 3:
                dve.wait_ge(ix_acc, j + 1)
                step(dve.tensor_tensor(s, s, causal_mask(qc), ALU.add))
        ROUNDS = TOPK // 8

        def select_round(i):
            qc, r = 1 + i // ROUNDS, i % ROUNDS
            s = score[:, SCORE_AT[qc]:SCORE_AT[qc] + P * (qc + 1)]
            step(dve.max(c8[:, 3, :], s))
            step(dve.match_replace(out=s, in_to_replace=c8[:, 3, :], in_values=s, imm_value=TAKEN))
            if r == ROUNDS - 1:
                step(dve.tensor_scalar(s, s, TAKEN / 2, NEG, ALU.is_gt, ALU.mult))

        step(dve.memset(v_diag[:], 0.0))
        selected = [0]

        def select(rounds):
            for _ in range(min(rounds, 3 * ROUNDS - selected[0])):
                select_round(selected[0])
                selected[0] += 1

        for i in range(4):
            rotate2(4 + i, qn[:, i])
            select(2)
        rotate2(8, kc[:, 0:T])
        select(2)
        for i, t in enumerate((ks, kw)):
            rotate2(9 + i, t[:])
            select(2)

        def blocks(j):
            src = (kc, vc)[j]
            if j:
                dve.wait_ge(vc_ev, 1)
            dve.wait_ge(rp_out, 9 + 9)
            v = src[:].rearrange("p (a b) -> p b a", b=CMP_STRIDE)
            for c in range(2):
                pe_col = vec[:, V_PE + 32 * j + 16 * c:V_PE + 32 * j + 16 * c + 16].unsqueeze(2).broadcast_to([P, 16, 32])
                dve.tensor_tensor(tt[:, c].rearrange("p (l n) -> p l n", n=32), v[:, :, c:c + 32], pe_col,
                                  ALU.add).then_inc(blk_t, 1)

        def blocks_low(j):
            dve.wait_ge(blk_t, 2 * j + 2)
            dve.wait_ge(blk_hi_done, j + 1)
            for gr in range(2):
                rows = slice(HD * gr, HD * gr + HD)
                last = dve.tensor_tensor(blk_lo[rows, :, gr, :], tt[rows].rearrange("p a (l n) -> p (a l) n", n=32),
                                         blk_hi[rows, :, gr, :].bitcast(F32), ALU.subtract)
            last.then_inc(blk_lo_done, 1)
            dve.wait_ge(blk_lo_done, j + 1)

        dve.wait_ge(rp_out, 9 + 11)
        blocks(0)
        blocks_low(0)
        for i in range(4):
            rotate2(11 + i, qd[:, i])
            select(3)
        dve.wait_ge(rp_out, 9 + 15)
        blocks(1)
        select(4)
        blocks_low(1)
        dve.wait_ge(cm_hid, 1)
        dve.tensor_copy(hid_k[:, :, 0:N_CMP], ps[:, 3, 0:HD].rearrange("p (g n) -> p g n", n=32)[:, :, 0:N_CMP]).then_inc(cm_hid_ev, 1)
        dve.wait_ge(cm_hid, 2)
        dve.tensor_copy(hid_v[:, :, :, 0:N_CMP], ps[:, 1, 0:HD].rearrange("p (g n) -> p g n", n=32)[:, :, 0:N_CMP]
                        .unsqueeze(2).broadcast_to([P, NSA_KV, 4, N_CMP])).then_inc(cm_hid_ev, 1)
        dve.wait_ge(cm_kv, 1)
        step(dve.tensor_copy(kcmp[:], ps[:, 6, 0:64]))
        for r in range(4):
            rows = slice(32 * r, 32 * r + 32)
            last = dve.tensor_copy(v_diag[rows, :, r, :], ps[rows, 6, 64:192].rearrange("p (g d) -> p g d", g=NSA_KV))
        last.then_inc(cm_kv_ev, 1)

        def per_head(col, qc):
            return c8[:, col, :].unsqueeze(2).broadcast_to([P, 8, 32])

        def mask8(first, qc):
            return kst[:, first + 32 * qc:first + 32 * qc + 32].unsqueeze(1).broadcast_to([P, 8, 32])

        def heads(t):
            return t.rearrange("p (h n) -> p h n", n=32)

        def cmp_scores(qc):
            s = heads(cs[:, qc % 2])
            dve.wait_ge(cm_s, qc + 1)
            if qc >= 2:
                dve.wait_ge(cm_tr, qc - 1)
            for gr in range(2):
                mask = kst[:, K_CADD + 32 * qc:K_CADD + 32 * qc + 32].unsqueeze(1).broadcast_to([P, 4, 32])
                ins = dve.tensor_tensor(s[:, 4 * gr:4 * gr + 4], heads(ps[:, 5 - qc % 2 + 2 * gr, 0:128]), mask, ALU.add)
            step(ins)
            step(dve.tensor_reduce(c8[:, 0, :], s, AX, ALU.max))
            dve.tensor_tensor(s, s, per_head(0, qc), ALU.subtract).then_inc(cm_sub, 1)

        def cmp_probs(qc):
            s = heads(cs[:, qc % 2])
            dve.wait_ge(cm_exp, qc + 1)
            step(dve.tensor_reduce(c8[:, 1, :], s, AX, ALU.add))
            step(dve.reciprocal(c8[:, 1, :], c8[:, 1, :]))
            g = gsig[:, qc, :].rearrange("p (h b) -> p h b", b=3)[:, :, 0]
            step(dve.tensor_tensor(c8[:, 2, :], c8[:, 1, :], g, ALU.mult))
            step(dve.tensor_tensor(s, s, mask8(K_CMUL, qc), ALU.mult))
            dve.tensor_tensor(s, s, per_head(2, qc), ALU.mult).then_inc(cm_p, 1)

        for qc in range(NQ + 1):
            if qc < NQ:
                cmp_scores(qc)
            if qc >= 1:
                cmp_probs(qc - 1)
        dve.wait_ge(rp_out, 9 + 15)
        dve.wait_ge(cm_o_ev, NQ)
        attention(ATT[1], h_hi, h_lo, between=select)

        def out2(m):
            wait_product(dve, wo2_mm, m, 2, W_OUT2)
            dve.tensor_copy(y2[:, m], ps[:, m % 4]).then_inc(y_ready, 1)

        def add_normed(factor, first):
            def chunk(m):
                if m:
                    dve.wait_ge(x_ready, first + m)
                step(dve.scalar_tensor_tensor(tt[:, m % 2], y2[:, m], column(fac, factor + m), rb[:], ALU.mult, ALU.mult))
                dve.tensor_tensor(xT[:, m], xT[:, m], tt[:, m % 2], ALU.add).then_inc(x_ready, 1)
            return chunk

        chunks_then_add(5, out2)
        norm_inverse(5)
        dve.wait_ge(y_ready, 8)
        chunks_then_add(6, add_normed(A_POSTMIX, X_ATT))
        norm_inverse(6)
        modulated(4, A_PREFFN, 72 + 24)
        for half in range(2):
            n0 = W_FFN3 + 16 * half
            start = count[0]
            with dve.Fori(0, 4) as it:
                count[0] = it * 4 + start
                for j in range(4):
                    k = 4 * it + j
                    dve.wait_ge(f3["relu"], it * 4 + (16 * half + j + 1 + START))
                    dve.wait_ge(f3["hid"], it * 4 + (16 * half + j + START))
                    dve.tensor_tensor(tt[:, j % 2], sg3[:, j], sg3[:, j], ALU.mult).then_inc(f3["sq"], 1)
                    dve.wait_ge(f3["sq"], it * 4 + (16 * half + j + 1 + START))
                    step(dve.tensor_copy(g_hi[:, bass.ds(k, 1)], tt[:, j % 2:j % 2 + 1]))
                    dve.tensor_tensor(g_lo[:, bass.ds(k, 1)], tt[:, j % 2:j % 2 + 1], g_hi[:, bass.ds(k, 1)].bitcast(F32),
                                      ALU.subtract).then_inc(f3["hid"], 1)
            count[0] = start + 16
            n1 = n0 + 8

            def down(m):
                dve.wait_ge(tile_used, n1 + 2 * (m // 2) + 2)
                if half == 0:
                    dve.tensor_copy(y2[:, m], ps[:, m % 4]).then_inc(y_ready, 1)
                else:
                    dve.tensor_tensor(y2[:, m], y2[:, m], ps[:, m % 4], ALU.add).then_inc(y_ready, 1)

            if half == 0:
                for m in range(NC):
                    down(m)
                dve.wait_ge(y_ready, 16)
            else:
                chunks_then_add(7, down)
        norm_inverse(7)
        dve.wait_ge(y_ready, 24)

        for m in range(NC):
            add_normed(A_POSTFFN, X_END)(m)
    ctx.close()


def make(nc, arrays):
    handles = {name: nc.dram_tensor(f"in_{name}", list(v.shape), mybir.dt.from_np(v.dtype), kind="ExternalInput").ap()
               for name, v in arrays.items()}
    out = nc.dram_tensor("out_x", [1, T, D], F32, kind="ExternalOutput").ap()
    build(nc, handles, out)


def kernel(**inputs):
    import concourse.bacc as bacc
    from concourse.bass_utils import run_bass_kernel_spmd

    arrays = {name: np.ascontiguousarray(v) for name, v in inputs.items()}
    arrays["kst"], arrays["dft_d"], arrays["dft_s"] = constants()
    nc = bacc.Bacc("TRN2", target_bir_lowering=False, num_devices=1)
    make(nc, arrays)
    r = run_bass_kernel_spmd(nc, [{f"in_{name}": v for name, v in arrays.items()}], core_ids=[0])
    return r.results[0]["out_x"]
```
